# Optimizing a Trainium2 kernel written in Bass

```python
import functools
import jax, jax.numpy as jnp
from jax import lax
import numpy as np
import math
import jax
import jax.numpy as jnp

D_MODEL = 1024
BATCH = 1
SEQ = 256
DEPTH = 1

NSA_HEADS = 8
NSA_KV_GROUPS = 2
NSA_HEAD_DIM = 64
NSA_WIDTH = NSA_HEADS * NSA_HEAD_DIM
NSA_KV_WIDTH = NSA_KV_GROUPS * NSA_HEAD_DIM
CMP_LEN = 32
CMP_STRIDE = 16
CMP_HIDDEN = 256
SEL_BLOCK = 64
SEL_TOPN = 16
WINDOW = 512
Q_BLOCK = 128
ROPE_THETA = 500000.0
ROPE_DIM = NSA_HEAD_DIM // 4

RET_HEADS = 4
RET_QK_DIM = 128
RET_V_DIM = 256
RET_QK_WIDTH = RET_HEADS * RET_QK_DIM
RET_V_WIDTH = RET_HEADS * RET_V_DIM
RET_CHUNK = 128
RET_ROPE_BASE = 10000.0

RMS_EPS = 1e-6
GN_EPS = 1e-6

PROJ_SIZES = (
    NSA_WIDTH,
    NSA_KV_WIDTH,
    NSA_KV_WIDTH,
    NSA_KV_WIDTH,
    NSA_KV_WIDTH,
    NSA_KV_WIDTH,
    NSA_KV_WIDTH,
    NSA_HEADS * 3,
    NSA_WIDTH,
    RET_QK_WIDTH,
    RET_QK_WIDTH,
    RET_V_WIDTH,
    RET_V_WIDTH,
    D_MODEL,
    D_MODEL,
)
PROJ_TOTAL = sum(PROJ_SIZES)


def rms_norm(x, g):
    x32 = x.astype(jnp.float32)
    y = x32 * lax.rsqrt(jnp.mean(x32 * x32, axis=-1, keepdims=True) + RMS_EPS)
    return (y * g.astype(jnp.float32)).astype(x.dtype)

def split_points():
    pts, acc = [], 0
    for s in PROJ_SIZES[:-1]:
        acc += s
        pts.append(acc)
    return pts

def apply_rotary(x, ang):
    half = ang.shape[-1]
    r = 2 * half
    cos = jnp.cos(ang)[:, None, :].astype(x.dtype)
    sin = jnp.sin(ang)[:, None, :].astype(x.dtype)
    x1 = x[..., :half]
    x2 = x[..., half:r]
    return jnp.concatenate([x1 * cos - x2 * sin, x2 * cos + x1 * sin, x[..., r:]], axis=-1)

def masked_softmax(s, mask):
    s = jnp.where(mask, s.astype(jnp.float32), -jnp.inf)
    m = jnp.max(s, axis=-1, keepdims=True)
    m = jnp.where(jnp.isfinite(m), m, 0.0)
    p = jnp.where(mask, jnp.exp(s - m), 0.0)
    return p / jnp.maximum(jnp.sum(p, axis=-1, keepdims=True), jnp.finfo(jnp.float32).tiny)

def compress_blocks(kv, pe, w1, w2):
    S, G, dh = kv.shape
    n_cmp = (S - CMP_LEN) // CMP_STRIDE + 1
    tok_idx = jnp.arange(n_cmp)[:, None] * CMP_STRIDE + jnp.arange(CMP_LEN)[None, :]
    blocks = kv[tok_idx] + pe[None, :, None, :]
    flat = blocks.transpose(0, 2, 1, 3).reshape(n_cmp, G, CMP_LEN * dh)
    return jax.nn.gelu(flat @ w1) @ w2

def nsa_sequence(q, k_cmp_raw, v_cmp_raw, k_sel, v_sel, k_win, v_win, gate,
                 cmp_pe_k, cmp_w1_k, cmp_w2_k, cmp_pe_v, cmp_w1_v, cmp_w2_v):
    S = q.shape[0]
    G, H, dh = NSA_KV_GROUPS, NSA_HEADS, NSA_HEAD_DIM
    hpg = H // G
    scale = dh ** -0.5

    kc = compress_blocks(k_cmp_raw, cmp_pe_k, cmp_w1_k, cmp_w2_k)
    vc = compress_blocks(v_cmp_raw, cmp_pe_v, cmp_w1_v, cmp_w2_v)
    n_cmp = kc.shape[0]
    cmp_start = jnp.arange(n_cmp) * CMP_STRIDE
    cmp_end = cmp_start + CMP_LEN - 1

    n_sel = S // SEL_BLOCK
    n_top = min(SEL_TOPN, n_sel)
    sel_start = jnp.arange(n_sel) * SEL_BLOCK
    overlap = ((cmp_start[:, None] < sel_start[None, :] + SEL_BLOCK)
               & (cmp_start[:, None] + CMP_LEN > sel_start[None, :])).astype(jnp.float32)
    kb = k_sel.reshape(n_sel, SEL_BLOCK, G, dh).transpose(2, 0, 1, 3)
    vb = v_sel.reshape(n_sel, SEL_BLOCK, G, dh).transpose(2, 0, 1, 3)

    k_pad = jnp.pad(k_win, ((WINDOW, 0), (0, 0), (0, 0)))
    v_pad = jnp.pad(v_win, ((WINDOW, 0), (0, 0), (0, 0)))

    n_qb = S // Q_BLOCK
    qb = q.reshape(n_qb, Q_BLOCK, G, hpg, dh)
    gb = gate.reshape(n_qb, Q_BLOCK, G, hpg, 3)
    blk_ids = jnp.arange(n_sel)
    g_idx = jnp.arange(G)[None, :, None]

    def block(args):
        qi, gi, b = args
        t = b * Q_BLOCK + jnp.arange(Q_BLOCK)
        s = jnp.einsum('qghd,cgd->qghc', qi, kc) * scale
        mask_c = (cmp_end[None, :] <= t[:, None])[:, None, None, :]
        p_c = masked_softmax(s, mask_c)
        o_c = jnp.einsum('qghc,cgd->qghd', p_c.astype(vc.dtype), vc)
        imp = jnp.einsum('qgc,cn->qgn', jnp.sum(p_c, axis=2), overlap)
        cur = t // SEL_BLOCK
        valid = blk_ids[None, :] <= cur[:, None]
        forced = ((blk_ids[None, :] == 0) | (blk_ids[None, :] == cur[:, None])
                  | (blk_ids[None, :] == cur[:, None] - 1))
        score = jnp.where(forced[:, None, :], jnp.inf,
                          jnp.where(valid[:, None, :], imp, -jnp.inf))
        _, idx = lax.top_k(score, n_top)
        sel_valid = jnp.take_along_axis(
            jnp.broadcast_to(valid[:, None, :], score.shape), idx, axis=-1)
        ks = kb[g_idx, idx]
        vs = vb[g_idx, idx]
        s = jnp.einsum('qghd,qgnbd->qghnb', qi, ks) * scale
        kpos = idx[..., None] * SEL_BLOCK + jnp.arange(SEL_BLOCK)
        mask_s = sel_valid[..., None] & (kpos <= t[:, None, None, None])
        nk = n_top * SEL_BLOCK
        p_s = masked_softmax(s.reshape(Q_BLOCK, G, hpg, nk),
                             mask_s.reshape(Q_BLOCK, G, 1, nk))
        o_s = jnp.einsum('qghk,qgkd->qghd', p_s.astype(vs.dtype),
                         vs.reshape(Q_BLOCK, G, nk, dh))
        kw = lax.dynamic_slice_in_dim(k_pad, b * Q_BLOCK, Q_BLOCK + WINDOW, axis=0)
        vw = lax.dynamic_slice_in_dim(v_pad, b * Q_BLOCK, Q_BLOCK + WINDOW, axis=0)
        wpos = b * Q_BLOCK - WINDOW + jnp.arange(Q_BLOCK + WINDOW)
        diff = t[:, None] - wpos[None, :]
        mask_w = ((wpos[None, :] >= 0) & (diff >= 0) & (diff < WINDOW))[:, None, None, :]
        s = jnp.einsum('qghd,kgd->qghk', qi, kw) * scale
        p_w = masked_softmax(s, mask_w)
        o_w = jnp.einsum('qghk,kgd->qghd', p_w.astype(vw.dtype), vw)
        g = jax.nn.sigmoid(gi.astype(jnp.float32))
        o = g[..., 0:1] * o_c + g[..., 1:2] * o_s + g[..., 2:3] * o_w
        return o.reshape(Q_BLOCK, H * dh).astype(q.dtype)

    out = lax.map(block, (qb, gb, jnp.arange(n_qb)))
    return out.reshape(S, H * dh)

def retention_sequence(q, k, v):
    S = q.shape[0]
    H, dk, dv, C = RET_HEADS, RET_QK_DIM, RET_V_DIM, RET_CHUNK
    nc = S // C
    log_g = jnp.log(1.0 - 2.0 ** (-5.0 - jnp.arange(H, dtype=jnp.float32)))
    n = jnp.arange(C, dtype=jnp.float32)
    diff = n[:, None] - n[None, :]
    decay_mask = jnp.where(diff >= 0, jnp.exp(jnp.maximum(diff, 0.0)[None] * log_g[:, None, None]), 0.0)
    q_dec = jnp.exp((n[None, :] + 1.0) * log_g[:, None])
    k_dec = jnp.exp((C - 1.0 - n[None, :]) * log_g[:, None])
    chunk_dec = jnp.exp(C * log_g)

    qc = q.reshape(nc, C, H, dk)
    kc = k.reshape(nc, C, H, dk)
    vc = v.reshape(nc, C, H, dv)
    att = jnp.einsum('nihd,njhd->nhij', qc, kc) * decay_mask[None]
    o_inner = jnp.einsum('nhij,njhe->nihe', att, vc)
    kv = jnp.einsum('njhd,hj,njhe->nhde', kc, k_dec, vc).astype(jnp.float32)

    def step(R, kv_i):
        return chunk_dec[:, None, None] * R + kv_i, R

    _, R_prev = lax.scan(step, jnp.zeros((H, dk, dv), jnp.float32), kv)
    o_cross = jnp.einsum('nihd,hi,nhde->nihe', qc, q_dec, R_prev)
    o = (o_inner + o_cross).reshape(S, H, dv).astype(jnp.float32)
    mu = jnp.mean(o, axis=-1, keepdims=True)
    var = jnp.mean(jnp.square(o - mu), axis=-1, keepdims=True)
    o = (o - mu) * lax.rsqrt(var + GN_EPS)
    return o.reshape(S, H * dv).astype(q.dtype)

def first_inputs(seed: int = 0) -> dict:
    key = jax.random.key(seed)
    ks = jax.random.split(key, 16)
    f32 = jnp.float32
    nrm = lambda k, shape, fan_in: jax.random.normal(k, shape, f32) * (fan_in ** -0.5)
    cmp_in = CMP_LEN * NSA_HEAD_DIM
    return {
        "x": jax.random.normal(ks[0], (BATCH, SEQ, D_MODEL), f32),
        "norm_pre": 1.0 + 0.05 * jax.random.normal(ks[1], (D_MODEL,), f32),
        "w_in": nrm(ks[2], (D_MODEL, PROJ_TOTAL), D_MODEL),
        "b_nsa_gate": 0.1 * jax.random.normal(ks[3], (NSA_HEADS * 3,), f32),
        "cmp_pe_k": 0.02 * jax.random.normal(ks[4], (CMP_LEN, NSA_HEAD_DIM), f32),
        "cmp_w1_k": nrm(ks[5], (cmp_in, CMP_HIDDEN), cmp_in),
        "cmp_w2_k": nrm(ks[6], (CMP_HIDDEN, NSA_HEAD_DIM), CMP_HIDDEN),
        "cmp_pe_v": 0.02 * jax.random.normal(ks[7], (CMP_LEN, NSA_HEAD_DIM), f32),
        "cmp_w1_v": nrm(ks[8], (cmp_in, CMP_HIDDEN), cmp_in),
        "cmp_w2_v": nrm(ks[9], (CMP_HIDDEN, NSA_HEAD_DIM), CMP_HIDDEN),
        "w_nsa_o": nrm(ks[10], (NSA_WIDTH, D_MODEL), NSA_WIDTH),
        "w_ret_o": nrm(ks[11], (RET_V_WIDTH, D_MODEL), RET_V_WIDTH),
        "w_out": nrm(ks[12], (D_MODEL, D_MODEL), D_MODEL),
        "norm_post": 1.0 + 0.05 * jax.random.normal(ks[13], (D_MODEL,), f32),
    }

def first_block(x, norm_pre, w_in, b_nsa_gate, cmp_pe_k, cmp_w1_k, cmp_w2_k,
              cmp_pe_v, cmp_w1_v, cmp_w2_v, w_nsa_o, w_ret_o, w_out, norm_post):
    B, S, _ = x.shape
    pos = jnp.arange(S, dtype=jnp.float32)
    nsa_inv = 1.0 / (ROPE_THETA ** (jnp.arange(0, ROPE_DIM, 2, dtype=jnp.float32) / ROPE_DIM))
    nsa_ang = pos[:, None] * nsa_inv[None, :]
    ret_inv = 1.0 / (RET_ROPE_BASE ** jnp.linspace(0.0, 1.0, RET_QK_DIM // 2, dtype=jnp.float32))
    ret_ang = pos[:, None] * ret_inv[None, :]

    for _ in range(DEPTH):
        h = rms_norm(x, norm_pre)
        proj = h @ w_in
        (q_n, k_c, v_c, k_s, v_s, k_w, v_w, g_n, z_n,
         q_r, k_r, v_r, z_r, m_a, m_b) = jnp.split(proj, split_points(), axis=-1)

        kvshape = (B, S, NSA_KV_GROUPS, NSA_HEAD_DIM)
        q_n = apply_rotary(q_n.reshape(B, S, NSA_HEADS, NSA_HEAD_DIM), nsa_ang)
        k_c = apply_rotary(k_c.reshape(kvshape), nsa_ang)
        k_s = apply_rotary(k_s.reshape(kvshape), nsa_ang)
        k_w = apply_rotary(k_w.reshape(kvshape), nsa_ang)
        gate_n = (g_n + b_nsa_gate).reshape(B, S, NSA_HEADS, 3)
        nsa_fn = lambda a, b_, c, d, e, f, g, gt: nsa_sequence(
            a, b_, c, d, e, f, g, gt,
            cmp_pe_k, cmp_w1_k, cmp_w2_k, cmp_pe_v, cmp_w1_v, cmp_w2_v)
        o_a = jax.vmap(nsa_fn)(q_n, k_c, v_c.reshape(kvshape), k_s, v_s.reshape(kvshape),
                               k_w, v_w.reshape(kvshape), gate_n)
        y_a = (o_a * jax.nn.silu(z_n)) @ w_nsa_o

        q_r = apply_rotary(q_r.reshape(B, S, RET_HEADS, RET_QK_DIM), ret_ang)
        k_r = apply_rotary(k_r.reshape(B, S, RET_HEADS, RET_QK_DIM), ret_ang) * (RET_QK_DIM ** -0.5)
        o_b = jax.vmap(retention_sequence)(q_r, k_r, v_r.reshape(B, S, RET_HEADS, RET_V_DIM))
        y_b = (o_b * jax.nn.silu(z_r)) @ w_ret_o

        merged = jax.nn.sigmoid(m_a) * y_a + jax.nn.sigmoid(m_b) * y_b
        x = x + rms_norm(merged @ w_out, norm_post)
    return x


N_MEM = 256
SSD_EXPAND = 2
D_INNER = SSD_EXPAND * D_MODEL
SSD_HEAD_DIM = 64
SSD_HEADS = D_INNER // SSD_HEAD_DIM
SSD_GROUPS = 4
SSD_STATE = 128
CONV_WIDTH = 4
SSD_CHUNK = 128
XBC_DIM = D_INNER + 2 * SSD_GROUPS * SSD_STATE
MLA_HEADS = 16
QK_NOPE_DIM = 64
QK_ROPE_DIM = 32
QK_HEAD_DIM = QK_NOPE_DIM + QK_ROPE_DIM
V_HEAD_DIM = 64
Q_LORA_RANK = 384
KV_LORA_RANK = 256
ROPE_THETA_2 = 10000.0
XA_HEADS = 4
XA_HEAD_DIM = D_MODEL // XA_HEADS
N_EXPERT_GROUPS = 4
EXPERTS_PER_GROUP = 8
N_EXPERTS = N_EXPERT_GROUPS * EXPERTS_PER_GROUP
TOP_K = 2
D_EXPERT = 256

IN_SPLITS = (D_INNER, XBC_DIM, SSD_HEADS, Q_LORA_RANK, KV_LORA_RANK, QK_ROPE_DIM, D_MODEL, D_MODEL)
IN_PROJ_DIM = D_INNER + XBC_DIM + SSD_HEADS + Q_LORA_RANK + KV_LORA_RANK + QK_ROPE_DIM + 2 * D_MODEL


def rms_norm_2(x, gain):
    xf = x.astype(jnp.float32)
    xf = xf * lax.rsqrt(jnp.mean(xf * xf, axis=-1, keepdims=True) + RMS_EPS)
    return xf.astype(x.dtype) * gain

def split_cols(x, sizes):
    offs = np.cumsum(np.array(sizes))[:-1].tolist()
    return jnp.split(x, offs, axis=-1)

def causal_depthwise_conv(x, w, b):
    k, c = w.shape
    y = lax.conv_general_dilated(x, w[:, None, :], window_strides=(1,), padding=[(k - 1, 0)],
                                 dimension_numbers=('NWC', 'WIO', 'NWC'), feature_group_count=c)
    return y + b

def apply_rope(x, positions):
    half = x.shape[-1] // 2
    inv_freq = ROPE_THETA_2 ** (-jnp.arange(half, dtype=jnp.float32) / half)
    ang = positions.astype(jnp.float32)[..., None] * inv_freq
    cos = jnp.cos(ang)[:, :, None, :]
    sin = jnp.sin(ang)[:, :, None, :]
    xf = x.astype(jnp.float32)
    x1, x2 = xf[..., :half], xf[..., half:]
    return jnp.concatenate([x1 * cos - x2 * sin, x2 * cos + x1 * sin], axis=-1).astype(x.dtype)

def ssd_chunked_scan(xh, dt, a, bm, cm):
    b, s, h, p = xh.shape
    g, n = bm.shape[2], bm.shape[3]
    r = h // g
    nc, l = s // SSD_CHUNK, SSD_CHUNK
    x_dt = (xh.astype(jnp.float32) * dt[..., None]).reshape(b, nc, l, g, r, p)
    a_dt = (dt * a).reshape(b, nc, l, g, r).transpose(0, 3, 4, 1, 2)
    bc = bm.astype(jnp.float32).reshape(b, nc, l, g, n)
    cc = cm.astype(jnp.float32).reshape(b, nc, l, g, n)
    a_cum = jnp.cumsum(a_dt, axis=-1)
    causal = jnp.tril(jnp.ones((l, l), dtype=bool))
    seg = a_cum[..., :, None] - a_cum[..., None, :]
    decay_in = jnp.exp(jnp.where(causal, seg, -jnp.inf))
    cb = jnp.einsum('bclgn,bcsgn->bcgls', cc, bc)
    y_diag = jnp.einsum('bcgls,bgrcls,bcsgrp->bclgrp', cb, decay_in, x_dt)
    decay_to_end = jnp.exp(a_cum[..., -1:] - a_cum)
    chunk_states = jnp.einsum('bclgn,bgrcl,bclgrp->bcgrpn', bc, decay_to_end, x_dt)
    chunk_decay = jnp.exp(a_cum[..., -1])

    def step(state, inp):
        st, dec = inp
        return state * dec[..., None, None] + st, state

    init = jnp.zeros((b, g, r, p, n), jnp.float32)
    _, prev_states = lax.scan(step, init, (jnp.moveaxis(chunk_states, 1, 0), jnp.moveaxis(chunk_decay, -1, 0)))
    prev_states = jnp.moveaxis(prev_states, 0, 1)
    y_off = jnp.einsum('bclgn,bcgrpn,bgrcl->bclgrp', cc, prev_states, jnp.exp(a_cum))
    return (y_diag + y_off).reshape(b, s, h, p)

def ssd_branch(z, xbc, dt_raw, conv_w, conv_b, dt_bias, a_log, d_skip, ssd_norm):
    b, s, _ = z.shape
    xbc = jax.nn.silu(causal_depthwise_conv(xbc, conv_w, conv_b))
    xs, bm, cm = split_cols(xbc, (D_INNER, SSD_GROUPS * SSD_STATE, SSD_GROUPS * SSD_STATE))
    xh = xs.reshape(b, s, SSD_HEADS, SSD_HEAD_DIM)
    bm = bm.reshape(b, s, SSD_GROUPS, SSD_STATE)
    cm = cm.reshape(b, s, SSD_GROUPS, SSD_STATE)
    dt = jax.nn.softplus(dt_raw.astype(jnp.float32) + dt_bias.astype(jnp.float32))
    a = -jnp.exp(a_log.astype(jnp.float32))
    y = ssd_chunked_scan(xh, dt, a, bm, cm)
    y = y + d_skip.astype(jnp.float32)[:, None] * xh.astype(jnp.float32)
    y = y.reshape(b, s, D_INNER) * jax.nn.silu(z.astype(jnp.float32))
    y = y.reshape(b, s, SSD_GROUPS, D_INNER // SSD_GROUPS)
    y = y * lax.rsqrt(jnp.mean(y * y, axis=-1, keepdims=True) + RMS_EPS)
    return y.reshape(b, s, D_INNER).astype(z.dtype) * ssd_norm

def causal_block_attention(q, k, v, scale):
    b, s, h, dq = q.shape
    nb = s // Q_BLOCK
    qb = jnp.moveaxis(q.reshape(b, nb, Q_BLOCK, h, dq), 1, 0)
    kpos = jnp.arange(s)

    def one_block(args):
        i, qi = args
        sc = jnp.einsum('bqhd,bkhd->bhqk', qi, k).astype(jnp.float32) * scale
        qpos = i * Q_BLOCK + jnp.arange(Q_BLOCK)
        sc = jnp.where(kpos[None, :] <= qpos[:, None], sc, -jnp.inf)
        pr = jax.nn.softmax(sc, axis=-1).astype(v.dtype)
        return jnp.einsum('bhqk,bkhd->bqhd', pr, v)

    out = lax.map(one_block, (jnp.arange(nb), qb))
    return jnp.moveaxis(out, 0, 1).reshape(b, s, h, v.shape[-1])

def mla_branch(q_a, c_kv, k_rope, positions, q_a_norm, w_q_b, kv_a_norm, w_kv_b):
    b, s, _ = q_a.shape
    q = (rms_norm_2(q_a, q_a_norm) @ w_q_b).reshape(b, s, MLA_HEADS, QK_HEAD_DIM)
    kv = (rms_norm_2(c_kv, kv_a_norm) @ w_kv_b).reshape(b, s, MLA_HEADS, QK_NOPE_DIM + V_HEAD_DIM)
    q_nope, q_pe = q[..., :QK_NOPE_DIM], q[..., QK_NOPE_DIM:]
    k_nope, v = kv[..., :QK_NOPE_DIM], kv[..., QK_NOPE_DIM:]
    q_pe = apply_rope(q_pe, positions)
    k_pe = apply_rope(k_rope[:, :, None, :], positions)
    q = jnp.concatenate([q_nope, q_pe], axis=-1)
    k = jnp.concatenate([k_nope, jnp.broadcast_to(k_pe, (b, s, MLA_HEADS, QK_ROPE_DIM))], axis=-1)
    o = causal_block_attention(q, k, v, QK_HEAD_DIM ** -0.5)
    return o.reshape(b, s, MLA_HEADS * V_HEAD_DIM)

def memory_cross_attention(h, mem, w_xq, w_xkv, w_xo):
    b, s, _ = h.shape
    m = mem.shape[1]
    q = (h @ w_xq).reshape(b, s, XA_HEADS, XA_HEAD_DIM)
    k, v = jnp.split(mem @ w_xkv, 2, axis=-1)
    k = k.reshape(b, m, XA_HEADS, XA_HEAD_DIM)
    v = v.reshape(b, m, XA_HEADS, XA_HEAD_DIM)
    sc = jnp.einsum('bshd,bmhd->bhsm', q, k).astype(jnp.float32) * XA_HEAD_DIM ** -0.5
    pr = jax.nn.softmax(sc, axis=-1).astype(v.dtype)
    o = jnp.einsum('bhsm,bmhd->bshd', pr, v).reshape(b, s, XA_HEADS * XA_HEAD_DIM)
    return o @ w_xo

def hierarchical_moe(h, w_rg, b_rg, w_re, b_re, w_gate, w_up, w_down):
    b, s, d = h.shape
    t = h.reshape(b * s, d)
    g_logits = (t @ w_rg).astype(jnp.float32) + b_rg
    g_prob = jax.nn.softmax(g_logits, axis=-1)
    g_sel = jnp.argmax(g_logits, axis=-1)
    g_w = jnp.take_along_axis(g_prob, g_sel[:, None], axis=1)
    e_logits = ((t @ w_re).astype(jnp.float32) + b_re).reshape(-1, N_EXPERT_GROUPS, EXPERTS_PER_GROUP)
    e_in = jnp.take_along_axis(e_logits, g_sel[:, None, None], axis=1)[:, 0]
    top_v, top_i = lax.top_k(e_in, TOP_K)
    w_top = jax.nn.softmax(top_v, axis=-1) * g_w
    expert_id = g_sel[:, None] * EXPERTS_PER_GROUP + top_i
    combine = jnp.sum(jax.nn.one_hot(expert_id, N_EXPERTS, dtype=jnp.float32) * w_top[..., None], axis=1).astype(t.dtype)
    hg = jnp.einsum('td,edf->tef', t, w_gate)
    hu = jnp.einsum('td,edf->tef', t, w_up)
    act = jax.nn.silu(hg) * hu * combine[:, :, None]
    y = jnp.einsum('tef,efd->td', act, w_down)
    return y.reshape(b, s, d)

def second_inputs(seed: int = 0) -> dict:
    key = jax.random.key(seed)
    ks = iter(jax.random.split(key, 48))
    f32 = jnp.float32
    L = DEPTH

    def nrm(shape, fan_in):
        return jax.random.normal(next(ks), shape, f32) * fan_in ** -0.5

    def gain(shape):
        return 1.0 + 0.02 * jax.random.normal(next(ks), shape, f32)

    x = jax.random.normal(next(ks), (BATCH, SEQ, D_MODEL), f32)
    mem = jax.random.normal(next(ks), (BATCH, N_MEM, D_MODEL), f32)
    offset = jax.random.randint(next(ks), (BATCH, 1), 0, 1024, dtype=jnp.int32)
    positions = (offset + jnp.arange(SEQ, dtype=jnp.int32)[None, :]).astype(jnp.int32)
    dt0 = jnp.exp(jax.random.uniform(next(ks), (L, SSD_HEADS), f32, math.log(1e-3), math.log(1e-1)))
    dt_bias = dt0 + jnp.log(-jnp.expm1(-dt0))
    a_log = jnp.log(jax.random.uniform(next(ks), (L, SSD_HEADS), f32, 1.0, 16.0))
    return {
        'x': x,
        'mem': mem,
        'positions': positions,
        'norm_mix': gain((L, D_MODEL)),
        'w_in': nrm((L, D_MODEL, IN_PROJ_DIM), D_MODEL),
        'conv_w': nrm((L, CONV_WIDTH, XBC_DIM), CONV_WIDTH),
        'conv_b': 0.02 * jax.random.normal(next(ks), (L, XBC_DIM), f32),
        'dt_bias': dt_bias,
        'a_log': a_log,
        'd_skip': 1.0 + 0.1 * jax.random.normal(next(ks), (L, SSD_HEADS), f32),
        'ssd_norm': gain((L, D_INNER)),
        'w_ssd_out': nrm((L, D_INNER, D_MODEL), D_INNER),
        'q_a_norm': gain((L, Q_LORA_RANK)),
        'w_q_b': nrm((L, Q_LORA_RANK, MLA_HEADS * QK_HEAD_DIM), Q_LORA_RANK),
        'kv_a_norm': gain((L, KV_LORA_RANK)),
        'w_kv_b': nrm((L, KV_LORA_RANK, MLA_HEADS * (QK_NOPE_DIM + V_HEAD_DIM)), KV_LORA_RANK),
        'w_mla_out': nrm((L, MLA_HEADS * V_HEAD_DIM, D_MODEL), MLA_HEADS * V_HEAD_DIM),
        'w_o': nrm((L, D_MODEL, D_MODEL), D_MODEL),
        'norm_xattn': gain((L, D_MODEL)),
        'norm_mem': gain((L, D_MODEL)),
        'w_xq': nrm((L, D_MODEL, XA_HEADS * XA_HEAD_DIM), D_MODEL),
        'w_xkv': nrm((L, D_MODEL, 2 * XA_HEADS * XA_HEAD_DIM), D_MODEL),
        'w_xo': nrm((L, XA_HEADS * XA_HEAD_DIM, D_MODEL), XA_HEADS * XA_HEAD_DIM),
        'norm_moe': gain((L, D_MODEL)),
        'w_router_group': nrm((L, D_MODEL, N_EXPERT_GROUPS), D_MODEL),
        'b_router_group': 0.01 * jax.random.normal(next(ks), (L, N_EXPERT_GROUPS), f32),
        'w_router_expert': nrm((L, D_MODEL, N_EXPERTS), D_MODEL),
        'b_router_expert': 0.01 * jax.random.normal(next(ks), (L, N_EXPERTS), f32),
        'w_exp_gate': nrm((L, N_EXPERTS, D_MODEL, D_EXPERT), D_MODEL),
        'w_exp_up': nrm((L, N_EXPERTS, D_MODEL, D_EXPERT), D_MODEL),
        'w_exp_down': nrm((L, N_EXPERTS, D_EXPERT, D_MODEL), D_EXPERT),
        'norm_final': gain((D_MODEL,)),
    }

def second_block(x, mem, positions, norm_mix, w_in, conv_w, conv_b, dt_bias, a_log, d_skip, ssd_norm, w_ssd_out,
              q_a_norm, w_q_b, kv_a_norm, w_kv_b, w_mla_out, w_o, norm_xattn, norm_mem, w_xq, w_xkv, w_xo,
              norm_moe, w_router_group, b_router_group, w_router_expert, b_router_expert,
              w_exp_gate, w_exp_up, w_exp_down, norm_final):
    h = x
    for i in range(DEPTH):
        u = rms_norm_2(h, norm_mix[i])
        z, xbc, dt_raw, q_a, c_kv, k_rope, gate_ssd, gate_mla = split_cols(u @ w_in[i], IN_SPLITS)
        y_ssd = ssd_branch(z, xbc, dt_raw, conv_w[i], conv_b[i], dt_bias[i], a_log[i], d_skip[i], ssd_norm[i]) @ w_ssd_out[i]
        y_mla = mla_branch(q_a, c_kv, k_rope, positions, q_a_norm[i], w_q_b[i], kv_a_norm[i], w_kv_b[i]) @ w_mla_out[i]
        merged = jax.nn.sigmoid(gate_ssd) * y_ssd + jax.nn.sigmoid(gate_mla) * y_mla
        h = h + merged @ w_o[i]
        h = h + memory_cross_attention(rms_norm_2(h, norm_xattn[i]), rms_norm_2(mem, norm_mem[i]), w_xq[i], w_xkv[i], w_xo[i])
        h = h + hierarchical_moe(rms_norm_2(h, norm_moe[i]), w_router_group[i], b_router_group[i],
                                 w_router_expert[i], b_router_expert[i], w_exp_gate[i], w_exp_up[i], w_exp_down[i])
    return rms_norm_2(h, norm_final)


def setup_inputs(seed=0):
    out = dict(first_inputs(seed))
    for name, value in second_inputs(seed + 1).items():
        if name != "x":
            out[name + "_2"] = value
    return out


def reference(
    x, norm_pre, w_in, b_nsa_gate, cmp_pe_k, cmp_w1_k, cmp_w2_k, cmp_pe_v, cmp_w1_v, cmp_w2_v,
    w_nsa_o, w_ret_o, w_out, norm_post, mem_2, positions_2, norm_mix_2, w_in_2, conv_w_2,
    conv_b_2, dt_bias_2, a_log_2, d_skip_2, ssd_norm_2, w_ssd_out_2, q_a_norm_2, w_q_b_2,
    kv_a_norm_2, w_kv_b_2, w_mla_out_2, w_o_2, norm_xattn_2, norm_mem_2, w_xq_2, w_xkv_2,
    w_xo_2, norm_moe_2, w_router_group_2, b_router_group_2, w_router_expert_2,
    b_router_expert_2, w_exp_gate_2, w_exp_up_2, w_exp_down_2, norm_final_2,
):
    x = first_block(
        x, norm_pre, w_in, b_nsa_gate, cmp_pe_k, cmp_w1_k, cmp_w2_k, cmp_pe_v, cmp_w1_v,
        cmp_w2_v, w_nsa_o, w_ret_o, w_out, norm_post,
    )
    return second_block(
        x, mem_2, positions_2, norm_mix_2, w_in_2, conv_w_2, conv_b_2, dt_bias_2, a_log_2,
        d_skip_2, ssd_norm_2, w_ssd_out_2, q_a_norm_2, w_q_b_2, kv_a_norm_2, w_kv_b_2,
        w_mla_out_2, w_o_2, norm_xattn_2, norm_mem_2, w_xq_2, w_xkv_2, w_xo_2, norm_moe_2,
        w_router_group_2, b_router_group_2, w_router_expert_2, b_router_expert_2, w_exp_gate_2,
        w_exp_up_2, w_exp_down_2, norm_final_2,
    )


_drawn_inputs = setup_inputs


def setup_inputs(seed=0):
    import zlib

    import numpy as np

    out = dict(_drawn_inputs(seed))
    spreads = {}
    factors = {'b_nsa_gate': 3.271,
     'cmp_pe_k': 8.0,
     'cmp_pe_v': 6.053,
     'norm_mix_2': 2.699,
     'conv_b_2': 3.283,
     'ssd_norm_2': 3.26,
     'q_a_norm_2': 8.0,
     'kv_a_norm_2': 6.017,
     'norm_xattn_2': 8.0,
     'norm_mem_2': 8.0,
     'b_router_group_2': 29.56,
     'b_router_expert_2': 34.92,
     'norm_final_2': 7.885,
     'd_skip_2': 3.025,
     'norm_moe_2': 8.0}
    for name, (base, spread) in spreads.items():
        noise = np.random.default_rng([zlib.crc32(name.encode()), seed]).standard_normal(out[name].shape)
        drawn = base * np.exp(spread * noise) if base else spread * noise
        out[name] = jnp.asarray(drawn.astype(out[name].dtype))
    for name, factor in factors.items():
        out[name] = (out[name] * factor).astype(out[name].dtype)
    return out
```

```python
import numpy as np
import concourse.bass as bass
from concourse import mybir
from contextlib import ExitStack

P, TT, S, DM = 128, 2, 256, 1024
UW = 2048
NRAW, NSPL = 3, 3
EPS = 1e-6
TWO_PI = 6.283185307179586
PI_PARTS = (6.28125, 1.93500518798828125e-3, 3.019916050561733e-7)
NEXP = 32
SCAN_UNITS = ("z0", "z1", "gs0", "z2", "gs1", "z3")
CONST = {}
SMALL = {}
for _n, _w in (("ident", 128), ("tri", 128), ("stri", 128), ("ones", 128), ("cmpmask", 30), ("cos", 16), ("sin", 16),
               ("invf", 16), ("iota", 32), ("rcos", 128), ("rsin", 128), ("negmask", 128)):
    CONST[_n] = (sum(w for _, w in CONST.values()), _w)
for _n, _w in (("g_pre", 8), ("g_mix", 8), ("g_xa", 8), ("g_mem", 8), ("g_moe", 8), ("g_ssd", 16), ("g_qa", 3),
               ("g_ckv", 2), ("conv_w", 96), ("conv_b", 24), ("pe_k", 16), ("pe_v", 16), ("b_gate", 24),
               ("dt_b", 32), ("a_log", 32), ("d_skip", 32), ("b_rt", 36), ("w2k", 256), ("w2v", 128)):
    SMALL[_n] = (sum(w for _, w in SMALL.values()), _w)
NCONST = sum(w for _, w in CONST.values())
NSMALL = sum(w for _, w in SMALL.values())


def unit_plan():
    plan = []

    def add(name, src, rows, cols, nk=4):
        for i, k0 in enumerate(range(0, rows // P, nk)):
            plan.append((name, i, src, k0 * P, min(nk, rows // P - k0), cols))

    r = np.arange
    w = "w_in"
    add("qn", w, 1024, r(0, 512))
    add("kv1", w, 1024, np.concatenate([r(512, 640), r(768, 896), r(1024, 1152), r(640, 768)]))
    add("kv2", w, 1024, np.concatenate([r(896, 1024), r(1152, 1280), r(1280, 1304)]))
    for i, n in enumerate(("qr", "kr", "vr0", "vr1")):
        add(n, w, 1024, r(1816 + 512 * i, 2328 + 512 * i))
    add("w1k", "cmp_w1_k", 2048, r(256), 8)
    add("w1v", "cmp_w1_v", 2048, r(256), 8)
    add("zn", w, 1024, r(1304, 1816))
    for i, n in enumerate(("zr0", "zr1", "ma0", "ma1", "mb0", "mb1")):
        add(n, w, 1024, r(3864 + 512 * i, 4376 + 512 * i))
    for i in range(2):
        add(f"ya{i}", "w_nsa_o", 512, r(512 * i, 512 * i + 512))
        add(f"yb{i}", "w_ret_o", 1024, r(512 * i, 512 * i + 512))
    for i in range(2):
        add(f"wo{i}", "w_out", 1024, r(512 * i, 512 * i + 512))
    w = "w_in_2"
    add("pa", w, 1024, r(5120, 5536))
    add("pb", w, 1024, r(5536, 5824))
    for i in range(3):
        add(f"wq{i}", "w_q_b_2", 384, r(512 * i, 512 * i + 512))
    heads = r(2048).reshape(16, 128)
    add("kn", "w_kv_b_2", 256, heads[:, :64].ravel())
    add("vv", "w_kv_b_2", 256, heads[:, 64:].ravel())
    for i in range(6):
        add(f"xbc{i}", w, 1024, r(2048 + 512 * i, 2560 + 512 * i))
    for i in range(2):
        add(f"gm{i}", w, 1024, r(6848 + 512 * i, 7360 + 512 * i))
    for i in range(2):
        add(f"ym{i}", "w_mla_out_2", 1024, r(512 * i, 512 * i + 512))
    for n in SCAN_UNITS:
        c = 512 * int(n[-1]) + (0 if n[0] == "z" else 5824)
        add(n, w, 1024, r(c, c + 512))
    for i in range(2):
        add(f"ys{i}", "w_ssd_out_2", 2048, r(512 * i, 512 * i + 512))
    for i in range(2):
        add(f"wp{i}", "w_o_2", 1024, r(512 * i, 512 * i + 512))
    for i in range(2):
        add(f"xk{i}", "w_xkv_2", 1024, r(512 * i, 512 * i + 512))
    for i in range(2):
        add(f"xv{i}", "w_xkv_2", 1024, r(1024 + 512 * i, 1536 + 512 * i))
    for i in range(2):
        add(f"xq{i}", "w_xq_2", 1024, r(512 * i, 512 * i + 512))
    for i in range(2):
        add(f"xo{i}", "w_xo_2", 1024, r(512 * i, 512 * i + 512))
    add("rt", "router", 1024, r(36), 8)

    def expert(kind, e):
        if kind == "down":
            plan.append((f"down{e}", 0, "w_exp_down_2", 256 * e, 2, r(1024)))
        else:
            plan.append((f"{kind}{e}", 0, f"w_exp_{kind}_2", 1024 * e, 8, r(256)))

    expert("gate", 0)
    expert("up", 0)
    for e in range(1, NEXP):
        expert("gate", e)
        expert("up", e)
        expert("down", e - 1)
    expert("down", NEXP - 1)
    return plan


def bank_plan(units):
    G, W, O, ends = [], [], [], {}

    def gemm(name, jobs=None):
        jobs = jobs or [(name, 0), (name, 1)]
        G.extend(jobs)
        ends[jobs[-1]] = max(i for i, u in enumerate(units) if u[0] == name)

    G += [("x", j) for j in range(4)]
    for n in ("qn", "kv1", "kv2"):
        gemm(n)
    for n in ("qr", "kr", "vr0", "vr1"):
        gemm(n)
    G += [("kT", 0), ("qT", 0), ("qT", 1), ("cT", 0), ("hid", 0)]
    ends[("hid", 0)] = max(i for i, u in enumerate(units) if u[0] == "w1v")
    gemm("zn")
    G += [("kvc", 0)]
    for n in ("zr0", "zr1", "ma0", "ma1"):
        gemm(n)
    G += [("on", 0), ("on", 1)]
    for n in ("mb0", "mb1"):
        gemm(n)
    G += [("or", j) for j in range(4)]
    for n in ("ya0", "yb0", "ya1", "yb1", "wo0", "wo1"):
        gemm(n)
    G += [("u", j) for j in range(4)]
    gemm("pa")
    gemm("pb")
    G += [("qa", 0), ("qa", 1), ("ck", 0), ("kp", 0)]
    for i in range(3):
        gemm(f"wq{i}")
    gemm("kn", [("kn", j) for j in range(4)])
    gemm("vv", [("vv", j) for j in range(4)])
    for i in range(6):
        gemm(f"xbc{i}")
    G += [("om", j) for j in range(4)]
    for n in ("gm0", "gm1", "ym0", "ym1", *SCAN_UNITS):
        gemm(n)
    G += [("y", j) for j in range(8)]
    for n in ("ys0", "ys1"):
        gemm(n)
    G += [("mem", j) for j in range(4)]
    for n in ("wp0", "wp1", "xk0", "xk1", "xv0", "xv1"):
        gemm(n)
    G += [("h", j) for j in range(4)]
    for n in ("xq0", "xq1", "xo0", "xo1"):
        gemm(n)
    G += [("m", j) for j in range(4)]
    gemm("rt")
    W += [("Sc", 0), ("Tc", 0)]
    W += [("S", 0)]
    for u in range(16):
        W += [("S", u + 1)] * (u < 15) + [("T", u)]
    O += [("Oc", 0), ("Oc", 1)] + [("O", q) for q in range(4)]
    for h in range(4):
        W += [("QK", h), ("A", h)]
        O += [("R", h)]
    W += [("mQ", 0), ("mS", 0)]
    for u in range(16):
        if u % 2 == 0 and u < 14:
            W += [("mQ", u // 2 + 1)]
        W += [("mS", u + 1)] * (u < 15) + [("mT", u)]
    O += [("mO", q) for q in range(4)]
    W += [("acum", 0), ("Bt", 0), ("CB", 0), ("CB", 1)]
    W += [("xt", i) for i in range(8)]
    for i in range(8):
        W += [("seg", 2 * i), ("seg", 2 * i + 1)]
        W += [("state" if i % 2 == 0 else "off", i // 2)]
        O += [("Y", i)]
    for h in range(4):
        W += [("xS", h), ("xT", h)]
        O += [("xO", h)]
    W += [("cb", 0)]
    jobs = {}
    counts = [0] * 8
    for pool, banks in ((G, (0, 1, 2, 3)), (W, (4, 5, 6)), (O, (7,))):
        for i, j in enumerate(pool):
            b = banks[i % len(banks)]
            full = None if j in ends else counts[b]
            counts[b] += j not in ends
            jobs[j] = (b, i // len(banks), full, ends.get(j), i)
    total = [sum(1 for j in jobs.values() if j[0] == b) for b in range(8)]
    return jobs, total


def program(nc, x_d, mem_d, pos_d, cst_d, sml_d, dec_d, npost_d, nfin_d, w_d, out_d, scratch):
    f32, f32r, bf16, i32 = mybir.dt.float32, mybir.dt.float32r, mybir.dt.bfloat16, mybir.dt.int32
    ACT, ALU, AX = mybir.ActivationFunctionType, mybir.AluOpType, mybir.AxisListType
    units = unit_plan()
    NU = len(units)
    UNIT = {}
    for i, u in enumerate(units):
        UNIT.setdefault(u[0], []).append(i)
    JOBS, TOTAL = bank_plan(units)
    NB = UNIT["gate0"][0]
    ctx = ExitStack()
    with ctx:
        base = 16512

        def at(name, off, shape, dt=f32):
            n = 4 if dt != bf16 else 2
            size = n * int(np.prod(shape[1:]))
            assert off + size <= 229344, (name, off + size)
            return nc.alloc_sbuf_tensor_at(name, shape, dt, offset=off)

        KB = 1024
        o = base
        raw = at("raw", o, [P, NRAW, UW]); o += NRAW * UW * 4
        whi = at("whi", o, [P, NSPL, UW], f32r); o += NSPL * UW * 4
        wlo = at("wlo", o, [P, NSPL, UW], f32r); o += NSPL * UW * 4
        xhi = at("xhi", o, [P, 16, S], f32r); o += 16 * KB
        xlo = at("xlo", o, [P, 16, S], f32r); o += 16 * KB
        x = at("x", o, [P, TT, DM]); o += 8 * KB
        cst = at("cst", o, [P, NCONST]); o += 4 * ((NCONST + 7) // 8 * 8)
        sml = at("sml", o, [P, NSMALL]); o += 4 * ((NSMALL + 7) // 8 * 8)
        identb = at("identb", o, [P, P], bf16); o += 256
        negb = at("negb", o, [P, P], bf16); o += 256
        stat = at("stat", o, [P, 256]); o += KB
        ropt = at("ropt", o, [P, 8, TT * 16]); o += KB
        posi = at("posi", o, [P, TT], i32); o += 32
        A = o

        def sub(tab, t, name):
            a, w = tab[name]
            return t[:, a:a + w]

        C = lambda n: sub(CONST, cst, n)
        D = lambda n: sub(SMALL, sml, n)
        ident, tri, stri, ones = C("ident"), C("tri"), C("stri"), C("ones")

        a = A
        xn = at("xn", a, [P, TT, DM])
        ropetmp = at("ropetmp", a, [P, 4, 512])
        a += 8 * KB
        nq = at("nq", a, [P, TT, 1304])
        mbT = at("mbT", a, [P, 8, S])
        a += 10432
        qk = at("qk", a, [P, TT, DM])
        mThi = at("mThi", a, [P, 8, S], f32r)
        a += 8 * KB
        vr = at("vr", a, [P, TT, DM])
        mTlo = at("mTlo", a, [P, 8, S], f32r)
        a += 8 * KB
        znT = at("znT", a, [P, 4, S])
        npost = at("npost", a, [P, DM])
        a += 4 * KB
        zrT = at("zrT", a, [P, 8, S])
        a += 8 * KB
        maT = at("maT", a, [P, 8, S])
        a += 8 * KB
        kT = at("kT", a, [P, 2, 512])
        a += 4 * KB
        qT = at("qT", a, [P, 4, S])
        decay = at("decay", a, [P, 4, S])
        a += 4 * KB
        oacc = at("oacc", a, [P, TT, 512])
        xcf = at("xcf", a, [P, 2, 16, 30])
        a += 4 * KB
        xchi = at("xchi", a, [P, 2, 16, 30], f32r)
        xclo = at("xclo", a + 3840, [P, 2, 16, 30], f32r)
        qkT = at("qkT", a, [P, 2, 512])
        a += 7680
        pr = at("pr", a, [P, 2, 512])
        hg = at("hg", a + 2 * KB, [P, 4, 120])
        a += 4 * KB
        pT = at("pT", a, [P, 2, 512])
        cs = at("cs", a + 2 * KB, [P, 16, 15])
        a += 4 * KB
        tmp = at("tmp", a, [P, 2, 512])
        vcb = at("vcb", a + 2 * KB, [P, 2, 4, 64])
        kcT = at("kcT", a + 1920, [P, 32])
        a += 4 * KB

        a = A
        pa = at("pa", a, [P, TT, 416])
        pb = at("pb", a + 3328, [P, TT, 288])
        a += 8 * KB
        qm = at("qm", a, [P, TT, 1536])
        a += 12 * KB
        vm = at("vm", a, [P, TT, DM])
        ymT = at("ymT", a, [P, 8, S])
        a += 8 * KB
        xbc = at("xbc", a, [P, 24, S])
        gsT = at("gsT", a, [P, 8, S])
        segR = at("segR", a + 8 * KB, [P, 2, 512])
        segE = at("segE", a + 12 * KB, [P, 2, 512])
        a += 24 * KB
        b0 = a
        km = at("km", a, [P, 16, S])
        a += 16 * KB
        qmT = at("qmT", a, [P, 2, 512])
        a += 4 * KB
        pr2 = at("pr2", a, [P, 2, 384])
        a += 3 * KB
        pT2 = at("pT2", a, [P, 2, 384])
        a += 3 * KB
        cv = at("cv", a, [P, 2, 2, S])
        ropetmp2 = at("ropetmp2", a, [P, 4, S])
        a += 4 * KB
        dts = at("dts", a, [P, 8, 64])
        a += 2 * KB
        zt = at("zt", A, [P, TT, 2048])
        btok = at("btok", A + 16 * KB, [P, 512])
        st = at("st", A + 18 * KB, [P, 512])
        xtok = at("xtok", b0, [P, TT, 2048])
        segM = at("segM", b0 + 16 * KB, [P, 2, 512])
        cbm = at("cbm", b0 + 20 * KB, [P, 2, 512])
        xd = at("xd", b0 + 24 * KB, [P, 512])
        yt = at("yt", b0 + 26 * KB, [P, 2, 512])
        m2hi = at("m2hi", b0, [P, 8, S], f32r)
        m2lo = at("m2lo", b0 + 8 * KB, [P, 8, S], f32r)
        memt = at("memt", A + 8 * KB, [P, TT, DM])
        kx = at("kx", A + 16 * KB, [P, 8, S])
        vx = at("vx", A + 24 * KB, [P, TT, DM])
        qx = at("qx", A + 32 * KB, [P, 8, S])
        px = at("px", A + 40 * KB, [P, 2, 512])
        pxT = at("pxT", A + 44 * KB, [P, 2, 512])
        comb = at("comb", A + 8 * KB, [P, NEXP, S])
        combt = at("combt", A + 40 * KB, [NEXP, S])
        rtl = at("rtl", A + 41 * KB, [P, 8, TT * 36])
        sg = at("sg", A + 44 * KB, [P, 2, 512])
        ga = at("ga", A + 48 * KB, [P, 2, 512])
        ahi = at("ahi", A + 52 * KB, [P, 2, 512], f32r)
        alo = at("alo", A + 56 * KB, [P, 2, 512], f32r)
        nfin = at("nfin", A + 60 * KB, [P, DM])

        STAT = {"x": 0, "post": 2, "u": 6, "qa": 8, "ck": 10, "y": 12, "mem": 20, "h": 22, "m": 24, "f": 26}
        RSTD, NMAX, SUMS, RSUM, GF, CMAX, CSUM, CGATE, GATE, MISC = 32, 64, 80, 96, 112, 128, 144, 160, 192, 240
        CW, CB_ = SMALL["conv_w"][0], SMALL["conv_b"][0]
        MAXN = {("S", u): u + 1 for u in range(16)} | {("mS", u): 17 + u for u in range(16)} | {("xS", h): 33 + h for h in range(4)}

        ps = [ctx.enter_context(nc.psum_tensor(f"ps{i}", [P, 512], f32)) for i in range(8)]
        sems = {}

        def sem(name):
            if name not in sems:
                sems[name] = ctx.enter_context(nc.semaphore(name))
            return sems[name]

        raw_loaded = [sem(f"raw_loaded{i}") for i in range(NRAW)]
        hi_ready, lo_ready, weights_used = sem("hi_ready"), sem("lo_ready"), sem("weights_used")
        bank_full = [sem(f"bank_full{i}") for i in range(8)]
        bank_done = [sem(f"bank_done{i}") for i in range(8)]

        def pj(job):
            return ps[JOBS[job][0]]

        def wait_full(eng, job):
            b, _, full, end, _ = JOBS[job]
            if end is not None:
                eng.wait_ge(weights_used, end + 1)
            else:
                eng.wait_ge(bank_full[b], full + 1)

        def wait_done(eng, job):
            b, k = JOBS[job][:2]
            eng.wait_ge(bank_done[b], k + 1)

        def release(ins, job):
            ins.then_inc(bank_done[JOBS[job][0]], 1)

        def xpair(k):
            return xhi[:, k, :], xlo[:, k, :]

        def GATE_UNIT(e):
            return NB + 2 + 3 * (e - 1)

        def halves(v, do, sync, buf, hi, lo, k0, ready):
            for j in range(2):
                b3 = buf[:, j, :].rearrange("p (c s) -> p c s", s=S)
                do(v.tensor_scalar(hi[:, k0 + 2 * j:k0 + 2 * j + 2, :], b3, 0.5, None, ALU.mult))
            sync()
            for j in range(2):
                b3 = buf[:, j, :].rearrange("p (c s) -> p c s", s=S)
                d = slice(k0 + 2 * j, k0 + 2 * j + 2)
                v.scalar_tensor_tensor(lo[:, d, :], b3, 0.5, hi[:, d, :].bitcast(f32), ALU.mult, ALU.subtract).then_inc(sem(ready), 1)

        block = ctx.enter_context(nc.Block())

        @block.sync
        def _(sp):
            sp.dma_start(x[:, :, :], x_d).then_inc(sem("x_loaded"), 16)
            sp.dma_start(cst[:, :], cst_d).then_inc(sem("cst_loaded"), 16)
            sp.dma_start(sml[:, :], sml_d).then_inc(sem("sml_loaded"), 16)
            sp.dma_start(posi[:, :], pos_d).then_inc(sem("pos_loaded"), 16)
            for n in range(NRAW):
                sp.dma_start(raw[:, n, :], w_d[n]).then_inc(raw_loaded[n], 16)
            with sp.Fori(1, NU // NRAW) as i:
                for j in range(NRAW):
                    sp.wait_ge(lo_ready, i * NRAW + (j + 1 - NRAW))
                    sp.dma_start(raw[:, j, :], w_d[bass.ds(i * NRAW + j, 1), :, :].rearrange("u p n -> (u p) n")).then_inc(raw_loaded[j], 16)
            for n in range(NU // NRAW * NRAW, NU):
                sp.wait_ge(lo_ready, n + 1 - NRAW)
                sp.dma_start(raw[:, n % NRAW, :], w_d[n]).then_inc(raw_loaded[n % NRAW], 16)

        @block.gpsimd
        def _(pool):
            def lo(value, j):
                pool.wait_ge(hi_ready, value)
                pool.tensor_tensor(wlo[:, j, :], raw[:, j, :], whi[:, j, :].bitcast(f32), ALU.subtract).then_inc(lo_ready, 1)

            with pool.Fori(0, NU // NSPL) as i:
                for j in range(NSPL):
                    lo(i * NSPL + (j + 1), j)
            for n in range(NU // NSPL * NSPL, NU):
                lo(n + 1, n % NSPL)

        @block.scalar
        def _(act):
            made = [0]
            step = [0]
            hi_count = [0]

            def hi_upto(last):
                while made[0] <= min(last, NU - 1):
                    n = made[0]
                    act.wait_ge(raw_loaded[n % NRAW], 16 * (n // NRAW + 1))
                    if n >= NSPL:
                        act.wait_ge(weights_used, n - NSPL + 1)
                    act.activation(whi[:, n % NSPL, :], raw[:, n % NRAW, :], ACT.Copy).then_inc(hi_ready, 1)
                    made[0] += 1

            def chain(ins):
                step[0] += 1
                ins.then_inc(sem("act_step"), 1)
                act.wait_ge(sem("act_step"), step[0])

            def norm_squares(name, src, dst):
                for t in range(TT):
                    act.activation(dst[:, t, :], src[:, t, :], ACT.Square, accum_out=stat[:, STAT[name] + t:STAT[name] + t + 1]).then_inc(sem("squares_" + name), 1)

            def hi_parts(name, nct, k0, gain=None):
                for c in range(nct):
                    job = (name, c // 2)
                    if c % 2 == 0:
                        wait_full(act, job)
                    act.activation(xhi[:, k0 + c, :], pj(job)[:, c % 2 * S:c % 2 * S + S], ACT.Copy,
                                   scale=1.0 if gain is None else gain[:, c:c + 1]).then_inc(sem("xhi_ready"), 1)

            def copy(job, dst, cols=slice(None), scale=1.0, rows=slice(None)):
                wait_full(act, job)
                release(act.activation(dst, pj(job)[rows, cols], ACT.Copy, scale=scale), job)

            def tanh_half(job, dst):
                wait_full(act, job)
                return act.activation(dst, pj(job)[:, :].rearrange("p (c s) -> p c s", s=S), ACT.Tanh, scale=0.5)

            hi_upto(2)
            act.wait_ge(sem("rope_arg"), 1)
            act.activation(ropt[:, 6:8, :], ropt[:, 4:6, :], ACT.Sin).then_inc(sem("rope_sin"), 1)
            act.wait_ge(sem("x_loaded"), 16)
            norm_squares("x", x, xn)
            act.wait_ge(sem("sml_loaded"), 16)
            hi_parts("x", 8, 0, D("g_pre"))
            for name, c0, w in (("qn", 0, 512), ("kv1", 512, 512), ("kv2", 1024, 280)):
                hi_upto(UNIT[name][0] + 2)
                hi_upto(UNIT[name][1] + 2)
                for t in range(TT):
                    copy((name, t), nq[:, t, c0:c0 + w], slice(0, w))
            for name, c0 in (("qr", 0), ("kr", 512)):
                hi_upto(UNIT[name][0] + 2)
                hi_upto(UNIT[name][1] + 2)
                for t in range(TT):
                    copy((name, t), qk[:, t, c0:c0 + 512])
            act.wait_ge(sem("gates_in"), TT)
            act.activation(stat[:, 192:240], stat[:, 192:240], ACT.Tanh, scale=0.5).then_inc(sem("gates_tanh"), 1)
            hi_upto(UNIT["vr0"][1] + 2)
            hi_upto(UNIT["vr1"][1] + 2)
            for j in range(2):
                copy(("qT", j), qT[:, 2 * j:2 * j + 2, :].rearrange("p c s -> p (c s)"), scale=0.125)
            wait_done(act, ("cT", 0))
            act.activation(xchi[:, :, :, :], xcf[:, :, :, :], ACT.Copy).then_inc(sem("xchi_ready"), 1)
            hi_upto(UNIT["w1v"][1] + 2)
            act.wait_ge(sem("gelu_in"), 1)
            act.activation(hg[:, 2, :], hg[:, 1, :], ACT.Tanh, scale=0.7978845608028654).then_inc(sem("gelu_tanh"), 1)
            hi_upto(UNIT["zn"][1] + 2)

            def silu_gate(name, dst, c0):
                for j in range(2):
                    tanh_half((name, j), dst[:, c0 + 2 * j:c0 + 2 * j + 2, :]).then_inc(sem("tanh_" + name), 1)

            silu_gate("zn", znT, 0)
            act.wait_ge(sem("cmp_scores"), 1)
            act.activation(pr[:, 0, :].rearrange("p (h c) -> p h c", c=32)[:, :, 0:15], cs[:, :, :], ACT.Exp).then_inc(sem("cmp_exp"), 1)
            copy(("Tc", 0), pT[:, 0, :])

            def exps(S_, u, p_buf, sums, width0, readers):
                act.wait_ge(sem("max_ready"), MAXN[(S_, u)])
                for t in range(TT):
                    c = slice(0, width0) if t == 0 else slice(width0, width0 + S)
                    k = 2 * (u % 8)
                    ins = act.activation(p_buf[:, c], pj((S_, u))[:, c], ACT.Exp, bias=stat[:, NMAX + k + t:NMAX + k + t + 1],
                                         accum_out=stat[:, sums + k + t:sums + k + t + 1])
                release(ins, (S_, u))

            fill = {0: "zr0", 2: "zr0", 4: "zr1", 6: "zr1", 7: "ma0", 9: "ma0", 11: "ma1", 13: "ma1"}
            seen = {}
            for u in range(16):
                if u >= 2:
                    wait_full(act, ("T", u - 2))
                exps("S", u, pr[:, u % 2, :], SUMS, P, None)
                if u in fill:
                    name = fill[u]
                    k = seen[name] = seen.get(name, -1) + 1
                    hi_upto(UNIT[name][k] + 2)
                    if k == 1:
                        if name[0] == "z":
                            silu_gate(name, zrT, 4 * int(name[2]))
                        else:
                            for j in range(2):
                                release(tanh_half((name, j), maT[:, 4 * int(name[2]) + 2 * j:4 * int(name[2]) + 2 * j + 2, :]), (name, j))
            act.dma_start(decay[:, :, :], dec_d).then_inc(sem("decay_loaded"), 16)
            for h in range(4):
                copy(("QK", h), qkT[:, h % 2, :])
                hi_upto(UNIT[f"mb{h // 2}"][h % 2] + 2)
                if h % 2:
                    for j in range(2):
                        c = 4 * (h // 2) + 2 * j
                        release(tanh_half((f"mb{h // 2}", j), mbT[:, c:c + 2, :]), (f"mb{h // 2}", j))
            wait_done(act, ("on", 1))
            act.dma_start(npost[:, :], npost_d).then_inc(sem("npost_loaded"), 16)
            hi_upto(UNIT["wo0"][0])
            hi_upto(UNIT["wo1"][1] + 2)
            for t in range(TT):
                if t:
                    act.wait_ge(sem("squares_post"), 2)
                for i in range(2):
                    wait_full(act, (f"wo{i}", t))
                    k = STAT["post"] + 2 * t + i
                    act.activation(tmp[:, i, :], pj((f"wo{i}", t))[:, :], ACT.Square, accum_out=stat[:, k:k + 1]).then_inc(sem("squares_post"), 1)
            for t in range(TT):
                act.wait_ge(sem("x1_ready"), t + 1)
                act.activation(xn[:, t, :], x[:, t, :], ACT.Square, accum_out=stat[:, STAT["u"] + t:STAT["u"] + t + 1]).then_inc(sem("squares_u"), 1)
            hi_parts("u", 8, 0, D("g_mix"))
            for name, dst, w in (("pa", pa, 416), ("pb", pb, 288)):
                hi_upto(UNIT[name][0] + 2)
                hi_upto(UNIT[name][1] + 2)
                for t in range(TT):
                    copy((name, t), dst[:, t, :], slice(0, w))
            for t in range(TT):
                wait_done(act, ("pa", t))
                wait_done(act, ("pb", t))
                act.activation(qm[:, t, 0:384], pa[:, t, 32:416], ACT.Square, accum_out=stat[:, STAT["qa"] + t:STAT["qa"] + t + 1]).then_inc(sem("squares_qa"), 1)
                act.activation(qm[:, t, 384:640], pb[:, t, 0:256], ACT.Square, accum_out=stat[:, STAT["ck"] + t:STAT["ck"] + t + 1]).then_inc(sem("squares_qa"), 1)
            act.wait_ge(sem("dt_in"), 1)
            act.activation(dts[:, 1, :], dts[:, 1, :], ACT.Exp).then_inc(sem("dt_exp"), 1)
            act.activation(dts[:, 5, 0:32], D("a_log"), ACT.Exp).then_inc(sem("dt_exp"), 1)
            act.wait_ge(sem("dt_one"), 1)
            act.activation(dts[:, 3, :], dts[:, 2, :], ACT.Ln).then_inc(sem("dt_ln"), 1)
            hi_parts("qa", 3, 8, D("g_qa"))
            hi_parts("ck", 2, 11, D("g_ckv"))
            for i in range(3):
                hi_upto(UNIT[f"wq{i}"][0] + 2)
                for t in range(TT):
                    copy((f"wq{i}", t), qm[:, t, 512 * i:512 * i + 512], scale=96 ** -0.5)
            hi_upto(UNIT["kn"][0] + 2)
            for j in range(4):
                wait_full(act, ("kn", j))
                v = pj(("kn", j))[:, :].rearrange("p (c s) -> p c s", s=S)
                act.activation(km[0:64, 4 * j:4 * j + 4:2, :], v[0:64, :, :], ACT.Copy)
                release(act.activation(km[0:64, 4 * j + 1:4 * j + 4:2, :], v[64:128, :, :], ACT.Copy), ("kn", j))
            hi_upto(UNIT["vv"][0] + 2)
            copy(("mQ", 0), qmT[0:96, 0, :], rows=slice(0, 96))

            def conv_first(i):
                for j in range(2):
                    job = (f"xbc{i}", j)
                    wait_full(act, job)
                    if i == 0:
                        act.wait_ge(sem("conv_halved"), 2)
                    if 2 * i + j >= 2:
                        act.wait_ge(sem("silu_done"), 2 * i + j - 1)
                    for c in range(2):
                        k = 4 * i + 2 * j + c
                        act.activation(cv[:, j, c, :], pj(job)[:, c * S:c * S + S], ACT.Identity,
                                       scale=sml[:, CW + 72 + k:CW + 73 + k], bias=sml[:, CB_ + k:CB_ + k + 1]).then_inc(sem("conv_first"), 1)

            def conv_tanh(i):
                for j in range(2):
                    wait_done(act, (f"xbc{i}", j))
                    act.activation(xbc[:, 4 * i + 2 * j:4 * i + 2 * j + 2, :], cv[:, j, :, :], ACT.Tanh).then_inc(sem("conv_tanh"), 1)

            for u in range(16):
                if u % 2 == 0 and u < 14:
                    p = u // 2 + 1
                    if p >= 2:
                        wait_full(act, ("mS", 2 * p - 3))
                    copy(("mQ", p), qmT[0:96, p % 2, :], rows=slice(0, 96))
                if u >= 2:
                    wait_full(act, ("mT", u - 2))
                exps("mS", u, pr2[:, u % 2, :], SUMS, P, None)
                if u < 12:
                    hi_upto(UNIT[f"xbc{u // 2}"][u % 2] + 2)
                if u < 12 and u % 2:
                    conv_first(u // 2)
                if u % 2 == 0 and 2 <= u <= 12:
                    conv_tanh(u // 2 - 1)
            hi_parts("om", 8, 8)
            for i in range(2):
                hi_upto(UNIT[f"gm{i}"][1] + 2)
                for j in range(2):
                    c = 4 * i + 2 * j
                    release(tanh_half((f"gm{i}", j), ymT[:, c:c + 2, :]), (f"gm{i}", j))
            hi_upto(UNIT["ym1"][1] + 2)
            wait_full(act, ("acum", 0))
            act.activation(dts[:, 6, 32:64], pj(("acum", 0))[:, 32:64], ACT.Exp).then_inc(sem("eac_ready"), 1)
            wait_done(act, ("acum", 0))
            act.activation(dts[:, 6, 0:32], dts[:, 6, 0:32], ACT.Exp).then_inc(sem("dte_ready"), 1)
            copy(("Bt", 0), btok[:, :])
            for i in range(8):
                copy(("xt", i), xtok[:, i // 4, i % 4 * 512:i % 4 * 512 + 512])

            def scan_unit(n):
                hi_upto(UNIT[n][1] + 2)
                k = int(n[-1])
                for j in range(2):
                    if n[0] == "z":
                        wait_full(act, (n, j))
                        act.activation(zt[:, j, 512 * k:512 * k + 512], pj((n, j))[:, :], ACT.Tanh, scale=0.5).then_inc(sem("tanh_z"), 1)
                    else:
                        release(tanh_half((n, j), gsT[:, 4 * k + 2 * j:4 * k + 2 * j + 2, :]), (n, j))

            scan_unit("z0")
            for i in range(8):
                g, t = i // 2, i % 2
                for q in (2 * i, 2 * i + 1):
                    if q >= 2:
                        act.wait_ge(sem("segM_ready"), q - 1)
                    wait_full(act, ("seg", q))
                    release(act.activation(segE[:, q % 2, :], pj(("seg", q))[:, :], ACT.Exp), ("seg", q))
                if t == 0:
                    if g >= 1:
                        wait_full(act, ("off", g - 1))
                    copy(("state", g), st[:, :])
                if i < 5:
                    scan_unit(SCAN_UNITS[i + 1])
                act.wait_ge(sem("y_gated"), i + 1)
                act.activation(yt[:, 1, :], zt[:, t, 512 * g:512 * g + 512], ACT.Square, accum_out=stat[:, STAT["y"] + i:STAT["y"] + i + 1]).then_inc(sem("squares_y"), 1)
            hi_parts("y", 16, 0, D("g_ssd"))
            act.dma_start(memt[:, :, :], mem_d).then_inc(sem("mem_loaded"), 16)
            hi_upto(UNIT["ys1"][-1])
            act.wait_ge(sem("mem_loaded"), 16)
            norm_squares("mem", memt, xn)
            hi_upto(UNIT["ys1"][-1] + 2)
            hi_parts("mem", 8, 8, D("g_mem"))
            hi_upto(UNIT["wp1"][1] + 2)
            for t in range(TT):
                wait_done(act, ("wp1", t))
                act.activation(xn[:, t, :], x[:, t, :], ACT.Square, accum_out=stat[:, STAT["h"] + t:STAT["h"] + t + 1]).then_inc(sem("squares_h"), 1)
            for i in range(2):
                hi_upto(UNIT[f"xk{i}"][1] + 2)
                for j in range(2):
                    c = 4 * i + 2 * j
                    copy((f"xk{i}", j), kx[:, c:c + 2, :].rearrange("p c s -> p (c s)"))
            hi_upto(UNIT["xv1"][1] + 2)
            hi_parts("h", 8, 0, D("g_xa"))
            for i in range(2):
                hi_upto(UNIT[f"xq{i}"][1] + 2)
                for j in range(2):
                    c = 4 * i + 2 * j
                    copy((f"xq{i}", j), qx[:, c:c + 2, :].rearrange("p c s -> p (c s)"), scale=0.0625)
            for h in range(4):
                if h >= 2:
                    wait_full(act, ("xT", h - 2))
                exps("xS", h, px[:, h % 2, :], SUMS, S, None)
                if h >= 2:
                    wait_full(act, ("xO", h - 2))
                copy(("xT", h), pxT[:, h % 2, :])
                wait_full(act, ("xO", h))
                act.activation(xhi[:, 8 + 2 * h:10 + 2 * h, :], pj(("xO", h))[:, :].rearrange("p (c s) -> p c s", s=S), ACT.Copy).then_inc(sem("xhi_ready"), 1)
            hi_upto(UNIT["xo1"][1] + 2)
            for t in range(TT):
                wait_done(act, ("xo1", t))
                act.activation(xn[:, t, :], x[:, t, :], ACT.Square, accum_out=stat[:, STAT["m"] + t:STAT["m"] + t + 1]).then_inc(sem("squares_m"), 1)
            hi_parts("m", 8, 0, D("g_moe"))
            hi_upto(UNIT["rt"][0] + 2)
            act.wait_ge(sem("router_arg"), 1)
            act.activation(rtl[:, 2, 0:8], rtl[:, 2, 0:8], ACT.Exp).then_inc(sem("router_exp"), 1)
            act.wait_ge(sem("router_arg"), 2)
            act.activation(rtl[:, 2, 8:10], rtl[:, 2, 8:10], ACT.Exp).then_inc(sem("router_exp"), 1)
            wait_done(act, ("cb", 0))
            act.dma_start(scratch, combt[:, :]).then_inc(sem("comb_out"), 16)
            act.wait_ge(sem("comb_out"), 16)
            act.dma_start(comb[:, :, :].rearrange("p e s -> p (e s)"),
                          scratch.rearrange("e s -> (e s)").partition_broadcast(P)).then_inc(sem("comb_loaded"), 16)
            act.dma_start(nfin[:, :], nfin_d).then_inc(sem("nfin_loaded"), 16)

            def expert_act(e, i, last=False):
                n, s = GATE_UNIT(e), e % 2

                def hi(m):
                    act.wait_ge(raw_loaded[m % NRAW], i * 32 + 16 * (m // NRAW + 1))
                    act.wait_ge(weights_used, i * 6 + (m - NSPL + 1))
                    act.activation(whi[:, m % NSPL, :], raw[:, m % NRAW, :], ACT.Copy).then_inc(hi_ready, 1)

                hi(n + 2)
                hi(n + 3)
                act.wait_ge(weights_used, i * 6 + (n + 1))
                if e >= 2:
                    act.wait_ge(sem("gated"), i * 2 + (e - 1))
                act.activation(sg[:, s, :], ps[2 * s][:, :], ACT.Silu).then_inc(sem("silu_ready"), 1)
                if not last:
                    hi(n + 4)

            hi_upto(NB + 3)
            act.wait_ge(weights_used, NB + 1)
            act.activation(sg[:, 0, :], ps[0][:, :], ACT.Silu).then_inc(sem("silu_ready"), 1)
            expert_act(1, 0)
            expert_act(2, 0)
            with act.Fori(0, (NEXP - 4) // 2) as i:
                expert_act(3, i)
                expert_act(4, i)
            expert_act(NEXP - 1, 0, last=True)
            for t in range(TT):
                act.wait_ge(sem("h3_ready"), t + 1)
                act.activation(xn[:, t, :], x[:, t, :], ACT.Square, accum_out=stat[:, STAT["f"] + t:STAT["f"] + t + 1]).then_inc(sem("squares_f"), 1)
            for t in range(TT):
                act.wait_ge(sem("out_ready"), t + 1)
                act.dma_start(out_d[:, t, :], xn[:, t, :]).then_inc(sem("out_stored"), 16)
            act.wait_ge(sem("out_stored"), 32)

        @block.vector
        def _(dve):
            v = nc.vector
            steps = [0]
            hi_seen = [0]

            def do(ins):
                steps[0] += 1
                ins.then_inc(sem("dve_step"), 1)

            def sync():
                dve.wait_ge(sem("dve_step"), steps[0])

            def bc(ap, shape):
                return ap.to_broadcast(shape)

            def col(k, n=1):
                return stat[:, k:k + n]

            def inverse_root(dst, src, n, factor=1.0):
                w, t = col(MISC + 6, n), col(MISC + 10, n)
                do(v.tensor_scalar(w, src, factor, EPS, ALU.mult, ALU.add))
                sync()
                do(v.tensor_scalar(dst.bitcast(i32), w.bitcast(i32), -0.5, 1597463007.0, ALU.mult, ALU.add))
                sync()
                for _ in range(3):
                    if n == 1:
                        do(v.scalar_tensor_tensor(t, dst, w, dst, ALU.mult, ALU.mult))
                    else:
                        do(v.tensor_tensor(t, dst, dst, ALU.mult))
                        sync()
                        do(v.tensor_tensor(t, t, w, ALU.mult))
                    sync()
                    do(v.tensor_scalar(t, t, -0.5, 1.5, ALU.mult, ALU.add))
                    sync()
                    do(v.tensor_tensor(dst, dst, t, ALU.mult))
                    sync()

            def rstd(name, n, width, extra=0):
                k = STAT[name] + extra
                inverse_root(col(k + RSTD, n), col(k, n), n, 1.0 / width)

            def norm(name, src, dst, ready):
                for t in range(TT):
                    dve.wait_ge(sem("squares_" + name), t + 1)
                    rstd(name, 1, DM, t)
                    k = STAT[name] + RSTD + t
                    v.tensor_scalar(dst[:, t, :], src[:, t, :], col(k), None, ALU.mult).then_inc(sem(ready), 1)

            def lo_parts(name, nct, k0, gain=None):
                for c in range(nct):
                    job = (name, c // 2)
                    if c % 2 == 0:
                        hi_seen[0] += min(2, nct - c)
                        dve.wait_ge(sem("xhi_ready"), hi_seen[0])
                    src = pj(job)[:, c % 2 * S:c % 2 * S + S]
                    if gain is None:
                        ins = v.tensor_tensor(xlo[:, k0 + c, :], src, xhi[:, k0 + c, :].bitcast(f32), ALU.subtract)
                    else:
                        ins = v.scalar_tensor_tensor(xlo[:, k0 + c, :], src, gain[:, c:c + 1], xhi[:, k0 + c, :].bitcast(f32), ALU.mult, ALU.subtract)
                    if c % 2 or c == nct - 1:
                        release(ins, job)

            def copy(job, dst, rows=slice(None), cols=slice(None)):
                wait_full(dve, job)
                release(v.tensor_copy(dst, pj(job)[rows, cols]), job)

            def rotate(x1, x2, cos, sin, t4, ready, nth=1):
                do(v.tensor_tensor(t4[0], x1, cos, ALU.mult))
                do(v.tensor_tensor(t4[1], x2, sin, ALU.mult))
                do(v.tensor_tensor(t4[2], x2, cos, ALU.mult))
                do(v.tensor_tensor(t4[3], x1, sin, ALU.mult))
                sync()
                do(v.tensor_tensor(x1, t4[0], t4[1], ALU.subtract))
                v.tensor_tensor(x2, t4[2], t4[3], ALU.add).then_inc(sem(ready), 1)
                sync()
                dve.wait_ge(sem(ready), nth)

            dve.wait_ge(sem("cst_loaded"), 16)
            v.tensor_copy(identb[:, :], ident).then_inc(sem("masks_ready"), 1)
            v.tensor_copy(negb[:, :], C("negmask")).then_inc(sem("masks_ready"), 1)
            dve.wait_ge(sem("pos_loaded"), 16)
            do(v.tensor_copy(col(MISC, 2), posi[:, :]))
            sync()
            ang, kf = ropt[:, 0, :], ropt[:, 1, :]
            ki = ropt[:, 3, :].bitcast(i32)
            sa, ca = ropt[:, 4, :], ropt[:, 5, :]
            for t in range(TT):
                do(v.tensor_scalar(ang[:, 16 * t:16 * t + 16], C("invf"), col(MISC + t), None, ALU.mult))
            sync()
            do(v.tensor_scalar(ki, ang, 1.0 / TWO_PI, None, ALU.mult))
            sync()
            do(v.tensor_copy(kf, ki))
            sync()
            for part in PI_PARTS:
                do(v.scalar_tensor_tensor(ang, kf, -part, ang, ALU.mult, ALU.add))
                sync()
            do(v.tensor_scalar(ca, ang, TWO_PI / 4, None, ALU.add))
            do(v.tensor_copy(sa, ang))
            sync()
            both = ropt[:, 4:6, :]
            turn = ropt[:, 1:3, :]
            for op, sign in ((ALU.is_gt, 1.0), (ALU.is_lt, -1.0)):
                do(v.tensor_scalar(turn, both, sign * TWO_PI / 2, -sign * TWO_PI, op, ALU.mult))
                sync()
                do(v.tensor_tensor(both, both, turn, ALU.add))
                sync()
            v.tensor_scalar(both, both, 3.1415925, -3.1415925, ALU.min, ALU.max).then_inc(sem("rope_arg"), 1)
            dve.wait_ge(sem("sml_loaded"), 16)
            v.tensor_scalar(D("conv_w"), D("conv_w"), 0.5, None, ALU.mult).then_inc(sem("conv_halved"), 1)
            v.tensor_scalar(D("conv_b"), D("conv_b"), 0.5, None, ALU.mult).then_inc(sem("conv_halved"), 1)
            do(v.memset(pr[:, 0, :], 0.0))
            do(v.memset(vcb[:, :, :, :], 0.0))
            sync()
            norm("x", x, xn, "xn_ready")
            lo_parts("x", 8, 0, D("g_pre"))

            for n in ("qn", "kv1"):
                for t in range(TT):
                    wait_done(dve, (n, t))
            heads = nq[:, :, 0:896].rearrange("p t (h d) -> p t h d", d=64)
            t4 = [ropetmp[:, k, 0:224].rearrange("p (t h d) -> p t h d", t=TT, d=8) for k in range(4)]
            cosb = C("cos").rearrange("p (t d) -> p t d", t=TT).unsqueeze(2).to_broadcast([P, TT, 14, 8])
            sinb = C("sin").rearrange("p (t d) -> p t d", t=TT).unsqueeze(2).to_broadcast([P, TT, 14, 8])
            rotate(heads[:, :, :, 0:8], heads[:, :, :, 8:16], cosb, sinb, t4, "nq_rotated")
            for t in range(TT):
                wait_done(dve, ("kv2", t))
                v.tensor_tensor(col(GATE + 24 * t, 24), nq[:, t, 1280:1304], D("b_gate"), ALU.add).then_inc(sem("gates_in"), 1)
            for i in range(2):
                for t in range(TT):
                    copy((f"vr{i}", t), vr[:, t, 512 * i:512 * i + 512])
            wait_full(dve, ("kT", 0))
            for g in range(2):
                for r in range(2):
                    ins = v.tensor_copy(kT[64 * r:64 * r + 64, g, :], pj(("kT", 0))[64 * g:64 * g + 64, :])
                    if (g, r) == (1, 1):
                        release(ins, ("kT", 0))
            wait_full(dve, ("cT", 0))
            for kv in range(2):
                pe_ = D("pe_k") if kv == 0 else D("pe_v")
                for j in range(2):
                    for g in range(2):
                        for late in range(2):
                            src = pj(("cT", 0))[64 * g:64 * g + 64, kv * S:kv * S + S].rearrange("p (c r) -> p r c", r=16)[:, j::2, late:late + 15]
                            dst = xcf[64 * j:64 * j + 64, kv, 8 * late:8 * late + 8, 15 * g:15 * g + 15]
                            code = pe_[64 * j:64 * j + 64, 8 * late:8 * late + 8].unsqueeze(2).to_broadcast([64, 8, 15])
                            ins = v.tensor_tensor(dst, src, code, ALU.add)
            release(ins, ("cT", 0))
            dve.wait_ge(sem("xchi_ready"), 1)
            v.tensor_tensor(xclo[:, :, :, :], xcf[:, :, :, :], xchi[:, :, :, :].bitcast(f32), ALU.subtract).then_inc(sem("xclo_ready"), 1)
            wait_full(dve, ("hid", 0))
            do(v.tensor_copy(hg[:, 0, :].rearrange("p (a c) -> p a c", c=30), pj(("hid", 0))[:, 0:128].rearrange("p (a c) -> p a c", c=32)[:, :, 0:30]))
            sync()
            v.tensor_copy(stat[:, MISC + 2:MISC + 3], pj(("hid", 0))[:, 0:1]).then_inc(bank_done[JOBS[("hid", 0)][0]], 1)
            do(v.tensor_tensor(hg[:, 1, :], hg[:, 0, :], hg[:, 0, :], ALU.mult))
            sync()
            do(v.scalar_tensor_tensor(hg[:, 3, :], hg[:, 1, :], 0.044715, hg[:, 0, :], ALU.mult, ALU.mult))
            sync()
            v.tensor_tensor(hg[:, 1, :], hg[:, 3, :], hg[:, 0, :], ALU.add).then_inc(sem("gelu_in"), 1)
            dve.wait_ge(sem("gelu_tanh"), 1)
            do(v.scalar_tensor_tensor(hg[:, 3, :], hg[:, 2, :], 1.0, hg[:, 0, :], ALU.add, ALU.mult))
            sync()
            v.tensor_scalar(hg[:, 3, :], hg[:, 3, :], 0.5, None, ALU.mult).then_inc(sem("gelu_ready"), 1)
            dve.wait_ge(sem("gates_tanh"), 1)
            do(v.tensor_scalar(col(GATE, 48), col(GATE, 48), 0.5, 0.5, ALU.mult, ALU.add))

            def silu_gate(name, dst, c0):
                for j in range(2):
                    dve.wait_ge(sem("tanh_" + name), j + 1)
                    d = dst[:, c0 + 2 * j:c0 + 2 * j + 2, :]
                    release(v.scalar_tensor_tensor(d, d, 1.0, pj((name, j))[:, :].rearrange("p (c s) -> p c s", s=S), ALU.add, ALU.mult), (name, j))

            silu_gate("zn", znT, 0)
            wait_full(dve, ("kvc", 0))
            do(v.tensor_copy(kcT[:, 0:30], pj(("kvc", 0))[:, 0:30]))
            for g in range(2):
                for i in range(4):
                    ins = v.tensor_copy(vcb[32 * i:32 * i + 15, g, i, :], pj(("kvc", 0))[0:15, 64 + 64 * g:128 + 64 * g])
            release(ins, ("kvc", 0))
            wait_full(dve, ("Sc", 0))
            cs4 = cs[:, :, :].rearrange("p (t h) c -> p t h c", t=TT)
            release(v.tensor_tensor(cs4, pj(("Sc", 0))[:, :].rearrange("p (t h c) -> p t h c", t=TT, c=32)[:, :, :, 0:15],
                                    C("cmpmask").rearrange("p (t c) -> p t c", t=TT).unsqueeze(2).to_broadcast([P, TT, 8, 15]), ALU.add), ("Sc", 0))
            wait_done(dve, ("Sc", 0))
            do(v.tensor_reduce(col(CMAX, 16), cs[:, :, :], AX.X, ALU.max))
            sync()
            do(v.tensor_scalar(col(CMAX, 16), col(CMAX, 16), -1e29, None, ALU.max))
            sync()
            v.tensor_tensor(cs[:, :, :], cs[:, :, :], col(CMAX, 16).unsqueeze(2).to_broadcast([P, 16, 15]), ALU.subtract).then_inc(sem("cmp_scores"), 1)
            dve.wait_ge(sem("cmp_exp"), 1)
            do(v.tensor_reduce(col(CSUM, 16), pr[:, 0, :].rearrange("p (h c) -> p h c", c=32)[:, :, 0:15], AX.X, ALU.add))
            sync()
            do(v.tensor_scalar(col(CSUM, 16), col(CSUM, 16), 1.1754944e-38, None, ALU.max))
            sync()
            do(v.reciprocal(col(CSUM, 16), col(CSUM, 16)))
            sync()
            gates = stat[:, GATE:GATE + 48].rearrange("p (t h b) -> p t h b", t=TT, b=3)
            do(v.tensor_tensor(col(CGATE, 16).rearrange("p (t h) -> p t h", t=TT), col(CSUM, 16).rearrange("p (t h) -> p t h", t=TT), gates[:, :, :, 0], ALU.mult))
            sync()
            def maxima(job, width0, u):
                wait_full(dve, job)
                k = NMAX + 2 * (u % 8)
                v.tensor_reduce(col(k), pj(job)[:, 0:width0], AX.X, ALU.max, negate=True)
                v.tensor_reduce(col(k + 1), pj(job)[:, width0:width0 + S], AX.X, ALU.max, negate=True).then_inc(sem("max_ready"), 1)

            def compressed_out(t):
                wait_full(dve, ("Oc", t))
                release(v.tensor_tensor(oacc[:, t, :].rearrange("p (h d) -> p h d", d=64), pj(("Oc", t))[:, :].rearrange("p (h d) -> p h d", d=64),
                                        col(CGATE + 8 * t, 8).unsqueeze(2).to_broadcast([P, 8, 64]), ALU.mult), ("Oc", t))

            def attention_out(q):
                br, h0 = q // 2 + 1, 4 * (q % 2)
                wait_full(dve, ("O", q))
                k = 2 * (4 * q % 8)
                do(v.reciprocal(col(RSUM + k, 8), col(SUMS + k, 8)))
                sync()
                gf = col(GF + k, 8).rearrange("p (h t) -> p h t", t=TT)
                do(v.tensor_tensor(gf, col(RSUM + k, 8).rearrange("p (h t) -> p h t", t=TT),
                                   gates[:, :, h0:h0 + 4, br].rearrange("p t h -> p h t"), ALU.mult))
                sync()
                src = pj(("O", q))[:, :].rearrange("p (h t d) -> p h t d", t=TT, d=64)
                for t in range(TT):
                    ins = v.tensor_tensor(tmp[:, t, 0:256].rearrange("p (h d) -> p h d", d=64), src[:, :, t, :],
                                          gf[:, :, t].unsqueeze(2).to_broadcast([P, 4, 64]), ALU.mult)
                release(ins, ("O", q))
                wait_done(dve, ("O", q))
                for t in range(TT):
                    d = oacc[:, t, 64 * h0:64 * h0 + 256]
                    v.tensor_tensor(d, d, tmp[:, t, 0:256], ALU.add).then_inc(sem("oacc_added"), 1)
                dve.wait_ge(sem("oacc_added"), 2 * (q + 1))

            qkh = qk[:, :, :].rearrange("p t (h d) -> p t h d", d=128)
            rc, rs_ = (C(n).rearrange("p (t d) -> p t d", t=TT) for n in ("rcos", "rsin"))
            maxima(("S", 0), P, 0)
            compressed_out(0)
            compressed_out(1)
            for u in range(16):
                if u < 15:
                    maxima(("S", u + 1), P, u + 1)
                copy(("T", u), pT[:, u % 2, 0:384], cols=slice(0, 384))
                if u in (2, 6):
                    silu_gate(f"zr{u // 4}", zrT, 4 * (u // 4))
                if u in (3, 5):
                    t = (u - 3) // 2
                    for n in ("qr", "kr"):
                        wait_done(dve, (n, t))
                    rotate(qkh[:, t, :, 0:64], qkh[:, t, :, 64:128], rc[:, t, :].unsqueeze(1).to_broadcast([P, 8, 64]),
                           rs_[:, t, :].unsqueeze(1).to_broadcast([P, 8, 64]),
                           [ropetmp[:, k, :].rearrange("p (h d) -> p h d", d=64) for k in range(4)], "qk_rotated", t + 1)
                if u % 4 == 0 and u:
                    attention_out(u // 4 - 1)
            attention_out(3)

            def gated_parts(job, gate, k0, slot, ready):
                wait_full(dve, job)
                buf = tmp[:, slot, :].rearrange("p (c s) -> p c s", s=S)
                release(v.scalar_tensor_tensor(buf, pj(job)[:, :].rearrange("p (c s) -> p c s", s=S), 0.5, gate, ALU.mult, ALU.mult), job)
                wait_done(dve, job)
                do(v.tensor_copy(xhi[:, k0:k0 + 2, :], buf))
                sync()
                v.tensor_tensor(xlo[:, k0:k0 + 2, :], buf, xhi[:, k0:k0 + 2, :].bitcast(f32), ALU.subtract).then_inc(sem(ready), 1)

            for j in range(2):
                gated_parts(("on", j), znT[:, 2 * j:2 * j + 2, :], 8 + 2 * j, j, "on_parts")
            dve.wait_ge(sem("decay_loaded"), 16)
            for h in range(4):
                wait_full(dve, ("A", h))
                v.tensor_tensor(pT[:, h % 2, 0:S], pj(("A", h))[:, 0:S], decay[:, h, :], ALU.mult)
                release(v.tensor_tensor(pT[:, h % 2, S:S + P], pj(("A", h))[:, S:S + P], decay[:, h, 0:P], ALU.mult), ("A", h))
                wait_full(dve, ("R", h))
                for t in range(TT):
                    do(v.bn_stats(tmp[:, 0, 8 * t:8 * t + 6], pj(("R", h))[:, t * S:t * S + S]))
                sync()
                for t in range(TT):
                    do(v.bn_aggr(tmp[:, 0, 16 + 2 * t:18 + 2 * t], tmp[:, 0, 8 * t:8 * t + 6]))
                sync()
                inverse_root(tmp[:, 0, 20:22], tmp[:, 0, 17:20:2], 2)
                for t in range(TT):
                    ins = v.tensor_scalar(xn[:, t, h * S:h * S + S], pj(("R", h))[:, t * S:t * S + S],
                                          tmp[:, 0, 16 + 2 * t:17 + 2 * t], tmp[:, 0, 20 + t:21 + t], ALU.subtract, ALU.mult)
                release(ins, ("R", h))
            for j in range(4):
                gated_parts(("or", j), zrT[:, 2 * j:2 * j + 2, :], 2 * j, j % 2, "or_parts")
            dve.wait_ge(sem("or_parts"), 4)
            for i in range(2):
                if i:
                    dve.wait_ge(sem("mT_parts"), 2)
                for name, gate, buf in (("ya", maT, tmp), ("yb", mbT, pr)):
                    for j in range(2):
                        job = (f"{name}{i}", j)
                        wait_full(dve, job)
                        c = 4 * i + 2 * j
                        release(v.scalar_tensor_tensor(buf[:, j, :].rearrange("p (c s) -> p c s", s=S), gate[:, c:c + 2, :], 1.0,
                                                       pj(job)[:, :].rearrange("p (c s) -> p c s", s=S), ALU.add, ALU.mult), job)
                wait_done(dve, (f"yb{i}", 1))
                for j in range(2):
                    do(v.tensor_tensor(pr[:, j, :], pr[:, j, :], tmp[:, j, :], ALU.add))
                sync()
                halves(v, do, sync, pr, mThi, mTlo, 4 * i, "mT_parts")
            dve.wait_ge(sem("squares_post"), 4)
            k = STAT["post"]
            pair = col(k, 4).rearrange("p (t i) -> p t i", i=2)
            do(v.tensor_tensor(col(k + RSTD, 2), pair[:, :, 0], pair[:, :, 1], ALU.add))
            sync()
            inverse_root(col(k + RSTD, 2), col(k + RSTD, 2), 2, 1.0 / DM)
            dve.wait_ge(sem("npost_loaded"), 16)
            for t in range(TT):
                for i in range(2):
                    release(v.scalar_tensor_tensor(tmp[:, i, :], pj((f"wo{i}", t))[:, :], col(k + RSTD + t), npost[:, 512 * i:512 * i + 512], ALU.mult, ALU.mult), (f"wo{i}", t))
                for i in range(2):
                    wait_done(dve, (f"wo{i}", t))
                v.tensor_tensor(x[:, t, :], x[:, t, :], tmp[:, :, :].rearrange("p a b -> p (a b)"), ALU.add).then_inc(sem("x1_ready"), 1)
                dve.wait_ge(sem("x1_ready"), t + 1)
            norm("u", x, xn, "un_ready")
            lo_parts("u", 8, 0, D("g_mix"))

            for t in range(TT):
                wait_done(dve, ("pa", t))
                do(v.tensor_tensor(dts[:, 0, 32 * t:32 * t + 32], pa[:, t, 0:32], D("dt_b"), ALU.add))
            sync()
            vv_, e_, one, ln_, den, msk = dts[:, 0, :], dts[:, 1, :], dts[:, 2, :], dts[:, 3, :], dts[:, 4, :], dts[:, 7, :]
            v.scalar_tensor_tensor(e_, vv_, -1.0, vv_, ALU.mult, ALU.min).then_inc(sem("dt_in"), 1)
            dve.wait_ge(sem("squares_qa"), 4)
            rstd("qa", 2, 384)
            rstd("ck", 2, 256)
            for t in range(TT):
                k = STAT["qa"] + RSTD + t
                v.tensor_scalar(pa[:, t, 32:416], pa[:, t, 32:416], col(k), None, ALU.mult).then_inc(sem("codes_ready"), 1)
                v.tensor_scalar(pb[:, t, 0:256], pb[:, t, 0:256], col(k + 2), None, ALU.mult).then_inc(sem("codes_ready"), 1)
            dve.wait_ge(sem("rope_sin"), 1)
            sin2, cos2 = (ropt[:, k, :].rearrange("p (t d) -> p t d", t=TT) for k in (6, 7))
            rotate(pb[:, :, 256:272], pb[:, :, 272:288], cos2, sin2,
                   [ropetmp2[:, k, 0:32].rearrange("p (t d) -> p t d", t=TT) for k in range(4)], "kp_rotated")
            dve.wait_ge(sem("dt_exp"), 2)
            v.tensor_scalar(one, e_, 1.0, None, ALU.add).then_inc(sem("dt_one"), 1)
            dve.wait_ge(sem("dt_one"), 1)
            do(v.tensor_scalar(den, one, -1.0, None, ALU.add))
            sync()
            do(v.tensor_scalar(msk, den, 0.0, None, ALU.is_equal))
            sync()
            do(v.tensor_tensor(den, den, msk, ALU.add))
            sync()
            do(v.reciprocal(den, den))
            dve.wait_ge(sem("dt_ln"), 1)
            do(v.tensor_tensor(ln_, ln_, msk, ALU.add))
            sync()
            do(v.tensor_tensor(ln_, ln_, e_, ALU.mult))
            sync()
            do(v.tensor_tensor(ln_, ln_, den, ALU.mult))
            sync()
            do(v.scalar_tensor_tensor(dts[:, 0, :], vv_, 0.0, ln_, ALU.max, ALU.add))
            sync()
            dt3 = dts[:, 0, :].rearrange("p (t h) -> p t h", t=TT)
            do(v.tensor_tensor(dts[:, 1, :].rearrange("p (t h) -> p t h", t=TT), dt3, dts[:, 5, 0:32].unsqueeze(1).to_broadcast([P, TT, 32]), ALU.mult))
            sync()
            v.tensor_scalar(dts[:, 1, :], dts[:, 1, :], -1.0, None, ALU.mult).then_inc(sem("adt_ready"), 1)
            lo_parts("qa", 3, 8, D("g_qa"))
            lo_parts("ck", 2, 11, D("g_ckv"))
            wait_full(dve, ("kp", 0))
            release(v.tensor_copy(km[64:96, :, :], pj(("kp", 0))[0:32, 0:S].unsqueeze(1).to_broadcast([32, 16, S])), ("kp", 0))
            for i in range(3):
                for t in range(TT):
                    wait_done(dve, (f"wq{i}", t))
            for t in range(TT):
                qh = qm[:, t, :].rearrange("p (h d) -> p h d", d=96)
                rotate(qh[:, :, 64:80], qh[:, :, 80:96], cos2[:, t, :].unsqueeze(1).to_broadcast([P, 16, 16]),
                       sin2[:, t, :].unsqueeze(1).to_broadcast([P, 16, 16]),
                       [ropetmp2[:, k, :].rearrange("p (h d) -> p h d", d=16) for k in range(4)], "qm_rotated", t + 1)
            for t in range(TT):
                for i in range(2):
                    copy(("vv", 2 * t + i), vm[:, t, 512 * i:512 * i + 512])

            def latent_out(q):
                wait_full(dve, ("mO", q))
                k = 2 * (4 * q % 8)
                do(v.reciprocal(col(RSUM + k, 8), col(SUMS + k, 8)))
                sync()
                rs2 = col(RSUM + k, 8).rearrange("p (h t) -> p h t", t=TT)
                src = pj(("mO", q))[:, :].rearrange("p (h t d) -> p h t d", t=TT, d=64)
                for t in range(TT):
                    for c in range(2):
                        d = qm[:, t, 384 * q + 192 * c:384 * q + 192 * c + P].rearrange("p (h d) -> p h d", d=64)
                        ins = v.tensor_tensor(d, src[:, 2 * c:2 * c + 2, t, :], rs2[:, 2 * c:2 * c + 2, t].unsqueeze(2).to_broadcast([P, 2, 64]), ALU.mult)
                release(ins, ("mO", q))

            def conv_taps(i):
                for j in range(2):
                    job = (f"xbc{i}", j)
                    dve.wait_ge(sem("conv_first"), 4 * i + 2 * j + 2)
                    for back in (1, 2, 3):
                        for c in range(2):
                            k = CW + 24 * (3 - back) + 4 * i + 2 * j + c
                            d = cv[:, j, c, back:S]
                            ins = v.scalar_tensor_tensor(d, pj(job)[:, c * S:c * S + S - back], sml[:, k:k + 1], d, ALU.mult, ALU.add)
                            if back < 3 or c == 0:
                                do(ins)
                        if back < 3:
                            sync()
                    release(ins, job)

            def conv_silu(i):
                for j in range(2):
                    dve.wait_ge(sem("conv_tanh"), 2 * i + j + 1)
                    d = xbc[:, 4 * i + 2 * j:4 * i + 2 * j + 2, :]
                    v.scalar_tensor_tensor(d, d, 1.0, cv[:, j, :, :], ALU.add, ALU.mult).then_inc(sem("silu_done"), 1)

            maxima(("mS", 0), P, 0)
            for u in range(16):
                if u < 15:
                    maxima(("mS", u + 1), P, u + 1)
                copy(("mT", u), pT2[:, u % 2, :], cols=slice(0, 384))
                if u < 12 and u % 2:
                    conv_taps(u // 2)
                if u % 2 == 0 and 2 <= u <= 12:
                    conv_silu(u // 2 - 1)
                if u % 4 == 0 and u:
                    latent_out(u // 4 - 1)
            latent_out(3)
            lo_parts("om", 8, 8)
            for i in range(2):
                for j in range(2):
                    job = (f"ym{i}", j)
                    wait_full(dve, job)
                    wait_done(dve, (f"gm{i}", j))
                    d = ymT[:, 4 * i + 2 * j:4 * i + 2 * j + 2, :]
                    release(v.scalar_tensor_tensor(d, d, 1.0, pj(job)[:, :].rearrange("p (c s) -> p c s", s=S), ALU.add, ALU.mult), job)

            wait_full(dve, ("acum", 0))
            dve.wait_ge(sem("eac_ready"), 1)
            do(v.tensor_copy(dts[:, 7, 0:32], pj(("acum", 0))[:, 0:32]))
            sync()
            release(v.tensor_tensor(dts[:, 6, 0:32], pj(("acum", 0))[:, 64:96], dts[:, 7, 0:32], ALU.subtract), ("acum", 0))
            adt = dts[:, 1, :].rearrange("p (t h) -> p t h", t=TT)
            eac, weight = dts[:, 6, 32:64], dts[:, 7, 32:64]

            def seg_operand(q):
                i, k = q // 2, q % 2
                g, t = i // 2, i % 2
                if q >= 2:
                    wait_full(dve, ("seg", q - 2))
                h0 = 8 * g + 4 * k
                v.tensor_tensor(segR[:, q % 2, :].rearrange("p (h l) -> p h l", l=P), tri.unsqueeze(1).to_broadcast([P, 4, P]),
                                adt[:, t, h0:h0 + 4].unsqueeze(2).to_broadcast([P, 4, P]), ALU.mult).then_inc(sem("segR_ready"), 1)

            for t in range(TT):
                wait_full(dve, ("CB", t))
                release(v.tensor_tensor(cbm[:, t, :].rearrange("p (g l) -> p g l", l=P), pj(("CB", t))[:, :].rearrange("p (g l) -> p g l", l=P),
                                        tri.unsqueeze(1).to_broadcast([P, 4, P]), ALU.mult), ("CB", t))
            dve.wait_ge(sem("dte_ready"), 1)
            do(v.tensor_tensor(weight, dts[:, 0, 0:32], dts[:, 6, 0:32], ALU.mult))
            sync()
            wait_full(dve, ("xt", 7))
            seg_operand(0)
            seg_operand(1)
            zs = [0]

            def z_silu(k):
                for t in range(TT):
                    zs[0] += 1
                    dve.wait_ge(sem("tanh_z"), zs[0])
                    d = zt[:, t, 512 * k:512 * k + 512]
                    release(v.scalar_tensor_tensor(d, d, 1.0, pj((f"z{k}", t))[:, :], ALU.add, ALU.mult), (f"z{k}", t))

            z_silu(0)

            def y_norm(i):
                g, t = i // 2, i % 2
                dve.wait_ge(sem("squares_y"), i + 1)
                rstd("y", 1, 512, i)
                d = zt[:, t, 512 * g:512 * g + 512]
                v.tensor_scalar(d, d, col(STAT["y"] + RSTD + i), None, ALU.mult).then_inc(sem("y_ready"), 1)

            for i in range(8):
                g, t = i // 2, i % 2
                xg = xtok[:, t, 512 * g:512 * g + 512].rearrange("p (h d) -> p h d", d=64)
                if t == 0:
                    wait_done(dve, ("xt", g))
                    if g:
                        wait_full(dve, ("state", g - 1))
                    v.tensor_tensor(xd[:, :].rearrange("p (h d) -> p h d", d=64), xg, weight[:, 8 * g:8 * g + 8].unsqueeze(2).to_broadcast([P, 8, 64]),
                                    ALU.mult).then_inc(sem("xd_ready"), 1)
                if i:
                    wait_full(dve, ("Y", i - 1))
                for q in (2 * i, 2 * i + 1):
                    wait_done(dve, ("seg", q))
                    for k in range(4):
                        h = 8 * g + 4 * (q % 2) + k
                        ins = v.scalar_tensor_tensor(segM[:, q % 2, P * k:P * k + P], segE[:, q % 2, P * k:P * k + P],
                                                     dts[:, 0, 32 * t + h:32 * t + h + 1], cbm[:, t, P * g:P * g + P], ALU.mult, ALU.mult)
                    ins.then_inc(sem("segM_ready"), 1)
                if i < 7:
                    seg_operand(2 * i + 2)
                    seg_operand(2 * i + 3)
                if i >= 1:
                    y_norm(i - 1)
                wait_done(dve, ("xt", 4 * t + g))
                y3 = yt[:, 0, :].rearrange("p (h d) -> p h d", d=64)
                do(v.tensor_tensor(y3, xg, D("d_skip")[:, 8 * g:8 * g + 8].unsqueeze(2).to_broadcast([P, 8, 64]), ALU.mult))
                sync()
                wait_full(dve, ("Y", i))
                release(v.tensor_tensor(yt[:, 0, :], yt[:, 0, :], pj(("Y", i))[:, :], ALU.add), ("Y", i))
                wait_done(dve, ("Y", i))
                if t == 1:
                    wait_full(dve, ("off", g))
                    release(v.tensor_tensor(xd[:, :].rearrange("p (h d) -> p h d", d=64), pj(("off", g))[:, :].rearrange("p (h d) -> p h d", d=64),
                                            eac[:, 8 * g:8 * g + 8].unsqueeze(2).to_broadcast([P, 8, 64]), ALU.mult), ("off", g))
                    wait_done(dve, ("off", g))
                    do(v.tensor_tensor(yt[:, 0, :], yt[:, 0, :], xd[:, :], ALU.add))
                    sync()
                d = zt[:, t, 512 * g:512 * g + 512]
                v.scalar_tensor_tensor(d, yt[:, 0, :], 0.5, d, ALU.mult, ALU.mult).then_inc(sem("y_gated"), 1)
                if i in (0, 2, 4):
                    z_silu(i // 2 + 1)
            y_norm(7)
            lo_parts("y", 16, 0, D("g_ssd"))
            for i in range(2):
                if i:
                    dve.wait_ge(sem("m2_parts"), 2)
                for j in range(2):
                    job = (f"ys{i}", j)
                    wait_full(dve, job)
                    wait_done(dve, (f"gs{i}", j))
                    c = 4 * i + 2 * j
                    b3 = yt[:, j, :].rearrange("p (c s) -> p c s", s=S)
                    release(v.scalar_tensor_tensor(b3, gsT[:, c:c + 2, :], 1.0, pj(job)[:, :].rearrange("p (c s) -> p c s", s=S), ALU.add, ALU.mult), job)
                    wait_done(dve, job)
                    do(v.tensor_tensor(b3, b3, ymT[:, c:c + 2, :], ALU.add))
                sync()
                halves(v, do, sync, yt, m2hi, m2lo, 4 * i, "m2_parts")
                if i == 0:
                    norm("mem", memt, xn, "memn_ready")
            lo_parts("mem", 8, 8, D("g_mem"))

            def residual(name):
                for i in range(2):
                    for t in range(TT):
                        job = (f"{name}{i}", t)
                        wait_full(dve, job)
                        d = x[:, t, 512 * i:512 * i + 512]
                        release(v.tensor_tensor(d, pj(job)[:, :], d, ALU.add), job)
                wait_done(dve, (f"{name}1", 1))

            residual("wp")
            norm("h", x, xn, "hn_ready")
            for i in range(2):
                for t in range(TT):
                    copy((f"xv{i}", t), vx[:, t, 512 * i:512 * i + 512])
            lo_parts("h", 8, 0, D("g_xa"))
            for h in range(4):
                maxima(("xS", h), S, h)
                wait_done(dve, ("xS", h))
                k = 2 * h
                do(v.reciprocal(col(RSUM + k, 2), col(SUMS + k, 2)))
                sync()
                for t in range(TT):
                    d = px[:, h % 2, S * t:S * t + S]
                    v.tensor_scalar(d, d, col(RSUM + k + t), None, ALU.mult).then_inc(sem("px_ready"), 1)
                hi_seen[0] += 1
                dve.wait_ge(sem("xhi_ready"), hi_seen[0])
                release(v.tensor_tensor(xlo[:, 8 + 2 * h:10 + 2 * h, :], pj(("xO", h))[:, :].rearrange("p (c s) -> p c s", s=S),
                                        xhi[:, 8 + 2 * h:10 + 2 * h, :].bitcast(f32), ALU.subtract), ("xO", h))
            residual("xo")
            norm("m", x, xn, "mn_ready")
            lo_parts("m", 8, 0, D("g_moe"))

            R3 = lambda k, w, o=0: rtl[:, k, :].rearrange("p (t w) -> p t w", t=TT)[:, :, o:o + w]
            for t in range(TT):
                wait_full(dve, ("rt", t))
                release(v.tensor_tensor(R3(0, 36)[:, t, :], pj(("rt", t))[:, 0:36], D("b_rt"), ALU.add), ("rt", t))
            for t in range(TT):
                wait_done(dve, ("rt", t))

            def first_of(src, w, mx, out):
                do(v.tensor_reduce(col(mx, 2), src, AX.X, ALU.max))
                sync()
                do(v.tensor_tensor(out, src, col(mx, 2).unsqueeze(2).to_broadcast([P, TT, w]), ALU.is_equal))
                sync()
                do(v.tensor_scalar(out, out, -1000.0, 1000.0, ALU.mult, ALU.add))
                sync()
                it = C("iota")[:, 0:w].unsqueeze(1).to_broadcast([P, TT, w])
                do(v.tensor_tensor(out, out, it, ALU.add))
                sync()
                do(v.tensor_reduce(col(mx + 2, 2), out, AX.X, ALU.min))
                sync()
                do(v.tensor_tensor(out, it, col(mx + 2, 2).unsqueeze(2).to_broadcast([P, TT, w]), ALU.is_equal))
                sync()

            G0, E1, E2 = NMAX, NMAX + 4, NMAX + 8
            WG, W1, W2 = NMAX + 12, SUMS, SUMS + 2
            first_of(R3(0, 4), 4, G0, R3(1, 4))
            v.tensor_tensor(rtl[:, 2, 0:8].rearrange("p (t w) -> p t w", t=TT), R3(0, 4), col(G0, 2).unsqueeze(2).to_broadcast([P, TT, 4]), ALU.subtract).then_inc(sem("router_arg"), 1)
            do(v.tensor_scalar(R3(1, 4), R3(1, 4), 1e30, -1e30, ALU.mult, ALU.add))
            sync()
            elog = R3(0, 32, 4).rearrange("p t (g e) -> p t g e", e=8)
            for t in range(TT):
                do(v.tensor_tensor(R3(4, 32)[:, t, :].rearrange("p (g e) -> p g e", e=8), elog[:, t, :, :],
                                   R3(1, 4)[:, t, :].unsqueeze(2).to_broadcast([P, 4, 8]), ALU.add))
            sync()
            first_of(R3(4, 32), 32, E1, R3(5, 32))
            for t in range(TT):
                do(v.scalar_tensor_tensor(R3(4, 32)[:, t, :], R3(5, 32)[:, t, :], -1e30, R3(4, 32)[:, t, :], ALU.mult, ALU.add))
            sync()
            first_of(R3(4, 32), 32, E2, R3(6, 32))
            v.tensor_tensor(rtl[:, 2, 8:10], col(E2, 2), col(E1, 2), ALU.subtract).then_inc(sem("router_arg"), 1)
            dve.wait_ge(sem("router_exp"), 2)
            do(v.tensor_reduce(col(WG, 2), rtl[:, 2, 0:8].rearrange("p (t w) -> p t w", t=TT), AX.X, ALU.add))
            do(v.tensor_scalar(col(W1, 2), rtl[:, 2, 8:10], 1.0, None, ALU.add))
            sync()
            do(v.tensor_tensor(col(W1, 2), col(W1, 2), col(WG, 2), ALU.mult))
            sync()
            do(v.reciprocal(col(W1, 2), col(W1, 2)))
            sync()
            do(v.tensor_tensor(col(W2, 2), col(W1, 2), rtl[:, 2, 8:10], ALU.mult))
            sync()
            for t in range(TT):
                do(v.tensor_scalar(R3(5, 32)[:, t, :], R3(5, 32)[:, t, :], col(W1 + t), None, ALU.mult))
            sync()
            for t in range(TT):
                v.scalar_tensor_tensor(R3(7, 32)[:, t, :], R3(6, 32)[:, t, :], col(W2 + t), R3(5, 32)[:, t, :], ALU.mult, ALU.add).then_inc(sem("comb_ready"), 1)
            wait_full(dve, ("cb", 0))
            release(v.tensor_copy(combt[:, :], pj(("cb", 0))[0:NEXP, 0:S]), ("cb", 0))
            dve.wait_ge(sem("comb_loaded"), 16)

            def expert_dve(e, i, first=False):
                s = e % 2
                up = NB + 1 if e == 0 else GATE_UNIT(e) + 1
                dve.wait_ge(sem("silu_ready"), i * 2 + (e + 1))
                dve.wait_ge(weights_used, i * 6 + (up + 1))
                v.tensor_tensor(ga[:, s, :], sg[:, s, :], ps[2 * s + 1][:, :], ALU.mult).then_inc(sem("gated"), 1)
                dve.wait_ge(sem("gated"), i * 2 + (e + 1))
                row = comb[:, e:e + 1, :] if isinstance(i, int) else comb[:, bass.ds(i * 2 + e, 1), :]
                g3 = ga[:, s, :].rearrange("p (f s) -> p f s", s=S)
                v.tensor_tensor(g3, g3, row.to_broadcast([P, 2, S]), ALU.mult).then_inc(sem("weighted"), 1)
                dve.wait_ge(sem("weighted"), i * 2 + (e + 1))
                v.tensor_copy(ahi[:, s, :], ga[:, s, :]).then_inc(sem("act_hi"), 1)
                dve.wait_ge(sem("act_hi"), i * 2 + (e + 1))
                v.tensor_tensor(alo[:, s, :], ga[:, s, :], ahi[:, s, :].bitcast(f32), ALU.subtract).then_inc(sem("act_ready"), 1)

            expert_dve(0, 0)
            expert_dve(1, 0)
            expert_dve(2, 0)
            with dve.Fori(0, (NEXP - 4) // 2) as i:
                expert_dve(3, i)
                expert_dve(4, i)
            expert_dve(NEXP - 1, 0)
            dve.wait_ge(weights_used, NU)
            for t in range(TT):
                for i in range(2):
                    d = x[:, t, 512 * i:512 * i + 512]
                    do(v.tensor_tensor(d, ps[4 + 2 * t + i][:, :], d, ALU.add))
                sync()
                v.tensor_copy(stat[:, MISC + 4 + t:MISC + 5 + t], x[:, t, 0:1]).then_inc(sem("h3_ready"), 1)
            dve.wait_ge(sem("nfin_loaded"), 16)
            for t in range(TT):
                dve.wait_ge(sem("squares_f"), t + 1)
                rstd("f", 1, DM, t)
                v.scalar_tensor_tensor(xn[:, t, :], x[:, t, :], col(STAT["f"] + RSTD + t), nfin[:, :], ALU.mult, ALU.mult).then_inc(sem("out_ready"), 1)

        @block.tensor
        def _(pe):
            mm = nc.tensor.matmul

            def begin(job):
                b, k = JOBS[job][:2]
                if k:
                    pe.wait_ge(bank_done[b], k)

            def end(ins, job):
                assert JOBS[job][3] is None
                ins.then_inc(bank_full[JOBS[job][0]], 1)

            def mm3(out, lh, ll, rh, rl, first, last, skip=False):
                mm(out, lh, rh, start=first, stop=False, skip_group_check=skip)
                mm(out, lh, rl, start=False, stop=False, skip_group_check=skip)
                return mm(out, ll, rh, start=False, stop=last, skip_group_check=skip)

            def parts(n, nk, nc_):
                pe.wait_ge(lo_ready, n + 1)
                s = n % NSPL
                return (whi[:, s, 0:nk * nc_].rearrange("p (k c) -> p k c", k=nk),
                        wlo[:, s, 0:nk * nc_].rearrange("p (k c) -> p k c", k=nk))

            def gemm_unit_tm(name, part, hi, lo, k0=0, kt=8):
                n = UNIT[name][part]
                nk, nc_ = units[n][4], len(units[n][5])
                wh, wl = parts(n, nk, nc_)
                r0 = sum(units[m][4] for m in UNIT[name][:part])
                for t in range(TT):
                    job = (name, t)
                    if part == 0:
                        begin(job)
                    for k in range(nk):
                        tok = slice(t * P, t * P + P)
                        ins = mm3(pj(job)[:, 0:nc_], hi[:, k0 + r0 + k, tok], lo[:, k0 + r0 + k, tok], wh[:, k, :], wl[:, k, :],
                                  r0 + k == 0, r0 + k == kt - 1)
                    if t == 0 and r0 + nk == kt:
                        end(ins, job)
                ins.then_inc(weights_used, 1)

            def gemm_unit_fm(name, part, hi, lo, k0=0, kt=8):
                n = UNIT[name][part]
                nk, nc_ = units[n][4], len(units[n][5])
                wh, wl = parts(n, nk, nc_)
                r0 = sum(units[m][4] for m in UNIT[name][:part])
                for c in range(nc_ // P):
                    job = (name, c // 2)
                    if part == 0 and c % 2 == 0:
                        begin(job)
                    for k in range(nk):
                        cc = slice(c * P, c * P + P)
                        o_ = pj(job)[:, c % 2 * S:c % 2 * S + S]
                        first, last = r0 + k == 0 and c % 2 == 0, r0 + k == kt - 1
                        mm(o_, wh[:, k, cc], hi[:, k0 + r0 + k, :], start=first, stop=False, skip_group_check=True)
                        mm(o_, wl[:, k, cc], hi[:, k0 + r0 + k, :], start=False, stop=False, skip_group_check=True)
                        ins = mm(o_, wh[:, k, cc], lo[:, k0 + r0 + k, :], start=False, stop=last, skip_group_check=True)
                    if c % 2 and c < nc_ // P - 1 and r0 + nk == kt:
                        end(ins, job)
                ins.then_inc(weights_used, 1)

            def gemm(name, kind, hi, lo, k0=0, kt=8):
                for part in range(len(UNIT[name])):
                    kind(name, part, hi, lo, k0, kt)

            def transposes(name, nct, src, ready=None, count=0):
                if ready:
                    pe.wait_ge(sem(ready), count)
                for c in range(nct):
                    job = (name, c // 2)
                    if c % 2 == 0:
                        begin(job)
                    for t in range(TT):
                        ins = nc.tensor.transpose(pj(job)[:, c % 2 * S + t * P:c % 2 * S + t * P + P], src(t, c), ident)
                    if c % 2 or c == nct - 1:
                        end(ins, job)

            def tiles(m):
                return lambda t, c: m[:, t, c * P:c * P + P]

            def scores(job, q, k, mask=True):
                begin(job)
                b = pj(job)
                mm(b[:, 0:P], identb[:, :], negb[:, :], start=True, stop=False)
                mm(b[:, 0:P], q[:, 0:P], k[:, 0:P], start=False, stop=True)
                mm(b[:, P:S], q[:, P:S], k[:, 0:P], start=True, stop=True)
                mm(b[:, S:S + P], identb[:, :], negb[:, :], start=True, stop=False)
                end(mm(b[:, S:S + P], q[:, P:S], k[:, P:S], start=False, stop=True), job)

            def weights_transposed(job, p, n, sjob=None):
                begin(job)
                if sjob:
                    wait_done(pe, sjob)
                for i in range(n):
                    ins = nc.tensor.transpose(pj(job)[:, i * P:i * P + P], p[:, i * P:i * P + P], ident)
                end(ins, job)

            def outputs(job, tjob, pt, val, h):
                wait_done(pe, tjob)
                if h == 0:
                    begin(job)
                b = pj(job)[:, h * P:h * P + P]
                mm(b[:, 0:64], pt[:, 0:P], val(0), start=True, stop=True)
                mm(b[:, 64:P], pt[:, P:S], val(0), start=True, stop=False)
                ins = mm(b[:, 64:P], pt[:, S:S + P], val(1), start=False, stop=True)
                if h == 3:
                    end(ins, job)

            tm, fm = gemm_unit_tm, gemm_unit_fm
            pe.wait_ge(sem("cst_loaded"), 16)
            transposes("x", 8, tiles(xn), "xn_ready", 2)
            for j in range(4):
                wait_done(pe, ("x", j))
            for n in ("qn", "kv1", "kv2", "qr", "kr", "vr0", "vr1"):
                gemm(n, tm, xhi, xlo)
            pe.wait_ge(sem("nq_rotated"), 1)
            begin(("kT", 0))
            for k, c in enumerate((640, 768)):
                for t in range(TT):
                    ins = nc.tensor.transpose(pj(("kT", 0))[:, k * S + t * P:k * S + t * P + P], nq[:, t, c:c + P], ident)
            end(ins, ("kT", 0))
            transposes("qT", 4, tiles(nq))
            begin(("cT", 0))
            for k, c in enumerate((512, 896)):
                for t in range(TT):
                    ins = nc.tensor.transpose(pj(("cT", 0))[:, k * S + t * P:k * S + t * P + P], nq[:, t, c:c + P], ident)
            end(ins, ("cT", 0))
            pe.wait_ge(sem("xclo_ready"), 1)
            begin(("hid", 0))
            for kv, name in enumerate(("w1k", "w1v")):
                for part in range(2):
                    wh, wl = parts(UNIT[name][part], 8, S)
                    for half in range(2):
                        c = (2 * kv + half) * 32
                        b = pj(("hid", 0))[:, c:c + 30]
                        for k in range(8):
                            l = 8 * part + k
                            lw = slice(half * P, half * P + P)
                            ins = mm3(b, wh[:, k, lw], wl[:, k, lw], xchi[:, kv, l, :], xclo[:, kv, l, :],
                                      kv == part == half == k == 0, l == 15, skip=True)
                    ins.then_inc(weights_used, 1)
            gemm("zn", fm, xhi, xlo)
            pe.wait_ge(sem("gelu_ready"), 1)
            begin(("kvc", 0))
            hv = hg[:, 3, :].rearrange("p (a c) -> p a c", c=30)
            w2k, w2v = D("w2k").rearrange("p (a c) -> p a c", a=2), D("w2v").rearrange("p (a c) -> p a c", a=2)
            for half in range(2):
                mm(pj(("kvc", 0))[:, 0:30], w2k[:, half, :], hv[:, half, :], start=half == 0, stop=half == 1)
            for g in range(2):
                for half in range(2):
                    ins = mm(pj(("kvc", 0))[0:15, 64 + 64 * g:128 + 64 * g], hv[:, 2 + half, 15 * g:15 * g + 15], w2v[:, half, :],
                             start=half == 0, stop=half == 1)
            end(ins, ("kvc", 0))
            for job in (("kvc", 0), ("qT", 1), ("kT", 0)):
                wait_done(pe, job)
            pe.wait_ge(sem("masks_ready"), 2)
            begin(("Sc", 0))
            for odd in range(2):
                for h in range(odd, 8, 2):
                    for t in range(TT):
                        r, g = 64 * odd, h // 4
                        ins = mm(pj(("Sc", 0))[:, (8 * t + h) * 32:(8 * t + h) * 32 + 15], qT[r:r + 64, h // 2, t * P:t * P + P],
                                 kcT[r:r + 64, 15 * g:15 * g + 15], start=True, stop=True)
                if not odd:
                    ins.then_inc(sem("even_scores"), 1)
                    pe.wait_ge(sem("even_scores"), 1)
            end(ins, ("Sc", 0))

            def head(u):
                r, g = 64 * (u % 2), u % 8 // 4
                return qT[r:r + 64, u % 8 // 2, :], kT[r:r + 64, g, u // 8 * S:u // 8 * S + S]

            def value(u):
                c = (1024, 1152)[u // 8] + 64 * (u % 8 // 4)
                return lambda t: nq[:, t, c:c + 64]

            pe.wait_ge(sem("cmp_exp"), 1)
            weights_transposed(("Tc", 0), pr[:, 0, :], 4)
            scores(("S", 0), *head(0))
            wait_done(pe, ("Tc", 0))
            for t in range(TT):
                begin(("Oc", t))
                for g in range(2):
                    ins = mm(pj(("Oc", t))[:, g * S:g * S + S], pT[:, 0, (2 * t + g) * P:(2 * t + g) * P + P],
                             vcb[:, g, :, :].rearrange("p h d -> p (h d)"), start=True, stop=True)
                end(ins, ("Oc", t))
            fill = {0: ("zr0", 0), 2: ("zr0", 1), 4: ("zr1", 0), 6: ("zr1", 1), 7: ("ma0", 0), 9: ("ma0", 1), 11: ("ma1", 0), 13: ("ma1", 1)}
            for u in range(16):
                if u < 15:
                    scores(("S", u + 1), *head(u + 1))
                if u in fill:
                    fm(*fill[u], xhi, xlo)
                weights_transposed(("T", u), pr[:, u % 2, :], 3, ("S", u))
                if u:
                    outputs(("O", (u - 1) // 4), ("T", u - 1), pT[:, (u - 1) % 2, :], value(u - 1), (u - 1) % 4)
            outputs(("O", 3), ("T", 15), pT[:, 1, :], value(15), 3)
            pe.wait_ge(sem("qk_rotated"), 2)

            def ret_transposed(h):
                begin(("QK", h))
                for k in range(2):
                    for t in range(TT):
                        ins = nc.tensor.transpose(pj(("QK", h))[:, k * S + t * P:k * S + t * P + P], qk[:, t, 512 * k + P * h:512 * k + P * h + P], ident)
                end(ins, ("QK", h))

            ret_transposed(0)
            transposes("on", 4, tiles(oacc), "oacc_added", 8)
            for h in range(4):
                fm(f"mb{h // 2}", h % 2, xhi, xlo)
                wait_done(pe, ("QK", h))
                begin(("A", h))
                b = pj(("A", h))
                mm(b[:, 0:S], qkT[:, h % 2, S:S + P], qkT[:, h % 2, 0:S], start=True, stop=True)
                end(mm(b[:, S:S + P], qkT[:, h % 2, S + P:2 * S], qkT[:, h % 2, P:S], start=True, stop=True), ("A", h))
                if h < 3:
                    ret_transposed(h + 1)
                wait_done(pe, ("A", h))
                begin(("R", h))
                b, at_ = pj(("R", h)), pT[:, h % 2, :]
                v0, v1 = vr[:, 0, h * S:h * S + S], vr[:, 1, h * S:h * S + S]
                mm(b[:, 0:S], at_[:, 0:P], v0, start=True, stop=True)
                mm(b[:, S:2 * S], at_[:, P:S], v0, start=True, stop=False)
                end(mm(b[:, S:2 * S], at_[:, S:S + P], v1, start=False, stop=True), ("R", h))
            wait_done(pe, ("R", 3))
            transposes("or", 8, tiles(xn))
            for i in range(2):
                if i == 0:
                    pe.wait_ge(sem("on_parts"), 2)
                gemm(f"ya{i}", fm, xhi, xlo, 8, 4)
                if i == 0:
                    pe.wait_ge(sem("or_parts"), 4)
                gemm(f"yb{i}", fm, xhi, xlo)
            pe.wait_ge(sem("mT_parts"), 4)
            for i in range(2):
                gemm(f"wo{i}", tm, mThi, mTlo)
            transposes("u", 8, tiles(xn), "un_ready", 2)
            for j in range(4):
                wait_done(pe, ("u", j))
            gemm("pa", tm, xhi, xlo)
            gemm("pb", tm, xhi, xlo)
            pe.wait_ge(sem("codes_ready"), 4)
            transposes("qa", 3, lambda t, c: pa[:, t, 32 + c * P:32 + c * P + P])
            transposes("ck", 2, tiles(pb))
            pe.wait_ge(sem("kp_rotated"), 1)
            begin(("kp", 0))
            for t in range(TT):
                ins = nc.tensor.transpose(pj(("kp", 0))[0:32, t * P:t * P + P], pb[:, t, 256:288], ident)
            end(ins, ("kp", 0))
            wait_done(pe, ("qa", 0))
            wait_done(pe, ("qa", 1))
            for i in range(3):
                gemm(f"wq{i}", tm, xhi, xlo, 8, 3)
            wait_done(pe, ("ck", 0))
            n = UNIT["kn"][0]
            wh, wl = parts(n, 2, 1024)
            for c in range(8):
                job = ("kn", c // 2)
                if c % 2 == 0:
                    begin(job)
                for k in range(2):
                    o_ = pj(job)[:, c % 2 * S:c % 2 * S + S]
                    cc = slice(c * P, c * P + P)
                    mm(o_, wh[:, k, cc], xhi[:, 11 + k, :], start=k == 0, stop=False)
                    mm(o_, wl[:, k, cc], xhi[:, 11 + k, :], start=False, stop=False)
                    ins = mm(o_, wh[:, k, cc], xlo[:, 11 + k, :], start=False, stop=k == 1)
                if c % 2 and c < 7:
                    end(ins, job)
            ins.then_inc(weights_used, 1)
            wh, wl = parts(UNIT["vv"][0], 2, 1024)
            for j in range(4):
                job, t, i = ("vv", j), j // 2, j % 2
                begin(job)
                for k in range(2):
                    tok, cc = slice(t * P, t * P + P), slice(512 * i, 512 * i + 512)
                    ins = mm3(pj(job)[:, :], xhi[:, 11 + k, tok], xlo[:, 11 + k, tok], wh[:, k, cc], wl[:, k, cc], k == 0, k == 1)
                if j < 3:
                    end(ins, job)
            ins.then_inc(weights_used, 1)
            pe.wait_ge(sem("qm_rotated"), 2)

            def latent_queries(p):
                begin(("mQ", p))
                for c in range(2):
                    for t in range(TT):
                        h = 2 * p + c
                        ins = nc.tensor.transpose(pj(("mQ", p))[0:96, c * S + t * P:c * S + t * P + P], qm[:, t, 96 * h:96 * h + 96], ident)
                end(ins, ("mQ", p))

            def latent_head(u):
                wait_done(pe, ("mQ", u // 2))
                return qmT[0:96, u // 2 % 2, u % 2 * S:u % 2 * S + S], km[0:96, u, :]

            latent_queries(0)
            wait_done(pe, ("kp", 0))
            wait_done(pe, ("kn", 3))
            scores(("mS", 0), *latent_head(0))
            for u in range(16):
                if u % 2 == 0 and u < 14:
                    latent_queries(u // 2 + 1)
                if u < 15:
                    scores(("mS", u + 1), *latent_head(u + 1))
                if u < 12:
                    fm(f"xbc{u // 2}", u % 2, xhi, xlo)
                weights_transposed(("mT", u), pr2[:, u % 2, :], 3, ("mS", u))
                if u:
                    h = u - 1
                    if h == 0:
                        wait_done(pe, ("vv", 3))
                    outputs(("mO", h // 4), ("mT", h), pT2[:, h % 2, :], lambda t: vm[:, t, 64 * h:64 * h + 64], h % 4)
            outputs(("mO", 3), ("mT", 15), pT2[:, 1, :], lambda t: vm[:, t, 64 * 15:64 * 16], 3)
            wait_done(pe, ("mO", 3))

            def om_tile(t, c):
                return qm[:, t, 192 * c:192 * c + P]

            transposes("om", 8, om_tile)
            for i in range(2):
                gemm(f"gm{i}", fm, xhi, xlo)
            for j in range(4):
                wait_done(pe, ("om", j))
            for i in range(2):
                gemm(f"ym{i}", fm, xhi, xlo, 8)
            pe.wait_ge(sem("adt_ready"), 1)
            pe.wait_ge(sem("silu_done"), 12)
            begin(("acum", 0))
            b = pj(("acum", 0))
            mm(b[:, 0:32], tri, dts[:, 1, 0:32], start=True, stop=True)
            mm(b[:, 32:64], tri, dts[:, 1, 32:64], start=True, stop=True)
            end(mm(b[:, 64:96], ones, dts[:, 1, 0:32], start=True, stop=True), ("acum", 0))
            begin(("Bt", 0))
            for g in range(4):
                ins = nc.tensor.transpose(pj(("Bt", 0))[:, g * P:g * P + P], xbc[:, 16 + g, 0:P], ident)
            end(ins, ("Bt", 0))
            for t in range(TT):
                begin(("CB", t))
                for g in range(4):
                    ins = mm(pj(("CB", t))[:, g * P:g * P + P], xbc[:, 16 + g, t * P:t * P + P], xbc[:, 20 + g, t * P:t * P + P], start=True, stop=True)
                end(ins, ("CB", t))
            for i in range(8):
                begin(("xt", i))
                for k in range(4):
                    ins = nc.tensor.transpose(pj(("xt", i))[:, k * P:k * P + P], xbc[:, 4 * (i % 4) + k, i // 4 * P:i // 4 * P + P], ident)
                end(ins, ("xt", i))

            def scan_unit(n):
                gemm(n, tm if n[0] == "z" else fm, xhi, xlo)

            scan_unit("z0")
            for i in range(8):
                g, t = i // 2, i % 2
                for q in (2 * i, 2 * i + 1):
                    begin(("seg", q))
                    pe.wait_ge(sem("segR_ready"), q + 1)
                    end(mm(pj(("seg", q))[:, :], stri, segR[:, q % 2, :], start=True, stop=True), ("seg", q))
                if t == 0:
                    begin(("state", g))
                    pe.wait_ge(sem("xd_ready"), g + 1)
                    end(mm(pj(("state", g))[:, :], btok[:, g * P:g * P + P], xd[:, :], start=True, stop=True), ("state", g))
                else:
                    begin(("off", g))
                    wait_done(pe, ("state", g))
                    end(mm(pj(("off", g))[:, :], xbc[:, 20 + g, P:S], st[:, :], start=True, stop=True), ("off", g))
                if i < 5:
                    scan_unit(SCAN_UNITS[i + 1])
                begin(("Y", i))
                pe.wait_ge(sem("segM_ready"), 2 * i + 2)
                for k in range(8):
                    c = 512 * g + 64 * k
                    ins = mm(pj(("Y", i))[:, 64 * k:64 * k + 64], segM[:, k // 4, k % 4 * P:k % 4 * P + P], xtok[:, t, c:c + 64], start=True, stop=True)
                end(ins, ("Y", i))
            transposes("y", 16, tiles(zt), "y_ready", 8)
            for j in range(8):
                wait_done(pe, ("y", j))
            for i in range(2):
                gemm(f"ys{i}", fm, xhi, xlo, 0, 16)
            transposes("mem", 8, tiles(xn), "memn_ready", 2)
            pe.wait_ge(sem("m2_parts"), 4)
            for i in range(2):
                gemm(f"wp{i}", tm, m2hi, m2lo)
            for j in range(4):
                wait_done(pe, ("mem", j))
            for i in range(2):
                gemm(f"xk{i}", fm, xhi, xlo, 8)
            for i in range(2):
                gemm(f"xv{i}", tm, xhi, xlo, 8)
            transposes("h", 8, tiles(xn), "hn_ready", 2)
            for j in range(4):
                wait_done(pe, ("h", j))
            for i in range(2):
                gemm(f"xq{i}", fm, xhi, xlo)
            for i in range(2):
                wait_done(pe, ("xq1", i))
                wait_done(pe, ("xk1", i))
                wait_done(pe, ("xv1", i))
            for h in range(4):
                begin(("xS", h))
                for t in range(TT):
                    for d in range(2):
                        ins = mm(pj(("xS", h))[:, t * S:t * S + S], qx[:, 2 * h + d, t * P:t * P + P], kx[:, 2 * h + d, :], start=d == 0, stop=d == 1)
                end(ins, ("xS", h))
                begin(("xT", h))
                pe.wait_ge(sem("px_ready"), 2 * h + 2)
                for k in range(2):
                    for t in range(TT):
                        ins = nc.tensor.transpose(pj(("xT", h))[:, k * S + t * P:k * S + t * P + P], px[:, h % 2, t * S + k * P:t * S + k * P + P], ident)
                end(ins, ("xT", h))
                wait_done(pe, ("xT", h))
                begin(("xO", h))
                for d in range(2):
                    for k in range(2):
                        ins = mm(pj(("xO", h))[:, d * S:d * S + S], vx[:, k, h * S + d * P:h * S + d * P + P], pxT[:, h % 2, k * S:k * S + S],
                                 start=k == 0, stop=k == 1)
                end(ins, ("xO", h))
            wait_done(pe, ("xO", 3))
            for i in range(2):
                gemm(f"xo{i}", tm, xhi, xlo, 8)
            transposes("m", 8, tiles(xn), "mn_ready", 2)
            for j in range(4):
                wait_done(pe, ("m", j))
            gemm("rt", tm, xhi, xlo)

            def expert_in(unit, b, i):
                pe.wait_ge(lo_ready, i * 6 + (unit + 1))
                wh = whi[:, unit % NSPL, :].rearrange("p (k c) -> p k c", k=8)
                wl = wlo[:, unit % NSPL, :].rearrange("p (k c) -> p k c", k=8)
                for f in range(2):
                    o_, cc = ps[b][:, f * S:f * S + S], slice(f * P, f * P + P)
                    for k in range(8):
                        mm(o_, wh[:, k, cc], xhi[:, k, :], start=k == 0, stop=False)
                        mm(o_, wl[:, k, cc], xhi[:, k, :], start=False, stop=False)
                        ins = mm(o_, wh[:, k, cc], xlo[:, k, :], start=False, stop=k == 7)
                ins.then_inc(weights_used, 1)

            def expert_down(e, unit, i):
                pe.wait_ge(lo_ready, i * 6 + (unit + 1))
                pe.wait_ge(sem("act_ready"), i * 2 + (e + 1))
                s = e % 2
                wh = whi[:, unit % NSPL, :].rearrange("p (k c) -> p k c", k=2)
                wl = wlo[:, unit % NSPL, :].rearrange("p (k c) -> p k c", k=2)
                for t in range(TT):
                    for half in range(2):
                        for k in range(2):
                            a_, cc = slice(k * S + t * P, k * S + t * P + P), slice(512 * half, 512 * half + 512)
                            ins = mm3(ps[4 + 2 * t + half][:, :], ahi[:, s, a_], alo[:, s, a_], wh[:, k, cc], wl[:, k, cc],
                                      e == 0 and k == 0, e == NEXP - 1 and k == 1, skip=True)
                ins.then_inc(weights_used, 1)

            for b in range(4):
                pe.wait_ge(bank_done[b], TOTAL[b])
            expert_in(NB, 0, 0)
            expert_in(NB + 1, 1, 0)
            begin(("cb", 0))
            pe.wait_ge(sem("comb_ready"), 2)
            for t in range(TT):
                ins = nc.tensor.transpose(pj(("cb", 0))[0:NEXP, t * P:t * P + P], rtl[:, 7, 36 * t:36 * t + 32], ident)
            end(ins, ("cb", 0))

            def expert_pe(e, i):
                n, s = GATE_UNIT(e), e % 2
                if e >= 2:
                    pe.wait_ge(sem("silu_ready"), i * 2 + (e - 1))
                expert_in(n, 2 * s, i)
                if e >= 2:
                    pe.wait_ge(sem("gated"), i * 2 + (e - 1))
                expert_in(n + 1, 2 * s + 1, i)
                if e == 1:
                    for b in range(4, 8):
                        pe.wait_ge(bank_done[b], TOTAL[b])
                expert_down(e - 1, n + 2, i)

            expert_pe(1, 0)
            expert_pe(2, 0)
            with pe.Fori(0, (NEXP - 4) // 2) as i:
                expert_pe(3, i)
                expert_pe(4, i)
            expert_pe(NEXP - 1, 0)
            expert_down(NEXP - 1, NU - 1, 0)


def constants():
    f = np.float32
    c = np.zeros((P, NCONST), f)
    p = np.arange(P)

    def put(name, a):
        o, w = CONST[name]
        c[:, o:o + w] = np.asarray(a, f).reshape(P, w)

    put("ident", np.eye(P))
    put("tri", p[:, None] <= p[None, :])
    put("stri", p[:, None] > p[None, :])
    put("ones", np.ones((P, P)))
    put("negmask", np.where(p[None, :] > p[:, None], -1e30, 0.0))
    tok = np.arange(TT)[None, :] * P + p[:, None]
    put("cmpmask", np.where(16 * np.arange(15) + 31 <= tok[:, :, None], 0.0, -1e30))
    nsa_inv = (f(1.0) / (f(500000.0) ** (np.arange(0, 16, 2, dtype=f) / f(16)))).astype(f)
    ang = tok.astype(f)[:, :, None] * nsa_inv
    put("cos", np.cos(ang.astype(np.float64)))
    put("sin", np.sin(ang.astype(np.float64)))
    ret_inv = (f(1.0) / (f(10000.0) ** np.linspace(0.0, 1.0, 64, dtype=f))).astype(f)
    ang = tok.astype(f)[:, :, None] * ret_inv
    put("rcos", np.cos(ang.astype(np.float64)))
    put("rsin", np.sin(ang.astype(np.float64)))
    put("invf", np.tile(f(10000.0) ** (-np.arange(16, dtype=f) / f(16)), (P, 1)))
    put("iota", np.tile(np.arange(32), (P, 1)))
    diff = np.arange(S)[None, :] - p[:, None]
    log_g = np.log(1.0 - 2.0 ** (-5.0 - np.arange(4)))
    dec = np.where(diff[:, None, :] >= 0, np.exp(np.maximum(diff, 0)[:, None, :] * log_g[None, :, None]), 0.0) * 128 ** -0.5
    return c, dec.astype(f)


def laid_out(inputs):
    a = {k: np.asarray(v) for k, v in inputs.items()}
    f = np.float32
    a["router"] = np.concatenate([a["w_router_group_2"][0], a["w_router_expert_2"][0]], axis=1)
    units = unit_plan()
    w = np.zeros((len(units), P, UW), f)
    flat = {}
    for n, (_, _, src, r0, nk, cols) in enumerate(units):
        if src not in flat:
            flat[src] = a[src].reshape(-1, a[src].shape[-1])
        m = flat[src][r0:r0 + nk * P]
        c0, c1 = int(cols[0]), int(cols[-1]) + 1
        m = m[:, c0:c1] if c1 - c0 == len(cols) else m[:, cols]
        w[n, :, :nk * len(cols)] = m.reshape(nk, P, len(cols)).transpose(1, 0, 2).reshape(P, -1)
    s = np.zeros((P, NSMALL), f)

    def put(name, v):
        o, width = SMALL[name]
        s[:, o:o + width] = np.broadcast_to(v, (P, width))

    for name, src in (("g_pre", "norm_pre"), ("g_mix", "norm_mix_2"), ("g_xa", "norm_xattn_2"), ("g_mem", "norm_mem_2"),
                      ("g_moe", "norm_moe_2"), ("g_ssd", "ssd_norm_2"), ("g_qa", "q_a_norm_2"), ("g_ckv", "kv_a_norm_2")):
        put(name, a[src].reshape(-1, P).T)
    put("conv_w", a["conv_w_2"][0].reshape(4 * 24, P).T)
    put("conv_b", a["conv_b_2"][0].reshape(24, P).T)
    put("pe_k", a["cmp_pe_k"].reshape(16, P).T)
    put("pe_v", a["cmp_pe_v"].reshape(16, P).T)
    put("b_gate", a["b_nsa_gate"][None])
    put("dt_b", a["dt_bias_2"])
    put("a_log", a["a_log_2"])
    put("d_skip", a["d_skip_2"])
    put("b_rt", np.concatenate([a["b_router_group_2"], a["b_router_expert_2"]], axis=1))
    w2 = a["cmp_w2_k"].reshape(2, P, 64).transpose(1, 0, 2)
    put("w2k", np.concatenate([w2, w2], axis=2).reshape(P, 256))
    put("w2v", a["cmp_w2_v"].reshape(2, P, 64).transpose(1, 0, 2).reshape(P, 128))
    tok = lambda m: np.ascontiguousarray(m.reshape(TT, P, -1).transpose(1, 0, 2))
    cst, dec = constants()
    return {
        "x": tok(a["x"]), "mem": tok(a["mem_2"]), "positions": np.ascontiguousarray(a["positions_2"].reshape(TT, P).T.astype(np.int32)),
        "constants": cst, "small": s, "decay": dec, "norm_post": np.ascontiguousarray(np.broadcast_to(a["norm_post"], (P, DM))),
        "norm_final": np.ascontiguousarray(np.broadcast_to(a["norm_final_2"], (P, DM))), "weights": w,
    }


def kernel(**inputs):
    import concourse.bacc as bacc
    from concourse.bass_utils import run_bass_kernel_spmd

    nc = bacc.Bacc("TRN2", target_bir_lowering=False, num_devices=1)
    arrays, args = {}, []
    for name, a in laid_out(inputs).items():
        arrays[f"in_{name}"] = a
        args.append(nc.dram_tensor(f"in_{name}", a.shape, mybir.dt.from_np(a.dtype), kind="ExternalInput").ap())
    out = nc.dram_tensor("out", (P, TT, DM), mybir.dt.float32, kind="ExternalOutput").ap()
    scratch = nc.dram_tensor("expert_weights", (NEXP, S), mybir.dt.float32, kind="Internal").ap()
    program(nc, *args, out, scratch)
    r = run_bass_kernel_spmd(nc, [arrays], core_ids=[0])
    got = r.results[0]["out"]
    return np.ascontiguousarray(got.transpose(1, 0, 2)).reshape(1, S, DM)
```

```python
import numpy as np
import concourse.bass as bass
from concourse import mybir
from contextlib import ExitStack

P, TT, S, DM = 128, 2, 256, 1024
UW = 2048
NRAW, NSPL = 3, 3
EPS = 1e-6
TWO_PI = 6.283185307179586
PI_PARTS = (6.28125, 1.93500518798828125e-3, 3.019916050561733e-7)
NEXP = 32
SCAN_UNITS = ("z0", "z1", "z2", "z3", "gs0", "gs1")
SCAN_FILL = ((("z1", 0), ("z1", 1)), (("z2", 0),), (("z2", 1), ("z3", 0)), (("z3", 1),), (("gs0", 0),), (("gs0", 1),), (("gs1", 0),), (("gs1", 1),))
CONST = {}
SMALL = {}
for _n, _w in (("ident", 128), ("tri", 128), ("stri", 128), ("ones", 128), ("cmpmask", 30), ("cos", 16), ("sin", 16),
               ("invf", 16), ("iota", 32), ("rcos", 128), ("rsin", 128), ("negmask", 128)):
    CONST[_n] = (sum(w for _, w in CONST.values()), _w)
for _n, _w in (("g_pre", 8), ("g_mix", 8), ("g_xa", 8), ("g_mem", 8), ("g_moe", 8), ("g_ssd", 16), ("g_qa", 3),
               ("g_ckv", 2), ("conv_w", 96), ("conv_b", 24), ("pe_k", 16), ("pe_v", 16), ("b_gate", 24),
               ("dt_b", 32), ("a_log", 32), ("d_skip", 32), ("b_rt", 36), ("w2k", 256), ("w2v", 128)):
    SMALL[_n] = (sum(w for _, w in SMALL.values()), _w)
NCONST = sum(w for _, w in CONST.values())
NSMALL = sum(w for _, w in SMALL.values())


def unit_plan():
    plan = []

    def add(name, src, rows, cols, nk=4):
        for i, k0 in enumerate(range(0, rows // P, nk)):
            plan.append((name, i, src, k0 * P, min(nk, rows // P - k0), cols))

    def add_pair(name, src):
        for i in range(2):
            for half in range(2):
                plan.append((f"{name}{half}", i, src, 512 * i, 4, r(512 * half, 512 * half + 512)))

    r = np.arange
    w = "w_in"
    add("qn", w, 1024, r(0, 512))
    add("kv1", w, 1024, np.concatenate([r(512, 640), r(768, 896), r(1024, 1152), r(640, 768)]))
    add("kv2", w, 1024, np.concatenate([r(896, 1024), r(1152, 1280), r(1280, 1304)]))
    for i, n in enumerate(("qr", "kr", "vr0", "vr1")):
        add(n, w, 1024, r(1816 + 512 * i, 2328 + 512 * i))
    add("zn", w, 1024, r(1304, 1816))
    late = plan.pop()
    add("w1k", "cmp_w1_k", 2048, r(256), 8)
    add("w1v", "cmp_w1_v", 2048, r(256), 8)
    plan.append(late)
    for i, n in enumerate(("zr0", "zr1", "ma0", "ma1", "mb0", "mb1")):
        add(n, w, 1024, r(3864 + 512 * i, 4376 + 512 * i))
    for i in range(2):
        add(f"ya{i}", "w_nsa_o", 512, r(512 * i, 512 * i + 512))
    for i in range(2):
        add(f"yb{i}", "w_ret_o", 1024, r(512 * i, 512 * i + 512))
    add_pair("wo", "w_out")
    w = "w_in_2"
    add("pa", w, 1024, r(5120, 5536))
    add("pb", w, 1024, r(5536, 5824))
    add("xbc0", w, 1024, r(2048, 2560))
    for i in range(3):
        add(f"wq{i}", "w_q_b_2", 384, r(512 * i, 512 * i + 512))
    heads = r(2048).reshape(16, 128)
    add("kn", "w_kv_b_2", 256, heads[:, :64].ravel())
    add("vv", "w_kv_b_2", 256, heads[:, 64:].ravel())
    for i in range(1, 6):
        add(f"xbc{i}", w, 1024, r(2048 + 512 * i, 2560 + 512 * i))
    for i in range(2):
        add(f"gm{i}", w, 1024, r(6848 + 512 * i, 7360 + 512 * i))
    for i in range(2):
        add(f"ym{i}", "w_mla_out_2", 1024, r(512 * i, 512 * i + 512))
    for n in SCAN_UNITS:
        c = 512 * int(n[-1]) + (0 if n[0] == "z" else 5824)
        add(n, w, 1024, r(c, c + 512))
    for i in range(2):
        add(f"ys{i}", "w_ssd_out_2", 2048, r(512 * i, 512 * i + 512))
    add_pair("wp", "w_o_2")
    for i in range(2):
        add(f"xk{i}", "w_xkv_2", 1024, r(512 * i, 512 * i + 512))
    for i in range(2):
        add(f"xv{i}", "w_xkv_2", 1024, r(1024 + 512 * i, 1536 + 512 * i))
    for i in range(2):
        add(f"xq{i}", "w_xq_2", 1024, r(512 * i, 512 * i + 512))
    add_pair("xo", "w_xo_2")
    add("rt", "router", 1024, r(36), 8)

    def expert(kind, e):
        if kind == "down":
            plan.append((f"down{e}", 0, "w_exp_down_2", 256 * e, 2, r(1024)))
        else:
            plan.append((f"{kind}{e}", 0, f"w_exp_{kind}_2", 1024 * e, 8, r(256)))

    expert("gate", 0)
    expert("up", 0)
    for e in range(1, NEXP):
        expert("gate", e)
        expert("up", e)
        expert("down", e - 1)
    expert("down", NEXP - 1)
    return plan


def bank_plan(units):
    G, W, O, ends = [], [], [], {}

    def gemm(name, jobs=None):
        jobs = jobs or [(name, 0), (name, 1)]
        G.extend(jobs)
        ends[jobs[-1]] = max(i for i, u in enumerate(units) if u[0] == name)

    G += [("x", j) for j in range(4)]
    for n in ("qn", "kv1", "kv2"):
        gemm(n)
    for n in ("qr", "kr", "vr0", "vr1"):
        gemm(n)
    G += [("kT", 0), ("qT", 0), ("qT", 1), ("cT", 0)]
    gemm("zn")
    G += [("hs", 0), ("hid", 0)]
    ends[("hs", 0)] = max(i for i, u in enumerate(units) if u[0] == "w1v")
    gemm("zr0")
    G += [("kvc", 0)]
    for n in ("zr1", "ma0", "ma1"):
        gemm(n)
    gemm("mb0")
    G += [("on", 0), ("on", 1)]
    for n in ("mb1", "ya0"):
        gemm(n)
    G += [("or", j) for j in range(4)]
    for n in ("ya1", "yb0", "yb1", "wo0", "wo1"):
        gemm(n)
    G += [("u", j) for j in range(4)]
    gemm("pa")
    gemm("pb")
    G += [("qa", 0), ("qa", 1)]
    gemm("xbc0")
    for i in range(3):
        gemm(f"wq{i}")
    gemm("kn", [("kn", j) for j in range(4)])
    gemm("vv", [("vv", j) for j in range(4)])
    for n in ("xbc1", "xbc2", "xbc3", "xbc4", "xbc5", "gm0", "gm1"):
        gemm(n)
    G += [("om", j) for j in range(4)]
    for n in ("ym0", "ym1", "z0", "z1", "z2", "z3"):
        gemm(n)
    G += [("y", 0), ("y", 1)]
    gemm("gs0")
    G += [("y", 2), ("y", 3)]
    gemm("gs1")
    G += [("y", 4), ("y", 5)]
    gemm("ys0")
    G += [("y", 6), ("y", 7)]
    gemm("ys1")
    for n in ("wp0", "wp1", "xk0", "xk1", "xv0"):
        gemm(n)
    G += [("h", j) for j in range(4)]
    for n in ("xv1", "xq0", "xq1", "xo0", "xo1"):
        gemm(n)
    G += [("m", j) for j in range(4)]
    gemm("rt", [("rt", 0)])
    W += [("Sc", 0), ("Tc", 0)]
    W += [("S", 0)]
    for u in range(16):
        W += [("S", u + 1)] * (u < 15) + [("T", u)]
    O += [("Oc", 0), ("Oc", 1)] + [("O", q) for q in range(4)]
    for h in range(4):
        W += [("QK", h), ("A", h)]
        O += [("R", h)]
    W += [("ck", 0), ("kp", 0), ("mQ", 0), ("mS", 0)]
    for u in range(16):
        if u % 2 == 0 and u < 14:
            W += [("mQ", u // 2 + 1)]
        W += [("mS", u + 1)] * (u < 15) + [("mT", u)]
    O += [("mO", q) for q in range(4)]
    W += [("acum", 0), ("Bt", 0), ("CB", 0), ("CB", 1)]
    W += [("xt", i) for i in range(8)]
    for i in range(8):
        W += [("seg", 2 * i), ("seg", 2 * i + 1)]
        W += [("state" if i % 2 == 0 else "off", i // 2)]
        O += [("Y", i)]
    W += [("mem", j) for j in range(4)]
    W += [("xS", 0), ("xT", 0), ("xS", 1), ("xT", 1), ("xS", 2), ("xS", 3), ("xT", 2), ("xT", 3)]
    O += [("xO", h) for h in range(4)]
    W += [("rtt", 0), ("cb", 0)]
    jobs = {}
    counts = [0] * 8
    for pool, banks in ((G, (0, 1, 2, 3)), (W, (4, 5, 6)), (O, (7,))):
        for i, j in enumerate(pool):
            b = banks[i % len(banks)]
            full = None if j in ends else counts[b]
            counts[b] += j not in ends
            jobs[j] = (b, i // len(banks), full, ends.get(j), i)
    total = [sum(1 for j in jobs.values() if j[0] == b) for b in range(8)]
    return jobs, total


def program(nc, x_d, mem_d, pos_d, cst_d, sml_d, dec_d, npost_d, nfin_d, w_d, out_d, scratch):
    f32, f32r, bf16, i32 = mybir.dt.float32, mybir.dt.float32r, mybir.dt.bfloat16, mybir.dt.int32
    ACT, ALU, AX = mybir.ActivationFunctionType, mybir.AluOpType, mybir.AxisListType
    units = unit_plan()
    NU = len(units)
    UNIT = {}
    for i, u in enumerate(units):
        UNIT.setdefault(u[0], []).append(i)
    JOBS, TOTAL = bank_plan(units)
    NB = UNIT["gate0"][0]
    ctx = ExitStack()
    with ctx:
        base = 16512

        def at(name, off, shape, dt=f32):
            n = 4 if dt != bf16 else 2
            size = n * int(np.prod(shape[1:]))
            assert off + size <= 229344, (name, off + size)
            return nc.alloc_sbuf_tensor_at(name, shape, dt, offset=off)

        KB = 1024
        o = base
        raw = at("raw", o, [P, NRAW, UW]); o += NRAW * UW * 4
        whi = at("whi", o, [P, NSPL, UW], f32r); o += NSPL * UW * 4
        wlo = at("wlo", o, [P, NSPL, UW], f32r); o += NSPL * UW * 4
        xhi = at("xhi", o, [P, 16, S], f32r); o += 16 * KB
        xlo = at("xlo", o, [P, 16, S], f32r); o += 16 * KB
        x = at("x", o, [P, TT, DM]); o += 8 * KB
        cst = at("cst", o, [P, NCONST]); o += 4 * ((NCONST + 7) // 8 * 8)
        sml = at("sml", o, [P, NSMALL]); o += 4 * ((NSMALL + 7) // 8 * 8)
        identb = at("identb", o, [P, P], bf16); o += 256
        negb = at("negb", o, [P, P], bf16); o += 256
        stat = at("stat", o, [P, 256]); o += KB
        ropt = at("ropt", o, [P, 8, TT * 16]); o += KB
        posi = at("posi", o, [P, TT], i32); o += 32
        A = o

        def sub(tab, t, name):
            a, w = tab[name]
            return t[:, a:a + w]

        C = lambda n: sub(CONST, cst, n)
        D = lambda n: sub(SMALL, sml, n)
        ident, tri, stri, ones = C("ident"), C("tri"), C("stri"), C("ones")

        a = A
        xn = at("xn", a, [P, TT, DM])
        ropetmp = at("ropetmp", a, [P, 4, 512])
        a += 8 * KB
        nq = at("nq", a, [P, TT, 1304])
        mbT = at("mbT", a, [P, 8, S])
        a += 10432
        qk = at("qk", a, [P, TT, DM])
        mThi = at("mThi", a, [P, 8, S], f32r)
        a += 8 * KB
        vr = at("vr", a, [P, TT, DM])
        mTlo = at("mTlo", a, [P, 8, S], f32r)
        a += 8 * KB
        znT = at("znT", a, [P, 4, S])
        npost = at("npost", a, [P, DM])
        a += 4 * KB
        zrT = at("zrT", a, [P, 8, S])
        a += 8 * KB
        maT = at("maT", a, [P, 8, S])
        a += 8 * KB
        kT = at("kT", a, [P, 2, 512])
        a += 4 * KB
        qT = at("qT", a, [P, 4, S])
        decay = at("decay", a, [P, 4, S])
        a += 4 * KB
        oacc = at("oacc", a, [P, TT, 512])
        xcf = at("xcf", a, [P, 2, 16, 30])
        a += 4 * KB
        xchi = at("xchi", a, [P, 2, 16, 30], f32r)
        xclo = at("xclo", a + 3840, [P, 2, 16, 30], f32r)
        qkT = at("qkT", a, [P, 2, 512])
        a += 7680
        pr = at("pr", a, [P, 2, 512])
        hg = at("hg", a + 2 * KB, [P, 4, 120])
        a += 4 * KB
        pT = at("pT", a, [P, 2, 512])
        cs = at("cs", a + 2 * KB, [P, 16, 15])
        a += 4 * KB
        tmp = at("tmp", a, [P, 2, 512])
        vcb = at("vcb", a + 2 * KB, [P, 2, 4, 64])
        kcT = at("kcT", a + 1920, [P, 32])
        a += 4 * KB

        a = A
        pa = at("pa", a, [P, TT, 416])
        pb = at("pb", a + 3328, [P, TT, 288])
        gmT = at("gmT", a, [P, 8, S])
        a += 8 * KB
        qm = at("qm", a, [P, TT, 1536])
        a += 12 * KB
        vm = at("vm", a, [P, TT, DM])
        ymT = at("ymT", a, [P, 8, S])
        a += 8 * KB
        xbc = at("xbc", a, [P, 24, S])
        gsT = at("gsT", a, [P, 8, S])
        segR = at("segR", a + 8 * KB, [P, 2, 512])
        segE = at("segE", a + 12 * KB, [P, 2, 512])
        ropetmp2 = at("ropetmp2", a + 20 * KB, [P, 4, S])
        a += 24 * KB
        b0 = a
        km = at("km", a, [P, 16, S])
        a += 16 * KB
        qmT = at("qmT", a, [P, 2, 512])
        a += 4 * KB
        pr2 = at("pr2", a, [P, 2, 384])
        a += 3 * KB
        pT2 = at("pT2", a, [P, 2, 384])
        a += 3 * KB
        cv = at("cv", a, [P, 2, 2, S])
        a += 4 * KB
        dts = at("dts", a, [P, 8, 64])
        a += 2 * KB
        zt = at("zt", A, [P, TT, 2048])
        btok = at("btok", A + 16 * KB, [P, 512])
        st = at("st", A + 18 * KB, [P, 512])
        xtok = at("xtok", b0, [P, TT, 2048])
        segM = at("segM", b0 + 16 * KB, [P, 2, 512])
        cbm = at("cbm", b0 + 20 * KB, [P, 2, 512])
        xd = at("xd", b0 + 24 * KB, [P, 512])
        carried = at("carried", b0 + 32 * KB, [P, 512])
        yt = at("yt", b0 + 26 * KB, [P, 2, 512])
        m2hi = at("m2hi", b0, [P, 8, S], f32r)
        m2lo = at("m2lo", b0 + 8 * KB, [P, 8, S], f32r)
        memt = at("memt", A + 8 * KB, [P, TT, DM])
        kx = at("kx", A + 16 * KB, [P, 8, S])
        vx = at("vx", A + 24 * KB, [P, TT, DM])
        qx = at("qx", A + 32 * KB, [P, 8, S])
        px = at("px", A + 40 * KB, [P, 2, 512])
        pxT = at("pxT", A + 44 * KB, [P, 2, 512])
        comb = at("comb", A + 8 * KB, [P, NEXP, S])
        combt = at("combt", A + 40 * KB, [NEXP, S])
        rtl = at("rtl", A + 41 * KB, [P, 8, TT * 36])
        sg = at("sg", A + 44 * KB, [P, 2, 512])
        ga = at("ga", A + 48 * KB, [P, 2, 512])
        ahi = at("ahi", A + 52 * KB, [P, 2, 512], f32r)
        alo = at("alo", A + 56 * KB, [P, 2, 512], f32r)
        nfin = at("nfin", A + 60 * KB, [P, DM])

        STAT = {"x": 0, "post": 2, "u": 6, "qa": 8, "ck": 10, "y": 12, "mem": 20, "h": 22, "m": 24, "f": 26}
        RSTD, NMAX, SUMS, RSUM, GF, CMAX, CSUM, CGATE, GATE, MISC = 32, 64, 80, 96, 112, 128, 144, 160, 192, 240
        CW, CB_ = SMALL["conv_w"][0], SMALL["conv_b"][0]
        MAXN = {("S", u): u + 1 for u in range(16)} | {("mS", u): 17 + u for u in range(16)} | {("xS", h): 33 + h for h in range(4)}

        ps = [ctx.enter_context(nc.psum_tensor(f"ps{i}", [P, 512], f32)) for i in range(8)]
        sems = {}

        def sem(name):
            if name not in sems:
                sems[name] = ctx.enter_context(nc.semaphore(name))
            return sems[name]

        raw_loaded = [sem(f"raw_loaded{i}") for i in range(NRAW)]
        hi_ready, lo_ready, weights_used = sem("hi_ready"), sem("lo_ready"), sem("weights_used")
        bank_full = [sem(f"bank_full{i}") for i in range(8)]
        bank_done = [sem(f"bank_done{i}") for i in range(8)]

        def pj(job):
            return ps[JOBS[job][0]]

        def wait_full(eng, job):
            b, _, full, end, _ = JOBS[job]
            if end is not None:
                eng.wait_ge(weights_used, end + 1)
            else:
                eng.wait_ge(bank_full[b], full + 1)

        def wait_done(eng, job):
            b, k = JOBS[job][:2]
            eng.wait_ge(bank_done[b], k + 1)

        def release(ins, job):
            ins.then_inc(bank_done[JOBS[job][0]], 1)

        def GATE_UNIT(e):
            return NB + 2 + 3 * (e - 1)

        def halves(v, do, sync, buf, hi, lo, k0, ready):
            for j in range(2):
                b3 = buf[:, j, :].rearrange("p (c s) -> p c s", s=S)
                do(v.tensor_scalar(hi[:, k0 + 2 * j:k0 + 2 * j + 2, :], b3, 0.5, None, ALU.mult))
            sync()
            for j in range(2):
                b3 = buf[:, j, :].rearrange("p (c s) -> p c s", s=S)
                d = slice(k0 + 2 * j, k0 + 2 * j + 2)
                v.scalar_tensor_tensor(lo[:, d, :], b3, 0.5, hi[:, d, :].bitcast(f32), ALU.mult, ALU.subtract).then_inc(sem(ready), 1)

        MLA_FILL = [n for name in ("xbc1", "xbc2", "xbc3", "xbc4", "xbc5", "gm0", "gm1") for n in UNIT[name]]

        block = ctx.enter_context(nc.Block())

        @block.sync
        def _(sp):
            for t in range(TT):
                sp.dma_start(x[:, t, :], x_d[:, t, :]).then_inc(sem(f"x{t}_loaded"), 16)
            sp.dma_start(cst[:, :], cst_d).then_inc(sem("cst_loaded"), 16)
            sp.dma_start(raw[:, 0, :], w_d[0]).then_inc(raw_loaded[0], 16)
            sp.dma_start(sml[:, :], sml_d).then_inc(sem("sml_loaded"), 16)
            sp.dma_start(posi[:, :], pos_d).then_inc(sem("pos_loaded"), 16)
            for n in range(1, NRAW):
                sp.dma_start(raw[:, n, :], w_d[n]).then_inc(raw_loaded[n], 16)
            with sp.Fori(1, NU // NRAW) as i:
                for j in range(NRAW):
                    sp.wait_ge(lo_ready, i * NRAW + (j + 1 - NRAW))
                    sp.dma_start(raw[:, j, :], w_d[bass.ds(i * NRAW + j, 1), :, :].rearrange("u p n -> (u p) n")).then_inc(raw_loaded[j], 16)
            for n in range(NU // NRAW * NRAW, NU):
                sp.wait_ge(lo_ready, n + 1 - NRAW)
                sp.dma_start(raw[:, n % NRAW, :], w_d[n]).then_inc(raw_loaded[n % NRAW], 16)

        @block.gpsimd
        def _(pool):
            def lo(value, j):
                pool.wait_ge(hi_ready, value)
                pool.tensor_tensor(wlo[:, j, :], raw[:, j, :], whi[:, j, :].bitcast(f32), ALU.subtract).then_inc(lo_ready, 1)

            with pool.Fori(0, NU // NSPL) as i:
                for j in range(NSPL):
                    lo(i * NSPL + (j + 1), j)
            for n in range(NU // NSPL * NSPL, NU):
                lo(n + 1, n % NSPL)

        @block.scalar
        def _(act):
            made = [0]

            def hi_upto(last):
                while made[0] <= min(last, NU - 1):
                    n = made[0]
                    act.wait_ge(raw_loaded[n % NRAW], 16 * (n // NRAW + 1))
                    if n >= NSPL:
                        act.wait_ge(weights_used, n - NSPL + 1)
                    act.activation(whi[:, n % NSPL, :], raw[:, n % NRAW, :], ACT.Copy).then_inc(hi_ready, 1)
                    made[0] += 1

            def norm_squares(name, src, dst, tiles=range(TT)):
                for t in tiles:
                    act.activation(dst[:, t, :], src[:, t, :], ACT.Square, accum_out=stat[:, STAT[name] + t:STAT[name] + t + 1]).then_inc(sem("squares_" + name), 1)

            def hi_parts(name, nct, k0, gain=None, c0=0):
                for c in range(c0, nct):
                    job = (name, c // 2)
                    if c % 2 == 0:
                        wait_full(act, job)
                    act.activation(xhi[:, k0 + c, :], pj(job)[:, c % 2 * S:c % 2 * S + S], ACT.Copy,
                                   scale=1.0 if gain is None else gain[:, c:c + 1]).then_inc(sem("xhi_ready"), 1)

            def copy(job, dst, cols=slice(None), scale=1.0, rows=slice(None)):
                wait_full(act, job)
                release(act.activation(dst, pj(job)[rows, cols], ACT.Copy, scale=scale), job)

            def tanh_half(job, dst):
                wait_full(act, job)
                return act.activation(dst, pj(job)[:, :].rearrange("p (c s) -> p c s", s=S), ACT.Tanh, scale=0.5)

            for t in range(TT):
                act.wait_ge(sem(f"x{t}_loaded"), 16)
                norm_squares("x", x, xn, (t,))
            hi_upto(0)
            act.wait_ge(sem("sml_loaded"), 16)
            hi_parts("x", 8, 0, D("g_pre"))
            hi_upto(2)
            act.wait_ge(sem("rope_arg"), 1)
            act.activation(ropt[:, 6:8, :], ropt[:, 4:6, :], ACT.Sin).then_inc(sem("rope_sin"), 1)
            for name, c0, w in (("qn", 0, 512), ("kv1", 512, 512), ("kv2", 1024, 280)):
                hi_upto(UNIT[name][0] + 2)
                hi_upto(UNIT[name][1] + 2)
                for t in range(TT):
                    copy((name, t), nq[:, t, c0:c0 + w], slice(0, w))
            for name, c0 in (("qr", 0), ("kr", 512)):
                hi_upto(UNIT[name][0] + 2)
                hi_upto(UNIT[name][1] + 2)
                for t in range(TT):
                    copy((name, t), qk[:, t, c0:c0 + 512])
            act.wait_ge(sem("gates_in"), TT)
            act.activation(stat[:, 192:240], stat[:, 192:240], ACT.Tanh, scale=0.5).then_inc(sem("gates_tanh"), 1)
            hi_upto(UNIT["vr0"][1] + 2)
            hi_upto(UNIT["vr1"][1] + 2)
            for j in range(2):
                copy(("qT", j), qT[:, 2 * j:2 * j + 2, :].rearrange("p c s -> p (c s)"), scale=0.125)
            wait_done(act, ("cT", 0))
            act.activation(xchi[:, :, :, :], xcf[:, :, :, :], ACT.Copy).then_inc(sem("xchi_ready"), 1)
            hi_upto(UNIT["w1v"][1] + 2)
            hi_upto(UNIT["zn"][1] + 2)

            def silu_gate(name, dst, c0):
                for j in range(2):
                    tanh_half((name, j), dst[:, c0 + 2 * j:c0 + 2 * j + 2, :]).then_inc(sem("tanh_" + name), 1)

            silu_gate("zn", znT, 0)
            act.wait_ge(sem("gelu_in"), 1)
            act.activation(hg[:, 2, :], hg[:, 1, :], ACT.Tanh, scale=0.7978845608028654).then_inc(sem("gelu_tanh"), 1)
            hi_upto(UNIT["zr0"][0] + 2)
            hi_upto(UNIT["zr0"][1] + 2)
            act.wait_ge(sem("cmp_scores"), 1)
            act.activation(pr[:, 0, :].rearrange("p (h c) -> p h c", c=32)[:, :, 0:15], cs[:, :, :], ACT.Exp).then_inc(sem("cmp_exp"), 1)
            copy(("Tc", 0), pT[:, 0, :])

            def exps(S_, u, p_buf, sums, width0):
                act.wait_ge(sem("max_ready"), MAXN[(S_, u)])
                for t in range(TT):
                    c = slice(0, width0) if t == 0 else slice(width0, width0 + S)
                    k = 2 * (u % 8)
                    ins = act.activation(p_buf[:, c], pj((S_, u))[:, c], ACT.Exp, bias=stat[:, NMAX + k + t:NMAX + k + t + 1],
                                         accum_out=stat[:, sums + k + t:sums + k + t + 1])
                release(ins, (S_, u))

            fill = {1: "zr1", 4: "zr1", 6: "ma0", 9: "ma0", 11: "ma1", 14: "ma1"}
            seen = {}
            silu_gate("zr0", zrT, 0)
            for u in range(16):
                if u >= 2:
                    wait_full(act, ("T", u - 2))
                exps("S", u, pr[:, u % 2, :], SUMS, P)
                if u in fill:
                    name = fill[u]
                    k = seen[name] = seen.get(name, -1) + 1
                    hi_upto(UNIT[name][k] + 2)
                    if k == 1:
                        if name[0] == "z":
                            silu_gate(name, zrT, 4 * int(name[2]))
                        else:
                            for j in range(2):
                                release(tanh_half((name, j), maT[:, 4 * int(name[2]) + 2 * j:4 * int(name[2]) + 2 * j + 2, :]), (name, j))
            act.dma_start(decay[:, :, :], dec_d).then_inc(sem("decay_loaded"), 16)
            for h in range(4):
                copy(("QK", h), qkT[:, h % 2, :])
                hi_upto(UNIT[f"mb{h // 2}"][h % 2] + 2)
                if h % 2:
                    for j in range(2):
                        c = 4 * (h // 2) + 2 * j
                        release(tanh_half((f"mb{h // 2}", j), mbT[:, c:c + 2, :]), (f"mb{h // 2}", j))
            wait_done(act, ("on", 1))
            act.dma_start(npost[:, :], npost_d).then_inc(sem("npost_loaded"), 16)
            hi_upto(UNIT["wo1"][1] + 1)
            for t in range(TT):
                if t:
                    act.wait_ge(sem("squares_post"), 2)
                for i in range(2):
                    wait_full(act, (f"wo{i}", t))
                    k = STAT["post"] + 2 * t + i
                    act.activation(pr[:, i, :], pj((f"wo{i}", t))[:, :], ACT.Square, accum_out=stat[:, k:k + 1]).then_inc(sem("squares_post"), 1)
                act.wait_ge(sem("x1_ready"), t + 1)
                act.activation(xn[:, t, :], x[:, t, :], ACT.Square, accum_out=stat[:, STAT["u"] + t:STAT["u"] + t + 1]).then_inc(sem("squares_u"), 1)
            hi_upto(UNIT["wo1"][1] + 2)
            hi_parts("u", 8, 0, D("g_mix"))
            def conv_first(i):
                for j in range(2):
                    job = (f"xbc{i}", j)
                    wait_full(act, job)
                    if i == 0:
                        act.wait_ge(sem("conv_halved"), 2)
                    if 2 * i + j >= 2:
                        act.wait_ge(sem("silu_done"), 2 * i + j - 1)
                    for c in range(2):
                        k = 4 * i + 2 * j + c
                        act.activation(cv[:, j, c, :], pj(job)[:, c * S:c * S + S], ACT.Identity,
                                       scale=sml[:, CW + 72 + k:CW + 73 + k], bias=sml[:, CB_ + k:CB_ + k + 1]).then_inc(sem("conv_first"), 1)

            def conv_tanh(i):
                for j in range(2):
                    wait_done(act, (f"xbc{i}", j))
                    act.activation(xbc[:, 4 * i + 2 * j:4 * i + 2 * j + 2, :], cv[:, j, :, :], ACT.Tanh).then_inc(sem("conv_tanh"), 1)

            for name, dst, w, junk, stat_, c0 in (("pa", pa, 416, 0, "qa", 32), ("pb", pb, 288, 384, "ck", 0)):
                hi_upto(UNIT[name][0] + 2)
                hi_upto(UNIT[name][1] + 2)
                width = 384 if name == "pa" else 256
                for t in range(TT):
                    copy((name, t), dst[:, t, :], slice(0, w))
                for t in range(TT):
                    wait_done(act, (name, t))
                    act.activation(qm[:, t, junk:junk + width], dst[:, t, c0:c0 + width], ACT.Square,
                                   accum_out=stat[:, STAT[stat_] + t:STAT[stat_] + t + 1]).then_inc(sem("squares_qa"), 1)
            hi_parts("qa", 3, 8, D("g_qa"))
            hi_upto(UNIT["xbc0"][0] + 2)
            hi_parts("ck", 2, 11, D("g_ckv"))
            hi_upto(UNIT["xbc0"][1] + 2)
            conv_first(0)
            for i in range(3):
                hi_upto(UNIT[f"wq{i}"][0] + 2)
                for t in range(TT):
                    copy((f"wq{i}", t), qm[:, t, 512 * i:512 * i + 512], scale=96 ** -0.5)
            hi_upto(UNIT["kn"][0] + 2)
            for j in range(4):
                wait_full(act, ("kn", j))
                v = pj(("kn", j))[:, :].rearrange("p (c s) -> p c s", s=S)
                act.activation(km[0:64, 4 * j:4 * j + 4:2, :], v[0:64, :, :], ACT.Copy)
                release(act.activation(km[0:64, 4 * j + 1:4 * j + 4:2, :], v[64:128, :, :], ACT.Copy), ("kn", j))
            hi_upto(UNIT["vv"][0] + 2)
            def latent_gate(i):
                for j in range(2):
                    c = 4 * i + 2 * j
                    release(tanh_half((f"gm{i}", j), gmT[:, c:c + 2, :]), (f"gm{i}", j))

            copy(("mQ", 0), qmT[0:96, 0, :], rows=slice(0, 96))

            for u in range(16):
                if u % 2 == 0 and u < 14:
                    p = u // 2 + 1
                    if p >= 2:
                        wait_full(act, ("mS", 2 * p - 3))
                    copy(("mQ", p), qmT[0:96, p % 2, :], rows=slice(0, 96))
                if u >= 2:
                    wait_full(act, ("mT", u - 2))
                exps("mS", u, pr2[:, u % 2, :], SUMS, P)
                if u < 13:
                    hi_upto(MLA_FILL[u] + 2)
                if u < 10 and u % 2:
                    conv_first(u // 2 + 1)
                if u % 2 == 0 and u <= 10:
                    conv_tanh(u // 2)
                if u == 11:
                    latent_gate(0)
            hi_upto(MLA_FILL[13] + 2)
            latent_gate(1)
            hi_parts("om", 8, 8)
            act.wait_ge(sem("dt_in"), 1)
            act.activation(dts[:, 1, :], dts[:, 1, :], ACT.Exp).then_inc(sem("dt_exp"), 1)
            act.activation(dts[:, 5, 0:32], D("a_log"), ACT.Exp).then_inc(sem("dt_exp"), 1)
            act.wait_ge(sem("dt_one"), 1)
            act.activation(dts[:, 3, :], dts[:, 2, :], ACT.Ln).then_inc(sem("dt_ln"), 1)
            hi_upto(UNIT["ym1"][1] + 2)
            wait_full(act, ("acum", 0))
            act.activation(dts[:, 6, 32:64], pj(("acum", 0))[:, 32:64], ACT.Exp).then_inc(sem("eac_ready"), 1)
            wait_done(act, ("acum", 0))
            act.activation(dts[:, 6, 0:32], dts[:, 6, 0:32], ACT.Exp).then_inc(sem("dte_ready"), 1)
            copy(("Bt", 0), btok[:, :])
            for i in range(8):
                copy(("xt", i), xtok[:, i // 4, i % 4 * 512:i % 4 * 512 + 512])

            def scan_unit(n, half):
                hi_upto(UNIT[n][half] + 2)
                if half == 0:
                    return
                k = int(n[-1])
                for j in range(2):
                    if n[0] == "z":
                        wait_full(act, (n, j))
                        act.activation(zt[:, j, 512 * k:512 * k + 512], pj((n, j))[:, :], ACT.Tanh, scale=0.5).then_inc(sem("tanh_z"), 1)
                    else:
                        release(tanh_half((n, j), gsT[:, 4 * k + 2 * j:4 * k + 2 * j + 2, :]), (n, j))

            def y_hi(g):
                hi_parts("y", 4 * g + 4, 8 if g < 2 else -8, D("g_ssd"), 4 * g)

            wait_done(act, ("ym1", 1))
            scan_unit("z0", 0)
            scan_unit("z0", 1)
            for i in range(8):
                g, t = i // 2, i % 2
                for q in (2 * i, 2 * i + 1):
                    if q >= 2:
                        act.wait_ge(sem("segM_ready"), q - 1)
                    wait_full(act, ("seg", q))
                    release(act.activation(segE[:, q % 2, :], pj(("seg", q))[:, :], ACT.Exp), ("seg", q))
                if t == 0:
                    if g >= 1:
                        wait_full(act, ("off", g - 1))
                    copy(("state", g), st[:, :])
                for unit in SCAN_FILL[i]:
                    scan_unit(*unit)
                if i in (3, 5, 7):
                    y_hi(i // 2 - 1)
                act.wait_ge(sem("y_gated"), i + 1)
                act.activation(yt[:, 1, :], zt[:, t, 512 * g:512 * g + 512], ACT.Square, accum_out=stat[:, STAT["y"] + i:STAT["y"] + i + 1]).then_inc(sem("squares_y"), 1)
            hi_upto(UNIT["ys0"][1] + 2)
            y_hi(3)
            act.dma_start(memt[:, :, :], mem_d).then_inc(sem("mem_loaded"), 16)
            hi_upto(UNIT["ys1"][-1])
            act.wait_ge(sem("mem_loaded"), 16)
            norm_squares("mem", memt, xn)
            hi_upto(UNIT["ys1"][-1] + 2)
            hi_upto(UNIT["wp1"][0] + 2)
            hi_parts("mem", 8, 8, D("g_mem"))
            for t in range(TT):
                hi_upto(UNIT["wp1"][1] + 1 + t)
                wait_done(act, ("wp1", t))
                act.activation(xn[:, t, :], x[:, t, :], ACT.Square, accum_out=stat[:, STAT["h"] + t:STAT["h"] + t + 1]).then_inc(sem("squares_h"), 1)
            for i in range(2):
                hi_upto(UNIT[f"xk{i}"][1] + 2)
                for j in range(2):
                    c = 4 * i + 2 * j
                    copy((f"xk{i}", j), kx[:, c:c + 2, :].rearrange("p c s -> p (c s)"))
            hi_upto(UNIT["xv0"][1] + 2)
            hi_parts("h", 8, 0, D("g_xa"))
            hi_upto(UNIT["xv1"][1] + 2)

            def query_copies(i):
                hi_upto(UNIT[f"xq{i}"][1] + 2)
                for j in range(2):
                    c = 4 * i + 2 * j
                    copy((f"xq{i}", j), qx[:, c:c + 2, :].rearrange("p c s -> p (c s)"), scale=0.0625)

            def cross_exps(h):
                exps("xS", h, px[:, h % 2, :], SUMS, S)

            def cross_hi(h):
                wait_full(act, ("xO", h))
                act.activation(xhi[:, 8 + 2 * h:10 + 2 * h, :], pj(("xO", h))[:, :].rearrange("p (c s) -> p c s", s=S), ACT.Copy).then_inc(sem("xhi_ready"), 1)

            query_copies(0)
            cross_exps(0)
            hi_upto(UNIT["xq1"][0] + 2)
            copy(("xT", 0), pxT[:, 0, :])
            cross_exps(1)
            query_copies(1)
            cross_hi(0)
            copy(("xT", 1), pxT[:, 1, :])
            cross_exps(2)
            cross_hi(1)
            cross_exps(3)
            hi_upto(UNIT["xo0"][0] + 2)
            for h in (2, 3):
                copy(("xT", h), pxT[:, h % 2, :])
                cross_hi(h)
            hi_upto(UNIT["xo1"][1] + 1)
            for t in range(TT):
                wait_done(act, ("xo1", t))
                act.activation(xn[:, t, :], x[:, t, :], ACT.Square, accum_out=stat[:, STAT["m"] + t:STAT["m"] + t + 1]).then_inc(sem("squares_m"), 1)
            hi_upto(UNIT["xo1"][1] + 2)
            hi_parts("m", 8, 0, D("g_moe"))
            hi_upto(UNIT["rt"][0] + 3)
            act.wait_ge(sem("router_arg"), 1)
            act.activation(rtl[:, 2, 0:8], rtl[:, 2, 0:8], ACT.Exp).then_inc(sem("router_exp"), 1)
            act.wait_ge(sem("router_arg"), 2)
            act.activation(rtl[:, 2, 8:10], rtl[:, 2, 8:10], ACT.Exp).then_inc(sem("router_exp"), 1)
            hi_upto(NB + 3)
            act.wait_ge(weights_used, NB + 1)
            act.activation(sg[:, 0, :], ps[0][:, :], ACT.Silu).then_inc(sem("silu_ready"), 1)
            wait_done(act, ("cb", 0))
            act.dma_start(scratch, combt[:, :]).then_inc(sem("comb_out"), 16)
            act.wait_ge(sem("comb_out"), 16)
            def repeated(e0, e1, loaded):
                act.dma_start(comb[:, e0:e1, :].rearrange("p e s -> p (e s)"),
                              scratch[e0:e1].rearrange("e s -> (e s)").partition_broadcast(P)).then_inc(sem(loaded), 16)

            repeated(0, 3, "comb_loaded")
            repeated(3, 12, "comb_rest")

            def expert_act(e, i, last=False):
                n, s = GATE_UNIT(e), e % 2

                def hi(m):
                    act.wait_ge(raw_loaded[m % NRAW], i * 32 + 16 * (m // NRAW + 1))
                    act.wait_ge(weights_used, i * 6 + (m - NSPL + 1))
                    act.activation(whi[:, m % NSPL, :], raw[:, m % NRAW, :], ACT.Copy).then_inc(hi_ready, 1)

                hi(n + 2)
                hi(n + 3)
                act.wait_ge(weights_used, i * 6 + (n + 1))
                if e >= 2:
                    act.wait_ge(sem("gated"), i * 2 + (e - 1))
                act.activation(sg[:, s, :], ps[2 * s][:, :], ACT.Silu).then_inc(sem("silu_ready"), 1)
                if not last:
                    hi(n + 4)

            expert_act(1, 0)
            repeated(12, 22, "comb_rest")
            expert_act(2, 0)
            repeated(22, NEXP, "comb_rest")
            with act.Fori(0, (NEXP - 4) // 2) as i:
                expert_act(3, i)
                expert_act(4, i)
            act.dma_start(nfin[:, :], nfin_d).then_inc(sem("nfin_loaded"), 16)
            expert_act(NEXP - 1, 0, last=True)
            for t in range(TT):
                act.wait_ge(sem("h3_ready"), t + 1)
                act.activation(xn[:, t, :], x[:, t, :], ACT.Square, accum_out=stat[:, STAT["f"] + t:STAT["f"] + t + 1]).then_inc(sem("squares_f"), 1)
            for t in range(TT):
                for i in range(2):
                    d = slice(512 * i, 512 * i + 512)
                    act.wait_ge(sem("out_ready"), 2 * t + i + 1)
                    act.dma_start(out_d[:, t, d], xn[:, t, d]).then_inc(sem("out_stored"), 16)
            act.wait_ge(sem("out_stored"), 64)

        @block.vector
        def _(dve):
            v = nc.vector
            steps = [0]
            hi_seen = [0]

            def do(ins):
                steps[0] += 1
                ins.then_inc(sem("dve_step"), 1)

            def sync():
                dve.wait_ge(sem("dve_step"), steps[0])

            def col(k, n=1):
                return stat[:, k:k + n]

            def inverse_roots(*items):
                w, m, t = ([col(MISC + k + i) for i in range(len(items))] for k in (6, 8, 10))
                for i, (dst, src, factor) in enumerate(items):
                    do(v.tensor_scalar(w[i], src, factor, EPS, ALU.mult, ALU.add))
                    do(v.tensor_scalar(m[i], src, -0.5 * factor, -0.5 * EPS, ALU.mult, ALU.add))
                sync()
                for i, (dst, _, _) in enumerate(items):
                    do(v.tensor_scalar(dst.bitcast(i32), w[i].bitcast(i32), -0.5, 1597463007.0, ALU.mult, ALU.add))
                sync()
                for _ in range(3):
                    for i, (dst, _, _) in enumerate(items):
                        do(v.scalar_tensor_tensor(t[i], dst, m[i], dst, ALU.mult, ALU.mult))
                    sync()
                    for i, (dst, _, _) in enumerate(items):
                        do(v.scalar_tensor_tensor(dst, t[i], 1.5, dst, ALU.add, ALU.mult))
                    sync()

            def rstd(name, n, width, extra=0):
                k = STAT[name] + extra
                inverse_roots(*((col(k + RSTD + i), col(k + i), 1.0 / width) for i in range(n)))

            def norm_tile(name, src, dst, ready, t):
                dve.wait_ge(sem("squares_" + name), t + 1)
                rstd(name, 1, DM, t)
                k = STAT[name] + RSTD + t
                v.tensor_scalar(dst[:, t, :], src[:, t, :], col(k), None, ALU.mult).then_inc(sem(ready), 1)

            def norm(name, src, dst, ready):
                for t in range(TT):
                    norm_tile(name, src, dst, ready, t)

            def lo_parts(name, nct, k0, gain=None, c0=0):
                for c in range(c0, nct):
                    job = (name, c // 2)
                    if c % 2 == 0:
                        hi_seen[0] += min(2, nct - c)
                        dve.wait_ge(sem("xhi_ready"), hi_seen[0])
                    src = pj(job)[:, c % 2 * S:c % 2 * S + S]
                    if gain is None:
                        ins = v.tensor_tensor(xlo[:, k0 + c, :], src, xhi[:, k0 + c, :].bitcast(f32), ALU.subtract)
                    else:
                        ins = v.scalar_tensor_tensor(xlo[:, k0 + c, :], src, gain[:, c:c + 1], xhi[:, k0 + c, :].bitcast(f32), ALU.mult, ALU.subtract)
                    if c % 2 or c == nct - 1:
                        release(ins, job)

            def copy(job, dst, rows=slice(None), cols=slice(None)):
                wait_full(dve, job)
                release(v.tensor_copy(dst, pj(job)[rows, cols]), job)

            def rotate(x1, x2, cos, sin, t4, ready, nth=1):
                do(v.tensor_tensor(t4[0], x1, cos, ALU.mult))
                do(v.tensor_tensor(t4[1], x2, sin, ALU.mult))
                do(v.tensor_tensor(t4[2], x2, cos, ALU.mult))
                do(v.tensor_tensor(t4[3], x1, sin, ALU.mult))
                sync()
                do(v.tensor_tensor(x1, t4[0], t4[1], ALU.subtract))
                v.tensor_tensor(x2, t4[2], t4[3], ALU.add).then_inc(sem(ready), 1)
                sync()
                dve.wait_ge(sem(ready), nth)

            norm("x", x, xn, "xn_ready")
            dve.wait_ge(sem("sml_loaded"), 16)
            lo_parts("x", 8, 0, D("g_pre"))
            dve.wait_ge(sem("cst_loaded"), 16)
            v.tensor_copy(identb[:, :], ident).then_inc(sem("masks_ready"), 1)
            v.tensor_copy(negb[:, :], C("negmask")).then_inc(sem("masks_ready"), 1)
            dve.wait_ge(sem("pos_loaded"), 16)
            do(v.tensor_copy(col(MISC, 2), posi[:, :]))
            sync()
            ang, kf = ropt[:, 0, :], ropt[:, 1, :]
            ki = ropt[:, 3, :].bitcast(i32)
            sa, ca = ropt[:, 4, :], ropt[:, 5, :]
            for t in range(TT):
                do(v.tensor_scalar(ang[:, 16 * t:16 * t + 16], C("invf"), col(MISC + t), None, ALU.mult))
            sync()
            do(v.tensor_scalar(ki, ang, 1.0 / TWO_PI, None, ALU.mult))
            sync()
            do(v.tensor_copy(kf, ki))
            sync()
            for part in PI_PARTS:
                do(v.scalar_tensor_tensor(ang, kf, -part, ang, ALU.mult, ALU.add))
                sync()
            do(v.tensor_scalar(ca, ang, TWO_PI / 4, None, ALU.add))
            do(v.tensor_copy(sa, ang))
            sync()
            both = ropt[:, 4:6, :]
            turn = ropt[:, 1:3, :]
            for op, sign in ((ALU.is_gt, 1.0), (ALU.is_lt, -1.0)):
                do(v.tensor_scalar(turn, both, sign * TWO_PI / 2, -sign * TWO_PI, op, ALU.mult))
                sync()
                do(v.tensor_tensor(both, both, turn, ALU.add))
                sync()
            v.tensor_scalar(both, both, 3.1415925, -3.1415925, ALU.min, ALU.max).then_inc(sem("rope_arg"), 1)
            v.tensor_scalar(D("conv_w"), D("conv_w"), 0.5, None, ALU.mult).then_inc(sem("conv_halved"), 1)
            v.tensor_scalar(D("conv_b"), D("conv_b"), 0.5, None, ALU.mult).then_inc(sem("conv_halved"), 1)
            do(v.memset(pr[:, 0, :], 0.0))
            do(v.memset(vcb[:, :, :, :], 0.0))
            sync()

            for n in ("qn", "kv1"):
                for t in range(TT):
                    wait_done(dve, (n, t))
            heads = nq[:, :, 0:896].rearrange("p t (h d) -> p t h d", d=64)
            t4 = [ropetmp[:, k, 0:224].rearrange("p (t h d) -> p t h d", t=TT, d=8) for k in range(4)]
            cosb = C("cos").rearrange("p (t d) -> p t d", t=TT).unsqueeze(2).to_broadcast([P, TT, 14, 8])
            sinb = C("sin").rearrange("p (t d) -> p t d", t=TT).unsqueeze(2).to_broadcast([P, TT, 14, 8])
            rotate(heads[:, :, :, 0:8], heads[:, :, :, 8:16], cosb, sinb, t4, "nq_rotated")
            for t in range(TT):
                wait_done(dve, ("kv2", t))
                v.tensor_tensor(col(GATE + 24 * t, 24), nq[:, t, 1280:1304], D("b_gate"), ALU.add).then_inc(sem("gates_in"), 1)
            for i in range(2):
                for t in range(TT):
                    copy((f"vr{i}", t), vr[:, t, 512 * i:512 * i + 512])
            wait_full(dve, ("kT", 0))
            for g in range(2):
                for r in range(2):
                    ins = v.tensor_copy(kT[64 * r:64 * r + 64, g, :], pj(("kT", 0))[64 * g:64 * g + 64, :])
                    if (g, r) == (1, 1):
                        release(ins, ("kT", 0))
            wait_full(dve, ("cT", 0))
            for kv in range(2):
                pe_ = D("pe_k") if kv == 0 else D("pe_v")
                for j in range(2):
                    for g in range(2):
                        for late in range(2):
                            src = pj(("cT", 0))[64 * g:64 * g + 64, kv * S:kv * S + S].rearrange("p (c r) -> p r c", r=16)[:, j::2, late:late + 15]
                            dst = xcf[64 * j:64 * j + 64, kv, 8 * late:8 * late + 8, 15 * g:15 * g + 15]
                            code = pe_[64 * j:64 * j + 64, 8 * late:8 * late + 8].unsqueeze(2).to_broadcast([64, 8, 15])
                            ins = v.tensor_tensor(dst, src, code, ALU.add)
            release(ins, ("cT", 0))
            dve.wait_ge(sem("xchi_ready"), 1)
            v.tensor_tensor(xclo[:, :, :, :], xcf[:, :, :, :], xchi[:, :, :, :].bitcast(f32), ALU.subtract).then_inc(sem("xclo_ready"), 1)
            copy(("hs", 0), pT[0:30, 0, :], rows=slice(0, 30))

            def silu_gate(name, dst, c0):
                for j in range(2):
                    dve.wait_ge(sem("tanh_" + name), j + 1)
                    d = dst[:, c0 + 2 * j:c0 + 2 * j + 2, :]
                    release(v.scalar_tensor_tensor(d, d, 1.0, pj((name, j))[:, :].rearrange("p (c s) -> p c s", s=S), ALU.add, ALU.mult), (name, j))

            silu_gate("zn", znT, 0)
            wait_full(dve, ("hid", 0))
            release(v.tensor_copy(hg[:, 0, :].rearrange("p (a c) -> p a c", c=30), pj(("hid", 0))[:, 0:128].rearrange("p (a c) -> p a c", c=32)[:, :, 0:30]), ("hid", 0))
            wait_done(dve, ("hid", 0))
            do(v.tensor_tensor(hg[:, 1, :], hg[:, 0, :], hg[:, 0, :], ALU.mult))
            sync()
            do(v.scalar_tensor_tensor(hg[:, 3, :], hg[:, 1, :], 0.044715, hg[:, 0, :], ALU.mult, ALU.mult))
            sync()
            v.tensor_tensor(hg[:, 1, :], hg[:, 3, :], hg[:, 0, :], ALU.add).then_inc(sem("gelu_in"), 1)
            dve.wait_ge(sem("gelu_tanh"), 1)
            do(v.scalar_tensor_tensor(hg[:, 3, :], hg[:, 2, :], 1.0, hg[:, 0, :], ALU.add, ALU.mult))
            sync()
            v.tensor_scalar(hg[:, 3, :], hg[:, 3, :], 0.5, None, ALU.mult).then_inc(sem("gelu_ready"), 1)
            dve.wait_ge(sem("gates_tanh"), 1)
            do(v.tensor_scalar(col(GATE, 48), col(GATE, 48), 0.5, 0.5, ALU.mult, ALU.add))

            wait_full(dve, ("kvc", 0))
            do(v.tensor_copy(kcT[:, 0:30], pj(("kvc", 0))[:, 0:30]))
            for g in range(2):
                for i in range(4):
                    ins = v.tensor_copy(vcb[32 * i:32 * i + 15, g, i, :], pj(("kvc", 0))[0:15, 64 + 64 * g:128 + 64 * g])
            release(ins, ("kvc", 0))
            wait_full(dve, ("Sc", 0))
            cs4 = cs[:, :, :].rearrange("p (t h) c -> p t h c", t=TT)
            release(v.tensor_tensor(cs4, pj(("Sc", 0))[:, :].rearrange("p (t h c) -> p t h c", t=TT, c=32)[:, :, :, 0:15],
                                    C("cmpmask").rearrange("p (t c) -> p t c", t=TT).unsqueeze(2).to_broadcast([P, TT, 8, 15]), ALU.add), ("Sc", 0))
            wait_done(dve, ("Sc", 0))
            do(v.tensor_reduce(col(CMAX, 16), cs[:, :, :], AX.X, ALU.max))
            sync()
            do(v.tensor_scalar(col(CMAX, 16), col(CMAX, 16), -1e29, None, ALU.max))
            sync()
            v.tensor_tensor(cs[:, :, :], cs[:, :, :], col(CMAX, 16).unsqueeze(2).to_broadcast([P, 16, 15]), ALU.subtract).then_inc(sem("cmp_scores"), 1)
            dve.wait_ge(sem("cmp_exp"), 1)
            do(v.tensor_reduce(col(CSUM, 16), pr[:, 0, :].rearrange("p (h c) -> p h c", c=32)[:, :, 0:15], AX.X, ALU.add))
            sync()
            do(v.tensor_scalar(col(CSUM, 16), col(CSUM, 16), 1.1754944e-38, None, ALU.max))
            sync()
            do(v.reciprocal(col(CSUM, 16), col(CSUM, 16)))
            sync()
            gates = stat[:, GATE:GATE + 48].rearrange("p (t h b) -> p t h b", t=TT, b=3)
            do(v.tensor_tensor(col(CGATE, 16).rearrange("p (t h) -> p t h", t=TT), col(CSUM, 16).rearrange("p (t h) -> p t h", t=TT), gates[:, :, :, 0], ALU.mult))
            sync()
            def maxima(job, width0, u):
                wait_full(dve, job)
                k = NMAX + 2 * (u % 8)
                v.tensor_reduce(col(k), pj(job)[:, 0:width0], AX.X, ALU.max, negate=True)
                v.tensor_reduce(col(k + 1), pj(job)[:, width0:width0 + S], AX.X, ALU.max, negate=True).then_inc(sem("max_ready"), 1)

            def compressed_out(t):
                wait_full(dve, ("Oc", t))
                release(v.tensor_tensor(oacc[:, t, :].rearrange("p (h d) -> p h d", d=64), pj(("Oc", t))[:, :].rearrange("p (h d) -> p h d", d=64),
                                        col(CGATE + 8 * t, 8).unsqueeze(2).to_broadcast([P, 8, 64]), ALU.mult), ("Oc", t))

            def attention_out(q):
                br, h0 = q // 2 + 1, 4 * (q % 2)
                wait_full(dve, ("O", q))
                k = 2 * (4 * q % 8)
                do(v.reciprocal(col(RSUM + k, 8), col(SUMS + k, 8)))
                sync()
                gf = col(GF + k, 8).rearrange("p (h t) -> p h t", t=TT)
                do(v.tensor_tensor(gf, col(RSUM + k, 8).rearrange("p (h t) -> p h t", t=TT),
                                   gates[:, :, h0:h0 + 4, br].rearrange("p t h -> p h t"), ALU.mult))
                sync()
                src = pj(("O", q))[:, :].rearrange("p (h t d) -> p h t d", t=TT, d=64)
                for t in range(TT):
                    ins = v.tensor_tensor(tmp[:, t, 0:256].rearrange("p (h d) -> p h d", d=64), src[:, :, t, :],
                                          gf[:, :, t].unsqueeze(2).to_broadcast([P, 4, 64]), ALU.mult)
                release(ins, ("O", q))
                wait_done(dve, ("O", q))
                for t in range(TT):
                    d = oacc[:, t, 64 * h0:64 * h0 + 256]
                    v.tensor_tensor(d, d, tmp[:, t, 0:256], ALU.add).then_inc(sem("oacc_added"), 1)
                dve.wait_ge(sem("oacc_added"), 2 * (q + 1))

            qkh = qk[:, :, :].rearrange("p t (h d) -> p t h d", d=128)
            rc, rs_ = (C(n).rearrange("p (t d) -> p t d", t=TT) for n in ("rcos", "rsin"))
            maxima(("S", 0), P, 0)
            compressed_out(0)
            compressed_out(1)
            for u in range(16):
                if u < 15:
                    maxima(("S", u + 1), P, u + 1)
                copy(("T", u), pT[:, u % 2, 0:384], cols=slice(0, 384))
                if u in (0, 4):
                    silu_gate(f"zr{u // 4}", zrT, u)
                if u in (3, 5):
                    t = (u - 3) // 2
                    for n in ("qr", "kr"):
                        wait_done(dve, (n, t))
                    rotate(qkh[:, t, :, 0:64], qkh[:, t, :, 64:128], rc[:, t, :].unsqueeze(1).to_broadcast([P, 8, 64]),
                           rs_[:, t, :].unsqueeze(1).to_broadcast([P, 8, 64]),
                           [ropetmp[:, k, :].rearrange("p (h d) -> p h d", d=64) for k in range(4)], "qk_rotated", t + 1)
                if u % 4 == 0 and u:
                    attention_out(u // 4 - 1)
            attention_out(3)

            def gated_parts(job, gate, k0, full, ready):
                wait_full(dve, job)
                buf = full.rearrange("p (c s) -> p c s", s=S)
                release(v.scalar_tensor_tensor(buf, pj(job)[:, :].rearrange("p (c s) -> p c s", s=S), 0.5, gate, ALU.mult, ALU.mult), job)
                wait_done(dve, job)
                do(v.tensor_copy(xhi[:, k0:k0 + 2, :], buf))
                sync()
                v.tensor_tensor(xlo[:, k0:k0 + 2, :], buf, xhi[:, k0:k0 + 2, :].bitcast(f32), ALU.subtract).then_inc(sem(ready), 1)

            dve.wait_ge(sem("decay_loaded"), 16)
            for h in range(4):
                wait_full(dve, ("A", h))
                v.tensor_tensor(pT[:, h % 2, 0:S], pj(("A", h))[:, 0:S], decay[:, h, :], ALU.mult)
                release(v.tensor_tensor(pT[:, h % 2, S:S + P], pj(("A", h))[:, S:S + P], decay[:, h, 0:P], ALU.mult), ("A", h))
                if h == 0:
                    for j in range(2):
                        gated_parts(("on", j), znT[:, 2 * j:2 * j + 2, :], 8 + 2 * j, tmp[:, j, :], "on_parts")
                    dve.wait_ge(sem("on_parts"), 2)
                wait_full(dve, ("R", h))
                for t in range(TT):
                    do(v.bn_stats(tmp[:, 0, 8 * t:8 * t + 6], pj(("R", h))[:, t * S:t * S + S]))
                sync()
                for t in range(TT):
                    do(v.bn_aggr(tmp[:, 0, 16 + 2 * t:18 + 2 * t], tmp[:, 0, 8 * t:8 * t + 6]))
                sync()
                inverse_roots(*((tmp[:, 0, 20 + t:21 + t], tmp[:, 0, 17 + 2 * t:18 + 2 * t], 1.0) for t in range(TT)))
                for t in range(TT):
                    ins = v.tensor_scalar(xn[:, t, h * S:h * S + S], pj(("R", h))[:, t * S:t * S + S],
                                          tmp[:, 0, 16 + 2 * t:17 + 2 * t], tmp[:, 0, 20 + t:21 + t], ALU.subtract, ALU.mult)
                release(ins, ("R", h))

            def gate_branch(name, i, gate):
                for j in range(2):
                    job = (f"{name}{i}", j)
                    wait_full(dve, job)
                    d = gate[:, 4 * i + 2 * j:4 * i + 2 * j + 2, :]
                    release(v.scalar_tensor_tensor(d, d, 1.0, pj(job)[:, :].rearrange("p (c s) -> p c s", s=S), ALU.add, ALU.mult), job)

            gate_branch("ya", 0, maT)
            for j in range(4):
                gated_parts(("or", j), zrT[:, 2 * j:2 * j + 2, :], 2 * j, pr[:, j % 2, :], "or_parts")
            gate_branch("ya", 1, maT)
            for i in range(2):
                gate_branch("yb", i, mbT)
                for j in range(2):
                    wait_done(dve, (f"ya{i}", j))
                    wait_done(dve, (f"yb{i}", j))
                for j in range(2):
                    d = slice(4 * i + 2 * j, 4 * i + 2 * j + 2)
                    do(v.tensor_tensor(mbT[:, d, :], mbT[:, d, :], maT[:, d, :], ALU.add))
                sync()
                halves(v, do, sync, mbT[:, 4 * i:4 * i + 4, :].rearrange("p (j c) s -> p j (c s)", j=2), mThi, mTlo, 4 * i, "mT_parts")
            k = STAT["post"]
            dve.wait_ge(sem("npost_loaded"), 16)
            def post_sum(t):
                dve.wait_ge(sem("squares_post"), 2 * t + 2)
                do(v.tensor_tensor(col(k + RSTD + t), col(k + 2 * t), col(k + 2 * t + 1), ALU.add))
                sync()

            def post_add(t):
                for i in range(2):
                    release(v.scalar_tensor_tensor(tmp[:, i, :], pj((f"wo{i}", t))[:, :], col(k + RSTD + t), npost[:, 512 * i:512 * i + 512], ALU.mult, ALU.mult), (f"wo{i}", t))
                for i in range(2):
                    wait_done(dve, (f"wo{i}", t))
                v.tensor_tensor(x[:, t, :], x[:, t, :], tmp[:, :, :].rearrange("p a b -> p (a b)"), ALU.add).then_inc(sem("x1_ready"), 1)

            def scaled(t):
                v.tensor_scalar(xn[:, t, :], x[:, t, :], col(STAT["u"] + RSTD + t), None, ALU.mult).then_inc(sem("un_ready"), 1)

            post_root = [(col(k + RSTD + t), col(k + RSTD + t), 1.0 / DM) for t in range(TT)]
            next_root = [(col(STAT["u"] + RSTD + t), col(STAT["u"] + t), 1.0 / DM) for t in range(TT)]
            post_sum(0)
            inverse_roots(post_root[0])
            post_add(0)
            post_sum(1)
            dve.wait_ge(sem("squares_u"), 1)
            inverse_roots(next_root[0], post_root[1])
            scaled(0)
            dve.wait_ge(sem("x1_ready"), 1)
            post_add(1)
            dve.wait_ge(sem("squares_u"), 2)
            inverse_roots(next_root[1])
            scaled(1)
            lo_parts("u", 8, 0, D("g_mix"))

            for t in range(TT):
                wait_done(dve, ("pa", t))
                do(v.tensor_tensor(dts[:, 0, 32 * t:32 * t + 32], pa[:, t, 0:32], D("dt_b"), ALU.add))
            k = STAT["qa"] + RSTD
            dve.wait_ge(sem("squares_qa"), 2)
            rstd("qa", 2, 384)
            for t in range(TT):
                v.tensor_scalar(pa[:, t, 32:416], pa[:, t, 32:416], col(k + t), None, ALU.mult).then_inc(sem("qa_ready"), 1)
            lo_parts("qa", 3, 8, D("g_qa"))
            dve.wait_ge(sem("squares_qa"), 4)
            rstd("ck", 2, 256)
            for t in range(TT):
                v.tensor_scalar(pb[:, t, 0:256], pb[:, t, 0:256], col(k + 2 + t), None, ALU.mult).then_inc(sem("ck_ready"), 1)
            dve.wait_ge(sem("rope_sin"), 1)
            sin2, cos2 = (ropt[:, k, :].rearrange("p (t d) -> p t d", t=TT) for k in (6, 7))
            rotate(pb[:, :, 256:272], pb[:, :, 272:288], cos2, sin2,
                   [ropetmp2[:, k, 0:32].rearrange("p (t d) -> p t d", t=TT) for k in range(4)], "kp_rotated")
            lo_parts("ck", 2, 11, D("g_ckv"))
            wait_full(dve, ("kp", 0))
            release(v.tensor_copy(km[64:96, :, :], pj(("kp", 0))[0:32, 0:S].unsqueeze(1).to_broadcast([32, 16, S])), ("kp", 0))
            def conv_taps(i):
                for j in range(2):
                    job = (f"xbc{i}", j)
                    dve.wait_ge(sem("conv_first"), 4 * i + 2 * j + 2)
                    for back in (1, 2, 3):
                        for c in range(2):
                            k = CW + 24 * (3 - back) + 4 * i + 2 * j + c
                            d = cv[:, j, c, back:S]
                            ins = v.scalar_tensor_tensor(d, pj(job)[:, c * S:c * S + S - back], sml[:, k:k + 1], d, ALU.mult, ALU.add)
                            if back < 3 or c == 0:
                                do(ins)
                        if back < 3:
                            sync()
                    release(ins, job)

            def conv_silu(i):
                for j in range(2):
                    dve.wait_ge(sem("conv_tanh"), 2 * i + j + 1)
                    d = xbc[:, 4 * i + 2 * j:4 * i + 2 * j + 2, :]
                    v.scalar_tensor_tensor(d, d, 1.0, cv[:, j, :, :], ALU.add, ALU.mult).then_inc(sem("silu_done"), 1)

            conv_taps(0)
            for i in range(3):
                for t in range(TT):
                    wait_done(dve, (f"wq{i}", t))
            for t in range(TT):
                qh = qm[:, t, :].rearrange("p (h d) -> p h d", d=96)
                rotate(qh[:, :, 64:80], qh[:, :, 80:96], cos2[:, t, :].unsqueeze(1).to_broadcast([P, 16, 16]),
                       sin2[:, t, :].unsqueeze(1).to_broadcast([P, 16, 16]),
                       [ropetmp2[:, k, :].rearrange("p (h d) -> p h d", d=16) for k in range(4)], "qm_rotated", t + 1)
            for t in range(TT):
                for i in range(2):
                    copy(("vv", 2 * t + i), vm[:, t, 512 * i:512 * i + 512])

            def latent_out(q):
                wait_full(dve, ("mO", q))
                k = 2 * (4 * q % 8)
                do(v.reciprocal(col(RSUM + k, 8), col(SUMS + k, 8)))
                sync()
                rs2 = col(RSUM + k, 8).rearrange("p (h t) -> p h t", t=TT)
                src = pj(("mO", q))[:, :].rearrange("p (h t d) -> p h t d", t=TT, d=64)
                for t in range(TT):
                    for c in range(2):
                        d = qm[:, t, 384 * q + 192 * c:384 * q + 192 * c + P].rearrange("p (h d) -> p h d", d=64)
                        ins = v.tensor_tensor(d, src[:, 2 * c:2 * c + 2, t, :], rs2[:, 2 * c:2 * c + 2, t].unsqueeze(2).to_broadcast([P, 2, 64]), ALU.mult)
                release(ins, ("mO", q))

            maxima(("mS", 0), P, 0)
            for u in range(16):
                if u < 15:
                    maxima(("mS", u + 1), P, u + 1)
                copy(("mT", u), pT2[:, u % 2, :], cols=slice(0, 384))
                if u < 10 and u % 2:
                    conv_taps(u // 2 + 1)
                if u % 2 == 0 and u <= 10:
                    conv_silu(u // 2)
                if u % 4 == 0 and u:
                    latent_out(u // 4 - 1)
            latent_out(3)
            lo_parts("om", 8, 8)
            vv_, e_, one, ln_, den, msk = dts[:, 0, :], dts[:, 1, :], dts[:, 2, :], dts[:, 3, :], dts[:, 4, :], dts[:, 7, :]
            v.scalar_tensor_tensor(e_, vv_, -1.0, vv_, ALU.mult, ALU.min).then_inc(sem("dt_in"), 1)
            dve.wait_ge(sem("dt_exp"), 2)
            v.tensor_scalar(one, e_, 1.0, None, ALU.add).then_inc(sem("dt_one"), 1)
            dve.wait_ge(sem("dt_one"), 1)
            do(v.tensor_scalar(den, one, -1.0, None, ALU.add))
            sync()
            do(v.tensor_scalar(msk, den, 0.0, None, ALU.is_equal))
            sync()
            do(v.tensor_tensor(den, den, msk, ALU.add))
            sync()
            do(v.reciprocal(den, den))
            dve.wait_ge(sem("dt_ln"), 1)
            do(v.tensor_tensor(ln_, ln_, msk, ALU.add))
            sync()
            do(v.tensor_tensor(ln_, ln_, e_, ALU.mult))
            sync()
            do(v.tensor_tensor(ln_, ln_, den, ALU.mult))
            sync()
            do(v.scalar_tensor_tensor(dts[:, 0, :], vv_, 0.0, ln_, ALU.max, ALU.add))
            sync()
            dt3 = dts[:, 0, :].rearrange("p (t h) -> p t h", t=TT)
            do(v.tensor_tensor(dts[:, 1, :].rearrange("p (t h) -> p t h", t=TT), dt3, dts[:, 5, 0:32].unsqueeze(1).to_broadcast([P, TT, 32]), ALU.mult))
            sync()
            v.tensor_scalar(dts[:, 1, :], dts[:, 1, :], -1.0, None, ALU.mult).then_inc(sem("adt_ready"), 1)
            for i in range(2):
                for j in range(2):
                    job = (f"ym{i}", j)
                    wait_full(dve, job)
                    wait_done(dve, (f"gm{i}", j))
                    c = slice(4 * i + 2 * j, 4 * i + 2 * j + 2)
                    release(v.scalar_tensor_tensor(ymT[:, c, :], gmT[:, c, :], 1.0, pj(job)[:, :].rearrange("p (c s) -> p c s", s=S), ALU.add, ALU.mult), job)

            wait_full(dve, ("acum", 0))
            dve.wait_ge(sem("eac_ready"), 1)
            do(v.tensor_copy(dts[:, 7, 0:32], pj(("acum", 0))[:, 0:32]))
            sync()
            release(v.tensor_tensor(dts[:, 6, 0:32], pj(("acum", 0))[:, 64:96], dts[:, 7, 0:32], ALU.subtract), ("acum", 0))
            adt = dts[:, 1, :].rearrange("p (t h) -> p t h", t=TT)
            eac, weight = dts[:, 6, 32:64], dts[:, 7, 32:64]

            def seg_operand(q):
                i, k = q // 2, q % 2
                g, t = i // 2, i % 2
                if q >= 2:
                    wait_full(dve, ("seg", q - 2))
                h0 = 8 * g + 4 * k
                v.tensor_tensor(segR[:, q % 2, :].rearrange("p (h l) -> p h l", l=P), tri.unsqueeze(1).to_broadcast([P, 4, P]),
                                adt[:, t, h0:h0 + 4].unsqueeze(2).to_broadcast([P, 4, P]), ALU.mult).then_inc(sem("segR_ready"), 1)

            for t in range(TT):
                wait_full(dve, ("CB", t))
                release(v.tensor_tensor(cbm[:, t, :].rearrange("p (g l) -> p g l", l=P), pj(("CB", t))[:, :].rearrange("p (g l) -> p g l", l=P),
                                        tri.unsqueeze(1).to_broadcast([P, 4, P]), ALU.mult), ("CB", t))
            dve.wait_ge(sem("dte_ready"), 1)
            do(v.tensor_tensor(weight, dts[:, 0, 0:32], dts[:, 6, 0:32], ALU.mult))
            sync()
            wait_full(dve, ("xt", 7))
            seg_operand(0)
            seg_operand(1)
            zs = [0]

            def z_silu(k):
                for t in range(TT):
                    zs[0] += 1
                    dve.wait_ge(sem("tanh_z"), zs[0])
                    d = zt[:, t, 512 * k:512 * k + 512]
                    release(v.scalar_tensor_tensor(d, d, 1.0, pj((f"z{k}", t))[:, :], ALU.add, ALU.mult), (f"z{k}", t))

            z_silu(0)

            def y_lo(g):
                lo_parts("y", 4 * g + 4, 8 if g < 2 else -8, D("g_ssd"), 4 * g)

            def y_norm(g):
                dve.wait_ge(sem("squares_y"), 2 * g + 2)
                rstd("y", 2, 512, 2 * g)
                for t in range(TT):
                    d = zt[:, t, 512 * g:512 * g + 512]
                    v.tensor_scalar(d, d, col(STAT["y"] + RSTD + 2 * g + t), None, ALU.mult).then_inc(sem("y_ready"), 1)

            def state_operand(g):
                wait_done(dve, ("xt", g))
                if g:
                    wait_full(dve, ("state", g - 1))
                v.tensor_tensor(xd[:, :].rearrange("p (h d) -> p h d", d=64), xtok[:, 0, 512 * g:512 * g + 512].rearrange("p (h d) -> p h d", d=64),
                                weight[:, 8 * g:8 * g + 8].unsqueeze(2).to_broadcast([P, 8, 64]), ALU.mult).then_inc(sem("xd_ready"), 1)

            state_operand(0)
            for i in range(8):
                g, t = i // 2, i % 2
                xg = xtok[:, t, 512 * g:512 * g + 512].rearrange("p (h d) -> p h d", d=64)
                if i:
                    wait_full(dve, ("Y", i - 1))
                for q in (2 * i, 2 * i + 1):
                    wait_done(dve, ("seg", q))
                    for k in range(4):
                        h = 8 * g + 4 * (q % 2) + k
                        ins = v.scalar_tensor_tensor(segM[:, q % 2, P * k:P * k + P], segE[:, q % 2, P * k:P * k + P],
                                                     dts[:, 0, 32 * t + h:32 * t + h + 1], cbm[:, t, P * g:P * g + P], ALU.mult, ALU.mult)
                    ins.then_inc(sem("segM_ready"), 1)
                if t == 1:
                    wait_full(dve, ("off", g))
                    release(v.tensor_tensor(carried[:, :].rearrange("p (h d) -> p h d", d=64), pj(("off", g))[:, :].rearrange("p (h d) -> p h d", d=64),
                                            eac[:, 8 * g:8 * g + 8].unsqueeze(2).to_broadcast([P, 8, 64]), ALU.mult), ("off", g))
                if i < 7:
                    seg_operand(2 * i + 2)
                    seg_operand(2 * i + 3)
                if t == 1 and g < 3:
                    state_operand(g + 1)
                if t == 0 and g:
                    y_norm(g - 1)
                if i in (3, 5, 7):
                    y_lo(i // 2 - 1)
                wait_done(dve, ("xt", 4 * t + g))
                y3 = yt[:, 0, :].rearrange("p (h d) -> p h d", d=64)
                do(v.tensor_tensor(y3, xg, D("d_skip")[:, 8 * g:8 * g + 8].unsqueeze(2).to_broadcast([P, 8, 64]), ALU.mult))
                sync()
                wait_full(dve, ("Y", i))
                release(v.tensor_tensor(yt[:, 0, :], yt[:, 0, :], pj(("Y", i))[:, :], ALU.add), ("Y", i))
                wait_done(dve, ("Y", i))
                if t == 1:
                    wait_done(dve, ("off", g))
                    do(v.tensor_tensor(yt[:, 0, :], yt[:, 0, :], carried[:, :], ALU.add))
                    sync()
                d = zt[:, t, 512 * g:512 * g + 512]
                v.scalar_tensor_tensor(d, yt[:, 0, :], 0.5, d, ALU.mult, ALU.mult).then_inc(sem("y_gated"), 1)
                if i in (0, 2, 3):
                    z_silu((1, None, 2, 3)[i])
            y_norm(3)
            y_lo(3)
            for i in range(2):
                if i:
                    dve.wait_ge(sem("m2_parts"), 2)
                for j in range(2):
                    job = (f"ys{i}", j)
                    wait_full(dve, job)
                    wait_done(dve, (f"gs{i}", j))
                    c = 4 * i + 2 * j
                    b3 = yt[:, j, :].rearrange("p (c s) -> p c s", s=S)
                    release(v.scalar_tensor_tensor(b3, gsT[:, c:c + 2, :], 1.0, pj(job)[:, :].rearrange("p (c s) -> p c s", s=S), ALU.add, ALU.mult), job)
                    wait_done(dve, job)
                    do(v.tensor_tensor(b3, b3, ymT[:, c:c + 2, :], ALU.add))
                sync()
                halves(v, do, sync, yt, m2hi, m2lo, 4 * i, "m2_parts")
                if i == 0:
                    norm("mem", memt, xn, "memn_ready")
            lo_parts("mem", 8, 8, D("g_mem"))

            def residual(name, norm_name, ready):
                for t in range(TT):
                    for i in range(2):
                        job = (f"{name}{i}", t)
                        wait_full(dve, job)
                        d = x[:, t, 512 * i:512 * i + 512]
                        release(v.tensor_tensor(d, pj(job)[:, :], d, ALU.add), job)
                    for i in range(2):
                        wait_done(dve, (f"{name}{i}", t))
                    norm_tile(norm_name, x, xn, ready, t)

            residual("wp", "h", "hn_ready")
            for t in range(TT):
                copy(("xv0", t), vx[:, t, 0:512])
            lo_parts("h", 8, 0, D("g_xa"))
            for t in range(TT):
                copy(("xv1", t), vx[:, t, 512:1024])
            def cross_weights(h):
                maxima(("xS", h), S, h)
                wait_done(dve, ("xS", h))
                k = 2 * h
                do(v.reciprocal(col(RSUM + k, 2), col(SUMS + k, 2)))
                sync()
                for t in range(TT):
                    d = px[:, h % 2, S * t:S * t + S]
                    v.tensor_scalar(d, d, col(RSUM + k + t), None, ALU.mult).then_inc(sem("px_ready"), 1)

            def cross_lo(h):
                hi_seen[0] += 1
                dve.wait_ge(sem("xhi_ready"), hi_seen[0])
                release(v.tensor_tensor(xlo[:, 8 + 2 * h:10 + 2 * h, :], pj(("xO", h))[:, :].rearrange("p (c s) -> p c s", s=S),
                                        xhi[:, 8 + 2 * h:10 + 2 * h, :].bitcast(f32), ALU.subtract), ("xO", h))

            cross_weights(0)
            cross_weights(1)
            cross_lo(0)
            cross_weights(2)
            cross_lo(1)
            cross_weights(3)
            cross_lo(2)
            cross_lo(3)
            residual("xo", "m", "mn_ready")
            lo_parts("m", 8, 0, D("g_moe"))

            R3 = lambda k, w, o=0: rtl[:, k, :].rearrange("p (t w) -> p t w", t=TT)[:, :, o:o + w]
            copy(("rt", 0), ga[0:36, 0, 0:S], rows=slice(0, 36), cols=slice(0, S))
            wait_full(dve, ("rtt", 0))
            release(v.tensor_tensor(R3(0, 36), pj(("rtt", 0))[:, 0:P].rearrange("p (t w) -> p t w", t=TT)[:, :, 0:36],
                                    D("b_rt").unsqueeze(1).to_broadcast([P, TT, 36]), ALU.add), ("rtt", 0))
            wait_done(dve, ("rtt", 0))

            def first_of(src, w, mx, out):
                do(v.tensor_reduce(col(mx, 2), src, AX.X, ALU.max))
                sync()
                do(v.tensor_tensor(out, src, col(mx, 2).unsqueeze(2).to_broadcast([P, TT, w]), ALU.is_equal))
                sync()
                do(v.tensor_scalar(out, out, -1000.0, 1000.0, ALU.mult, ALU.add))
                sync()
                it = C("iota")[:, 0:w].unsqueeze(1).to_broadcast([P, TT, w])
                do(v.tensor_tensor(out, out, it, ALU.add))
                sync()
                do(v.tensor_reduce(col(mx + 2, 2), out, AX.X, ALU.min))
                sync()
                do(v.tensor_tensor(out, it, col(mx + 2, 2).unsqueeze(2).to_broadcast([P, TT, w]), ALU.is_equal))
                sync()

            G0, E1, E2 = NMAX, NMAX + 4, NMAX + 8
            WG, W1, W2 = NMAX + 12, SUMS, SUMS + 2
            first_of(R3(0, 4), 4, G0, R3(1, 4))
            v.tensor_tensor(rtl[:, 2, 0:8].rearrange("p (t w) -> p t w", t=TT), R3(0, 4), col(G0, 2).unsqueeze(2).to_broadcast([P, TT, 4]), ALU.subtract).then_inc(sem("router_arg"), 1)
            do(v.tensor_scalar(R3(1, 4), R3(1, 4), 1e30, -1e30, ALU.mult, ALU.add))
            sync()
            elog = R3(0, 32, 4).rearrange("p t (g e) -> p t g e", e=8)
            for t in range(TT):
                do(v.tensor_tensor(R3(4, 32)[:, t, :].rearrange("p (g e) -> p g e", e=8), elog[:, t, :, :],
                                   R3(1, 4)[:, t, :].unsqueeze(2).to_broadcast([P, 4, 8]), ALU.add))
            sync()
            first_of(R3(4, 32), 32, E1, R3(5, 32))
            for t in range(TT):
                do(v.scalar_tensor_tensor(R3(4, 32)[:, t, :], R3(5, 32)[:, t, :], -1e30, R3(4, 32)[:, t, :], ALU.mult, ALU.add))
            sync()
            first_of(R3(4, 32), 32, E2, R3(6, 32))
            v.tensor_tensor(rtl[:, 2, 8:10], col(E2, 2), col(E1, 2), ALU.subtract).then_inc(sem("router_arg"), 1)
            dve.wait_ge(sem("router_exp"), 2)
            do(v.tensor_reduce(col(WG, 2), rtl[:, 2, 0:8].rearrange("p (t w) -> p t w", t=TT), AX.X, ALU.add))
            do(v.tensor_scalar(col(W1, 2), rtl[:, 2, 8:10], 1.0, None, ALU.add))
            sync()
            do(v.tensor_tensor(col(W1, 2), col(W1, 2), col(WG, 2), ALU.mult))
            sync()
            do(v.reciprocal(col(W1, 2), col(W1, 2)))
            sync()
            do(v.tensor_tensor(col(W2, 2), col(W1, 2), rtl[:, 2, 8:10], ALU.mult))
            sync()
            for t in range(TT):
                do(v.tensor_scalar(R3(5, 32)[:, t, :], R3(5, 32)[:, t, :], col(W1 + t), None, ALU.mult))
            sync()
            for t in range(TT):
                v.scalar_tensor_tensor(R3(7, 32)[:, t, :], R3(6, 32)[:, t, :], col(W2 + t), R3(5, 32)[:, t, :], ALU.mult, ALU.add).then_inc(sem("comb_ready"), 1)
            wait_full(dve, ("cb", 0))
            release(v.tensor_copy(combt[:, :], pj(("cb", 0))[0:NEXP, 0:S]), ("cb", 0))
            dve.wait_ge(sem("comb_loaded"), 16)

            def expert_dve(e, i):
                s = e % 2
                up = NB + 1 if e == 0 else GATE_UNIT(e) + 1
                dve.wait_ge(sem("silu_ready"), i * 2 + (e + 1))
                dve.wait_ge(weights_used, i * 6 + (up + 1))
                v.tensor_tensor(ga[:, s, :], sg[:, s, :], ps[2 * s + 1][:, :], ALU.mult).then_inc(sem("gated"), 1)
                dve.wait_ge(sem("gated"), i * 2 + (e + 1))
                row = comb[:, e:e + 1, :] if isinstance(i, int) else comb[:, bass.ds(i * 2 + e, 1), :]
                g3 = ga[:, s, :].rearrange("p (f s) -> p f s", s=S)
                v.tensor_tensor(g3, g3, row.to_broadcast([P, 2, S]), ALU.mult).then_inc(sem("weighted"), 1)
                dve.wait_ge(sem("weighted"), i * 2 + (e + 1))
                v.tensor_copy(ahi[:, s, :], ga[:, s, :]).then_inc(sem("act_hi"), 1)
                dve.wait_ge(sem("act_hi"), i * 2 + (e + 1))
                v.tensor_tensor(alo[:, s, :], ga[:, s, :], ahi[:, s, :].bitcast(f32), ALU.subtract).then_inc(sem("act_ready"), 1)

            expert_dve(0, 0)
            expert_dve(1, 0)
            expert_dve(2, 0)
            dve.wait_ge(sem("comb_rest"), 48)
            with dve.Fori(0, (NEXP - 4) // 2) as i:
                expert_dve(3, i)
                expert_dve(4, i)
            expert_dve(NEXP - 1, 0)
            for t in range(TT):
                if t == 0:
                    dve.wait_ge(sem("sum_ready"), 1)
                else:
                    dve.wait_ge(weights_used, NU)
                for i in range(2):
                    d = x[:, t, 512 * i:512 * i + 512]
                    do(v.tensor_tensor(d, ps[4 + 2 * t + i][:, :], d, ALU.add))
                sync()
                v.tensor_copy(stat[:, MISC + 4 + t:MISC + 5 + t], x[:, t, 0:1]).then_inc(sem("h3_ready"), 1)
            dve.wait_ge(sem("nfin_loaded"), 16)
            for t in range(TT):
                dve.wait_ge(sem("squares_f"), t + 1)
                rstd("f", 1, DM, t)
                for i in range(2):
                    d = slice(512 * i, 512 * i + 512)
                    v.scalar_tensor_tensor(xn[:, t, d], x[:, t, d], col(STAT["f"] + RSTD + t), nfin[:, d], ALU.mult, ALU.mult).then_inc(sem("out_ready"), 1)

        @block.tensor
        def _(pe):
            mm = nc.tensor.matmul

            def begin(job):
                b, k = JOBS[job][:2]
                if k:
                    pe.wait_ge(bank_done[b], k)

            def end(ins, job):
                assert JOBS[job][3] is None
                ins.then_inc(bank_full[JOBS[job][0]], 1)

            def mm3(out, lh, ll, rh, rl, first, last, skip=False):
                mm(out, lh, rh, start=first, stop=False, skip_group_check=skip)
                mm(out, lh, rl, start=False, stop=False, skip_group_check=skip)
                return mm(out, ll, rh, start=False, stop=last, skip_group_check=skip)

            def parts(n, nk, nc_):
                pe.wait_ge(lo_ready, n + 1)
                s = n % NSPL
                return (whi[:, s, 0:nk * nc_].rearrange("p (k c) -> p k c", k=nk),
                        wlo[:, s, 0:nk * nc_].rearrange("p (k c) -> p k c", k=nk))

            def tile_wait(after, first, k):
                if after and first and k % 2 == 0:
                    wait_done(pe, (after, k // 2))

            def gemm_unit_tm(name, part, hi, lo, k0=0, kt=8, after=None):
                n = UNIT[name][part]
                nk, nc_ = units[n][4], len(units[n][5])
                wh, wl = parts(n, nk, nc_)
                r0 = sum(units[m][4] for m in UNIT[name][:part])
                for t in range(TT):
                    job = (name, t)
                    if part == 0:
                        begin(job)
                    for k in range(nk):
                        tok = slice(t * P, t * P + P)
                        tile_wait(after, t == 0, r0 + k)
                        ins = mm3(pj(job)[:, 0:nc_], hi[:, k0 + r0 + k, tok], lo[:, k0 + r0 + k, tok], wh[:, k, :], wl[:, k, :],
                                  r0 + k == 0, r0 + k == kt - 1)
                    if t == 0 and r0 + nk == kt:
                        end(ins, job)
                ins.then_inc(weights_used, 1)

            def gemm_unit_fm(name, part, hi, lo, k0=0, kt=8, after=None):
                n = UNIT[name][part]
                nk, nc_ = units[n][4], len(units[n][5])
                wh, wl = parts(n, nk, nc_)
                r0 = sum(units[m][4] for m in UNIT[name][:part])
                for c in range(nc_ // P):
                    job = (name, c // 2)
                    if part == 0 and c % 2 == 0:
                        begin(job)
                    for k in range(nk):
                        cc = slice(c * P, c * P + P)
                        o_ = pj(job)[:, c % 2 * S:c % 2 * S + S]
                        tile_wait(after, c == 0, r0 + k)
                        first, last = r0 + k == 0 and c % 2 == 0, r0 + k == kt - 1
                        mm(o_, wh[:, k, cc], hi[:, k0 + r0 + k, :], start=first, stop=False, skip_group_check=True)
                        mm(o_, wl[:, k, cc], hi[:, k0 + r0 + k, :], start=False, stop=False, skip_group_check=True)
                        ins = mm(o_, wh[:, k, cc], lo[:, k0 + r0 + k, :], start=False, stop=last, skip_group_check=True)
                    if c % 2 and c < nc_ // P - 1 and r0 + nk == kt:
                        end(ins, job)
                ins.then_inc(weights_used, 1)

            def gemm(name, kind, hi, lo, k0=0, kt=8, after=None):
                for part in range(len(UNIT[name])):
                    kind(name, part, hi, lo, k0, kt, after)

            def pair_ends(a, b, hi, lo, k0=0):
                w = [parts(UNIT[name][1], 4, 512) for name in (a, b)]
                for t in range(TT):
                    for name, (wh, wl) in zip((a, b), w):
                        tok = slice(t * P, t * P + P)
                        for k in range(4):
                            ins = mm3(pj((name, t))[:, :], hi[:, k0 + 4 + k, tok], lo[:, k0 + 4 + k, tok], wh[:, k, :], wl[:, k, :], False, k == 3)
                        if t == 0:
                            end(ins, (name, t))
                        else:
                            ins.then_inc(weights_used, 1)

            def transposes(name, nct, src, ready=None, count=0):
                if nct == 8 and ready:
                    for t in range(TT):
                        pe.wait_ge(sem(ready), count - 1 + t)
                        for c in range(nct):
                            job = (name, c // 2)
                            if t == 0 and c % 2 == 0:
                                begin(job)
                            ins = nc.tensor.transpose(pj(job)[:, c % 2 * S + t * P:c % 2 * S + t * P + P], src(t, c), ident)
                            if t == 1 and c % 2:
                                end(ins, job)
                    return
                if ready:
                    pe.wait_ge(sem(ready), count)
                for c in range(nct):
                    job = (name, c // 2)
                    if c % 2 == 0:
                        begin(job)
                    for t in range(TT):
                        ins = nc.tensor.transpose(pj(job)[:, c % 2 * S + t * P:c % 2 * S + t * P + P], src(t, c), ident)
                    if c % 2 or c == nct - 1:
                        end(ins, job)

            def tiles(m):
                return lambda t, c: m[:, t, c * P:c * P + P]

            def scores(job, q, k, mask=True):
                begin(job)
                b = pj(job)
                mm(b[:, 0:P], identb[:, :], negb[:, :], start=True, stop=False)
                mm(b[:, 0:P], q[:, 0:P], k[:, 0:P], start=False, stop=True)
                mm(b[:, P:S], q[:, P:S], k[:, 0:P], start=True, stop=True)
                mm(b[:, S:S + P], identb[:, :], negb[:, :], start=True, stop=False)
                end(mm(b[:, S:S + P], q[:, P:S], k[:, P:S], start=False, stop=True), job)

            def weights_transposed(job, p, n, sjob=None):
                begin(job)
                if sjob:
                    wait_done(pe, sjob)
                for i in range(n):
                    ins = nc.tensor.transpose(pj(job)[:, i * P:i * P + P], p[:, i * P:i * P + P], ident)
                end(ins, job)

            def outputs(job, tjob, pt, val, h):
                wait_done(pe, tjob)
                if h == 0:
                    begin(job)
                b = pj(job)[:, h * P:h * P + P]
                mm(b[:, 0:64], pt[:, 0:P], val(0), start=True, stop=True)
                mm(b[:, 64:P], pt[:, P:S], val(0), start=True, stop=False)
                ins = mm(b[:, 64:P], pt[:, S:S + P], val(1), start=False, stop=True)
                if h == 3:
                    end(ins, job)

            tm, fm = gemm_unit_tm, gemm_unit_fm
            pe.wait_ge(sem("cst_loaded"), 16)
            transposes("x", 8, tiles(xn), "xn_ready", 2)
            gemm("qn", tm, xhi, xlo, after="x")
            for n in ("kv1", "kv2", "qr", "kr", "vr0", "vr1"):
                gemm(n, tm, xhi, xlo)
            pe.wait_ge(sem("nq_rotated"), 1)
            begin(("kT", 0))
            for k, c in enumerate((640, 768)):
                for t in range(TT):
                    ins = nc.tensor.transpose(pj(("kT", 0))[:, k * S + t * P:k * S + t * P + P], nq[:, t, c:c + P], ident)
            end(ins, ("kT", 0))
            transposes("qT", 4, tiles(nq))
            begin(("cT", 0))
            for k, c in enumerate((512, 896)):
                for t in range(TT):
                    ins = nc.tensor.transpose(pj(("cT", 0))[:, k * S + t * P:k * S + t * P + P], nq[:, t, c:c + P], ident)
            end(ins, ("cT", 0))
            fm("zn", 0, xhi, xlo)
            pe.wait_ge(sem("xclo_ready"), 1)
            begin(("hs", 0))
            for kv, name in enumerate(("w1k", "w1v")):
                for part in range(2):
                    wh, wl = parts(UNIT[name][part], 8, S)
                    for k in range(8):
                        l = 8 * part + k
                        ins = mm3(pj(("hs", 0))[0:30, kv * S:kv * S + S], xchi[:, kv, l, :], xclo[:, kv, l, :], wh[:, k, :], wl[:, k, :],
                                  kv == part == k == 0, l == 15, skip=True)
                    ins.then_inc(weights_used, 1)
            fm("zn", 1, xhi, xlo)
            wait_done(pe, ("hs", 0))
            begin(("hid", 0))
            for c in range(4):
                ins = nc.tensor.transpose(pj(("hid", 0))[:, 32 * c:32 * c + 30], pT[0:30, 0, c * P:c * P + P], ident[0:30, 0:30])
            end(ins, ("hid", 0))
            fm("zr0", 0, xhi, xlo)
            pe.wait_ge(sem("gelu_ready"), 1)
            begin(("kvc", 0))
            hv = hg[:, 3, :].rearrange("p (a c) -> p a c", c=30)
            w2k, w2v = D("w2k").rearrange("p (a c) -> p a c", a=2), D("w2v").rearrange("p (a c) -> p a c", a=2)
            for half in range(2):
                mm(pj(("kvc", 0))[:, 0:30], w2k[:, half, :], hv[:, half, :], start=half == 0, stop=half == 1)
            for g in range(2):
                for half in range(2):
                    ins = mm(pj(("kvc", 0))[0:15, 64 + 64 * g:128 + 64 * g], hv[:, 2 + half, 15 * g:15 * g + 15], w2v[:, half, :],
                             start=half == 0, stop=half == 1)
            end(ins, ("kvc", 0))
            for job in (("kvc", 0), ("qT", 1), ("kT", 0)):
                wait_done(pe, job)
            pe.wait_ge(sem("masks_ready"), 2)
            begin(("Sc", 0))
            for odd in range(2):
                for h in range(odd, 8, 2):
                    for t in range(TT):
                        r, g = 64 * odd, h // 4
                        ins = mm(pj(("Sc", 0))[:, (8 * t + h) * 32:(8 * t + h) * 32 + 15], qT[r:r + 64, h // 2, t * P:t * P + P],
                                 kcT[r:r + 64, 15 * g:15 * g + 15], start=True, stop=True)
                if not odd:
                    ins.then_inc(sem("even_scores"), 1)
                    pe.wait_ge(sem("even_scores"), 1)
            end(ins, ("Sc", 0))

            def head(u):
                r, g = 64 * (u % 2), u % 8 // 4
                return qT[r:r + 64, u % 8 // 2, :], kT[r:r + 64, g, u // 8 * S:u // 8 * S + S]

            def value(u):
                c = (1024, 1152)[u // 8] + 64 * (u % 8 // 4)
                return lambda t: nq[:, t, c:c + 64]

            fm("zr0", 1, xhi, xlo)
            pe.wait_ge(sem("cmp_exp"), 1)
            weights_transposed(("Tc", 0), pr[:, 0, :], 4)
            scores(("S", 0), *head(0))
            wait_done(pe, ("Tc", 0))
            for t in range(TT):
                begin(("Oc", t))
                for g in range(2):
                    ins = mm(pj(("Oc", t))[:, g * S:g * S + S], pT[:, 0, (2 * t + g) * P:(2 * t + g) * P + P],
                             vcb[:, g, :, :].rearrange("p h d -> p (h d)"), start=True, stop=True)
                end(ins, ("Oc", t))
            fill = {1: ("zr1", 0), 4: ("zr1", 1), 6: ("ma0", 0), 9: ("ma0", 1), 11: ("ma1", 0), 14: ("ma1", 1)}
            for u in range(16):
                if u < 15:
                    scores(("S", u + 1), *head(u + 1))
                if u in fill:
                    fm(*fill[u], xhi, xlo)
                weights_transposed(("T", u), pr[:, u % 2, :], 3, ("S", u))
                if u:
                    outputs(("O", (u - 1) // 4), ("T", u - 1), pT[:, (u - 1) % 2, :], value(u - 1), (u - 1) % 4)
            outputs(("O", 3), ("T", 15), pT[:, 1, :], value(15), 3)
            pe.wait_ge(sem("qk_rotated"), 2)

            def ret_transposed(h):
                begin(("QK", h))
                for k in range(2):
                    for t in range(TT):
                        ins = nc.tensor.transpose(pj(("QK", h))[:, k * S + t * P:k * S + t * P + P], qk[:, t, 512 * k + P * h:512 * k + P * h + P], ident)
                end(ins, ("QK", h))

            ret_transposed(0)
            for h in range(4):
                fm(f"mb{h // 2}", h % 2, xhi, xlo)
                if h == 0:
                    transposes("on", 4, tiles(oacc), "oacc_added", 8)
                wait_done(pe, ("QK", h))
                begin(("A", h))
                b = pj(("A", h))
                mm(b[:, 0:S], qkT[:, h % 2, S:S + P], qkT[:, h % 2, 0:S], start=True, stop=True)
                end(mm(b[:, S:S + P], qkT[:, h % 2, S + P:2 * S], qkT[:, h % 2, P:S], start=True, stop=True), ("A", h))
                if h < 3:
                    ret_transposed(h + 1)
                wait_done(pe, ("A", h))
                begin(("R", h))
                b, at_ = pj(("R", h)), pT[:, h % 2, :]
                v0, v1 = vr[:, 0, h * S:h * S + S], vr[:, 1, h * S:h * S + S]
                mm(b[:, 0:S], at_[:, 0:P], v0, start=True, stop=True)
                mm(b[:, S:2 * S], at_[:, P:S], v0, start=True, stop=False)
                end(mm(b[:, S:2 * S], at_[:, S:S + P], v1, start=False, stop=True), ("R", h))
            pe.wait_ge(sem("on_parts"), 2)
            gemm("ya0", fm, xhi, xlo, 8, 4)
            wait_done(pe, ("R", 3))
            transposes("or", 8, tiles(xn))
            gemm("ya1", fm, xhi, xlo, 8, 4)
            pe.wait_ge(sem("or_parts"), 4)
            gemm("yb0", fm, xhi, xlo)
            gemm("yb1", fm, xhi, xlo)
            pe.wait_ge(sem("mT_parts"), 2)
            tm("wo0", 0, mThi, mTlo)
            tm("wo1", 0, mThi, mTlo)
            pe.wait_ge(sem("mT_parts"), 4)
            pair_ends("wo0", "wo1", mThi, mTlo)
            transposes("u", 8, tiles(xn), "un_ready", 2)
            gemm("pa", tm, xhi, xlo, after="u")
            gemm("pb", tm, xhi, xlo)
            pe.wait_ge(sem("qa_ready"), 2)
            transposes("qa", 3, lambda t, c: pa[:, t, 32 + c * P:32 + c * P + P])
            fm("xbc0", 0, xhi, xlo)
            pe.wait_ge(sem("ck_ready"), 2)
            transposes("ck", 2, tiles(pb))
            pe.wait_ge(sem("kp_rotated"), 1)
            begin(("kp", 0))
            for t in range(TT):
                ins = nc.tensor.transpose(pj(("kp", 0))[0:32, t * P:t * P + P], pb[:, t, 256:288], ident)
            end(ins, ("kp", 0))
            fm("xbc0", 1, xhi, xlo)
            for i in range(3):
                gemm(f"wq{i}", tm, xhi, xlo, 8, 3, None if i else "qa")
            wait_done(pe, ("ck", 0))
            n = UNIT["kn"][0]
            wh, wl = parts(n, 2, 1024)
            for c in range(8):
                job = ("kn", c // 2)
                if c % 2 == 0:
                    begin(job)
                for k in range(2):
                    o_ = pj(job)[:, c % 2 * S:c % 2 * S + S]
                    cc = slice(c * P, c * P + P)
                    mm(o_, wh[:, k, cc], xhi[:, 11 + k, :], start=k == 0, stop=False)
                    mm(o_, wl[:, k, cc], xhi[:, 11 + k, :], start=False, stop=False)
                    ins = mm(o_, wh[:, k, cc], xlo[:, 11 + k, :], start=False, stop=k == 1)
                if c % 2 and c < 7:
                    end(ins, job)
            ins.then_inc(weights_used, 1)
            wh, wl = parts(UNIT["vv"][0], 2, 1024)
            for j in range(4):
                job, t, i = ("vv", j), j // 2, j % 2
                begin(job)
                for k in range(2):
                    tok, cc = slice(t * P, t * P + P), slice(512 * i, 512 * i + 512)
                    ins = mm3(pj(job)[:, :], xhi[:, 11 + k, tok], xlo[:, 11 + k, tok], wh[:, k, cc], wl[:, k, cc], k == 0, k == 1)
                if j < 3:
                    end(ins, job)
            ins.then_inc(weights_used, 1)
            pe.wait_ge(sem("qm_rotated"), 2)

            def latent_queries(p):
                begin(("mQ", p))
                for c in range(2):
                    for t in range(TT):
                        h = 2 * p + c
                        ins = nc.tensor.transpose(pj(("mQ", p))[0:96, c * S + t * P:c * S + t * P + P], qm[:, t, 96 * h:96 * h + 96], ident)
                end(ins, ("mQ", p))

            def latent_head(u):
                wait_done(pe, ("mQ", u // 2))
                return qmT[0:96, u // 2 % 2, u % 2 * S:u % 2 * S + S], km[0:96, u, :]

            latent_queries(0)
            wait_done(pe, ("kp", 0))
            wait_done(pe, ("kn", 3))
            scores(("mS", 0), *latent_head(0))
            for u in range(16):
                if u % 2 == 0 and u < 14:
                    latent_queries(u // 2 + 1)
                if u < 13:
                    fm(units[MLA_FILL[u]][0], units[MLA_FILL[u]][1], xhi, xlo)
                if u < 15:
                    scores(("mS", u + 1), *latent_head(u + 1))
                weights_transposed(("mT", u), pr2[:, u % 2, :], 3, ("mS", u))
                if u:
                    h = u - 1
                    if h == 0:
                        wait_done(pe, ("vv", 3))
                    outputs(("mO", h // 4), ("mT", h), pT2[:, h % 2, :], lambda t: vm[:, t, 64 * h:64 * h + 64], h % 4)
            outputs(("mO", 3), ("mT", 15), pT2[:, 1, :], lambda t: vm[:, t, 64 * 15:64 * 16], 3)
            fm("gm1", 1, xhi, xlo)
            wait_done(pe, ("mO", 3))

            def om_tile(t, c):
                return qm[:, t, 192 * c:192 * c + P]

            transposes("om", 8, om_tile)
            for i in range(2):
                gemm(f"ym{i}", fm, xhi, xlo, 8, after=None if i else "om")
            pe.wait_ge(sem("adt_ready"), 1)
            pe.wait_ge(sem("silu_done"), 12)
            begin(("acum", 0))
            b = pj(("acum", 0))
            mm(b[:, 0:32], tri, dts[:, 1, 0:32], start=True, stop=True)
            mm(b[:, 32:64], tri, dts[:, 1, 32:64], start=True, stop=True)
            end(mm(b[:, 64:96], ones, dts[:, 1, 0:32], start=True, stop=True), ("acum", 0))
            begin(("Bt", 0))
            for g in range(4):
                ins = nc.tensor.transpose(pj(("Bt", 0))[:, g * P:g * P + P], xbc[:, 16 + g, 0:P], ident)
            end(ins, ("Bt", 0))
            for t in range(TT):
                begin(("CB", t))
                for g in range(4):
                    ins = mm(pj(("CB", t))[:, g * P:g * P + P], xbc[:, 16 + g, t * P:t * P + P], xbc[:, 20 + g, t * P:t * P + P], start=True, stop=True)
                end(ins, ("CB", t))
            for i in range(8):
                begin(("xt", i))
                for k in range(4):
                    ins = nc.tensor.transpose(pj(("xt", i))[:, k * P:k * P + P], xbc[:, 4 * (i % 4) + k, i // 4 * P:i // 4 * P + P], ident)
                end(ins, ("xt", i))

            def scan_unit(n, half):
                (tm if n[0] == "z" else fm)(n, half, xhi, xlo)

            def y_transposed(g):
                pe.wait_ge(sem("y_ready"), 2 * g + 2)
                for c in range(4 * g, 4 * g + 4):
                    job = ("y", c // 2)
                    if c % 2 == 0:
                        begin(job)
                    for t in range(TT):
                        ins = nc.tensor.transpose(pj(job)[:, c % 2 * S + t * P:c % 2 * S + t * P + P], zt[:, t, c * P:c * P + P], ident)
                    if c % 2:
                        end(ins, job)

            scan_unit("z0", 0)
            scan_unit("z0", 1)
            for i in range(8):
                g, t = i // 2, i % 2
                for q in (2 * i, 2 * i + 1):
                    begin(("seg", q))
                    pe.wait_ge(sem("segR_ready"), q + 1)
                    end(mm(pj(("seg", q))[:, :], stri, segR[:, q % 2, :], start=True, stop=True), ("seg", q))
                if t == 0:
                    begin(("state", g))
                    pe.wait_ge(sem("xd_ready"), g + 1)
                    end(mm(pj(("state", g))[:, :], btok[:, g * P:g * P + P], xd[:, :], start=True, stop=True), ("state", g))
                else:
                    begin(("off", g))
                    wait_done(pe, ("state", g))
                    end(mm(pj(("off", g))[:, :], xbc[:, 20 + g, P:S], st[:, :], start=True, stop=True), ("off", g))
                for unit in SCAN_FILL[i]:
                    scan_unit(*unit)
                if i in (3, 5, 7):
                    y_transposed(i // 2 - 1)
                begin(("Y", i))
                pe.wait_ge(sem("segM_ready"), 2 * i + 2)
                for k in range(8):
                    c = 512 * g + 64 * k
                    ins = mm(pj(("Y", i))[:, 64 * k:64 * k + 64], segM[:, k // 4, k % 4 * P:k % 4 * P + P], xtok[:, t, c:c + 64], start=True, stop=True)
                end(ins, ("Y", i))

            def ssd_out(i, g):
                fm(f"ys{i}", g, xhi, xlo, 8 if g < 2 else -8, 16, None if i else "y")

            ssd_out(0, 0)
            ssd_out(0, 1)
            y_transposed(3)
            for i, g in ((0, 2), (0, 3), (1, 0), (1, 1), (1, 2), (1, 3)):
                ssd_out(i, g)
            pe.wait_ge(sem("m2_parts"), 2)
            tm("wp0", 0, m2hi, m2lo)
            tm("wp1", 0, m2hi, m2lo)
            pe.wait_ge(sem("memn_ready"), 2)
            transposes("mem", 8, tiles(xn))
            pe.wait_ge(sem("m2_parts"), 4)
            pair_ends("wp0", "wp1", m2hi, m2lo)
            gemm("xk0", fm, xhi, xlo, 8, after="mem")
            gemm("xk1", fm, xhi, xlo, 8)
            gemm("xv0", tm, xhi, xlo, 8)
            transposes("h", 8, tiles(xn), "hn_ready", 2)
            gemm("xv1", tm, xhi, xlo, 8)
            gemm("xq0", fm, xhi, xlo, after="h")

            def cross_scores(h):
                if h % 2 == 0:
                    for i in range(2):
                        wait_done(pe, (f"xq{h // 2}", i))
                        wait_done(pe, (f"xk{h // 2}", i))
                begin(("xS", h))
                for t in range(TT):
                    for d in range(2):
                        ins = mm(pj(("xS", h))[:, t * S:t * S + S], qx[:, 2 * h + d, t * P:t * P + P], kx[:, 2 * h + d, :], start=d == 0, stop=d == 1)
                end(ins, ("xS", h))

            def cross_transposed(h):
                begin(("xT", h))
                pe.wait_ge(sem("px_ready"), 2 * h + 2)
                for k in range(2):
                    for t in range(TT):
                        ins = nc.tensor.transpose(pj(("xT", h))[:, k * S + t * P:k * S + t * P + P], px[:, h % 2, t * S + k * P:t * S + k * P + P], ident)
                end(ins, ("xT", h))

            def cross_output(h):
                wait_done(pe, ("xT", h))
                if h % 2 == 0:
                    for i in range(2):
                        wait_done(pe, (f"xv{h // 2}", i))
                begin(("xO", h))
                for d in range(2):
                    for k in range(2):
                        ins = mm(pj(("xO", h))[:, d * S:d * S + S], vx[:, k, h * S + d * P:h * S + d * P + P], pxT[:, h % 2, k * S:k * S + S],
                                 start=k == 0, stop=k == 1)
                end(ins, ("xO", h))

            cross_scores(0)
            fm("xq1", 0, xhi, xlo)
            cross_transposed(0)
            cross_scores(1)
            fm("xq1", 1, xhi, xlo)
            cross_output(0)
            cross_transposed(1)
            cross_scores(2)
            cross_output(1)
            cross_scores(3)
            wait_done(pe, ("xO", 1))
            tm("xo0", 0, xhi, xlo, 8)
            cross_transposed(2)
            cross_output(2)
            cross_transposed(3)
            cross_output(3)
            tm("xo1", 0, xhi, xlo, 8)
            wait_done(pe, ("xO", 3))
            pair_ends("xo0", "xo1", xhi, xlo, 8)
            transposes("m", 8, tiles(xn), "mn_ready", 2)
            begin(("rt", 0))
            wh, wl = parts(UNIT["rt"][0], 8, 36)
            for k in range(8):
                o_ = pj(("rt", 0))[0:36, 0:S]
                tile_wait("m", True, k)
                mm(o_, wh[:, k, :], xhi[:, k, :], start=k == 0, stop=False)
                mm(o_, wl[:, k, :], xhi[:, k, :], start=False, stop=False)
                ins = mm(o_, wh[:, k, :], xlo[:, k, :], start=False, stop=k == 7)
            ins.then_inc(weights_used, 1)

            def expert_in(unit, b, i):
                pe.wait_ge(lo_ready, i * 6 + (unit + 1))
                wh = whi[:, unit % NSPL, :].rearrange("p (k c) -> p k c", k=8)
                wl = wlo[:, unit % NSPL, :].rearrange("p (k c) -> p k c", k=8)
                for f in range(2):
                    o_, cc = ps[b][:, f * S:f * S + S], slice(f * P, f * P + P)
                    for k in range(8):
                        mm(o_, wh[:, k, cc], xhi[:, k, :], start=k == 0, stop=False)
                        mm(o_, wl[:, k, cc], xhi[:, k, :], start=False, stop=False)
                        ins = mm(o_, wh[:, k, cc], xlo[:, k, :], start=False, stop=k == 7)
                ins.then_inc(weights_used, 1)

            def expert_down(e, unit, i):
                pe.wait_ge(lo_ready, i * 6 + (unit + 1))
                pe.wait_ge(sem("act_ready"), i * 2 + (e + 1))
                s = e % 2
                wh = whi[:, unit % NSPL, :].rearrange("p (k c) -> p k c", k=2)
                wl = wlo[:, unit % NSPL, :].rearrange("p (k c) -> p k c", k=2)
                for t in range(TT):
                    for half in range(2):
                        for k in range(2):
                            a_, cc = slice(k * S + t * P, k * S + t * P + P), slice(512 * half, 512 * half + 512)
                            ins = mm3(ps[4 + 2 * t + half][:, :], ahi[:, s, a_], alo[:, s, a_], wh[:, k, cc], wl[:, k, cc],
                                      e == 0 and k == 0, e == NEXP - 1 and k == 1, skip=True)
                    if e == NEXP - 1 and t == 0:
                        ins.then_inc(sem("sum_ready"), 1)
                ins.then_inc(weights_used, 1)

            begin(("rtt", 0))
            wait_done(pe, ("rt", 0))
            for t in range(TT):
                ins = nc.tensor.transpose(pj(("rtt", 0))[:, 64 * t:64 * t + 36], ga[0:36, 0, t * P:t * P + P], ident[0:36, 0:36])
            end(ins, ("rtt", 0))
            pe.wait_ge(bank_done[0], TOTAL[0])
            expert_in(NB, 0, 0)
            pe.wait_ge(bank_done[1], TOTAL[1])
            expert_in(NB + 1, 1, 0)
            begin(("cb", 0))
            pe.wait_ge(sem("comb_ready"), 2)
            for t in range(TT):
                ins = nc.tensor.transpose(pj(("cb", 0))[0:NEXP, t * P:t * P + P], rtl[:, 7, 36 * t:36 * t + 32], ident)
            end(ins, ("cb", 0))
            for b in (2, 3):
                pe.wait_ge(bank_done[b], TOTAL[b])

            def expert_pe(e, i):
                n, s = GATE_UNIT(e), e % 2
                if e >= 2:
                    pe.wait_ge(sem("silu_ready"), i * 2 + (e - 1))
                expert_in(n, 2 * s, i)
                if e >= 2:
                    pe.wait_ge(sem("gated"), i * 2 + (e - 1))
                expert_in(n + 1, 2 * s + 1, i)
                if e == 1:
                    for b in range(4, 8):
                        pe.wait_ge(bank_done[b], TOTAL[b])
                expert_down(e - 1, n + 2, i)

            expert_pe(1, 0)
            expert_pe(2, 0)
            with pe.Fori(0, (NEXP - 4) // 2) as i:
                expert_pe(3, i)
                expert_pe(4, i)
            expert_pe(NEXP - 1, 0)
            expert_down(NEXP - 1, NU - 1, 0)


def constants():
    f = np.float32
    c = np.zeros((P, NCONST), f)
    p = np.arange(P)

    def put(name, a):
        o, w = CONST[name]
        c[:, o:o + w] = np.asarray(a, f).reshape(P, w)

    put("ident", np.eye(P))
    put("tri", p[:, None] <= p[None, :])
    put("stri", p[:, None] > p[None, :])
    put("ones", np.ones((P, P)))
    put("negmask", np.where(p[None, :] > p[:, None], -1e30, 0.0))
    tok = np.arange(TT)[None, :] * P + p[:, None]
    put("cmpmask", np.where(16 * np.arange(15) + 31 <= tok[:, :, None], 0.0, -1e30))
    nsa_inv = (f(1.0) / (f(500000.0) ** (np.arange(0, 16, 2, dtype=f) / f(16)))).astype(f)
    ang = tok.astype(f)[:, :, None] * nsa_inv
    put("cos", np.cos(ang.astype(np.float64)))
    put("sin", np.sin(ang.astype(np.float64)))
    ret_inv = (f(1.0) / (f(10000.0) ** np.linspace(0.0, 1.0, 64, dtype=f))).astype(f)
    ang = tok.astype(f)[:, :, None] * ret_inv
    put("rcos", np.cos(ang.astype(np.float64)))
    put("rsin", np.sin(ang.astype(np.float64)))
    put("invf", np.tile(f(10000.0) ** (-np.arange(16, dtype=f) / f(16)), (P, 1)))
    put("iota", np.tile(np.arange(32), (P, 1)))
    diff = np.arange(S)[None, :] - p[:, None]
    log_g = np.log(1.0 - 2.0 ** (-5.0 - np.arange(4)))
    dec = np.where(diff[:, None, :] >= 0, np.exp(np.maximum(diff, 0)[:, None, :] * log_g[None, :, None]), 0.0) * 128 ** -0.5
    return c, dec.astype(f)


def laid_out(inputs):
    a = {k: np.asarray(v) for k, v in inputs.items()}
    f = np.float32
    a["router"] = np.concatenate([a["w_router_group_2"][0], a["w_router_expert_2"][0]], axis=1)
    units = unit_plan()
    w = np.zeros((len(units), P, UW), f)
    flat = {}
    for n, (_, _, src, r0, nk, cols) in enumerate(units):
        if src not in flat:
            flat[src] = a[src].reshape(-1, a[src].shape[-1])
        m = flat[src][r0:r0 + nk * P]
        c0, c1 = int(cols[0]), int(cols[-1]) + 1
        m = m[:, c0:c1] if c1 - c0 == len(cols) else m[:, cols]
        w[n, :, :nk * len(cols)] = m.reshape(nk, P, len(cols)).transpose(1, 0, 2).reshape(P, -1)
    s = np.zeros((P, NSMALL), f)

    def put(name, v):
        o, width = SMALL[name]
        s[:, o:o + width] = np.broadcast_to(v, (P, width))

    for name, src in (("g_pre", "norm_pre"), ("g_mix", "norm_mix_2"), ("g_xa", "norm_xattn_2"), ("g_mem", "norm_mem_2"),
                      ("g_moe", "norm_moe_2"), ("g_ssd", "ssd_norm_2"), ("g_qa", "q_a_norm_2"), ("g_ckv", "kv_a_norm_2")):
        put(name, a[src].reshape(-1, P).T)
    put("conv_w", a["conv_w_2"][0].reshape(4 * 24, P).T)
    put("conv_b", a["conv_b_2"][0].reshape(24, P).T)
    put("pe_k", a["cmp_pe_k"].reshape(16, P).T)
    put("pe_v", a["cmp_pe_v"].reshape(16, P).T)
    put("b_gate", a["b_nsa_gate"][None])
    put("dt_b", a["dt_bias_2"])
    put("a_log", a["a_log_2"])
    put("d_skip", a["d_skip_2"])
    put("b_rt", np.concatenate([a["b_router_group_2"], a["b_router_expert_2"]], axis=1))
    w2 = a["cmp_w2_k"].reshape(2, P, 64).transpose(1, 0, 2)
    put("w2k", np.concatenate([w2, w2], axis=2).reshape(P, 256))
    put("w2v", a["cmp_w2_v"].reshape(2, P, 64).transpose(1, 0, 2).reshape(P, 128))
    tok = lambda m: np.ascontiguousarray(m.reshape(TT, P, -1).transpose(1, 0, 2))
    cst, dec = constants()
    return {
        "x": tok(a["x"]), "mem": tok(a["mem_2"]), "positions": np.ascontiguousarray(a["positions_2"].reshape(TT, P).T.astype(np.int32)),
        "constants": cst, "small": s, "decay": dec, "norm_post": np.ascontiguousarray(np.broadcast_to(a["norm_post"], (P, DM))),
        "norm_final": np.ascontiguousarray(np.broadcast_to(a["norm_final_2"], (P, DM))), "weights": w,
    }


def kernel(**inputs):
    import concourse.bacc as bacc
    from concourse.bass_utils import run_bass_kernel_spmd

    nc = bacc.Bacc("TRN2", target_bir_lowering=False, num_devices=1)
    arrays, args = {}, []
    for name, a in laid_out(inputs).items():
        arrays[f"in_{name}"] = a
        args.append(nc.dram_tensor(f"in_{name}", a.shape, mybir.dt.from_np(a.dtype), kind="ExternalInput").ap())
    out = nc.dram_tensor("out", (P, TT, DM), mybir.dt.float32, kind="ExternalOutput").ap()
    scratch = nc.dram_tensor("expert_weights", (NEXP, S), mybir.dt.float32, kind="Internal").ap()
    program(nc, *args, out, scratch)
    r = run_bass_kernel_spmd(nc, [arrays], core_ids=[0])
    got = r.results[0]["out"]
    return np.ascontiguousarray(got.transpose(1, 0, 2)).reshape(1, S, DM)
```
